# Optimizing a Trainium2 kernel written in Bass

```python
import jax, jax.numpy as jnp
from jax import lax
import numpy as np
import math

D_MODEL = 1024
BATCH = 1
SEQ = 256
DEPTH = 2

POOL_WINDOWS = (2, 4, 8, 16)
POOL_GROUPS = len(POOL_WINDOWS)
POOL_GROUP_DIM = D_MODEL // POOL_GROUPS
POOL_WIDTH = POOL_GROUPS * POOL_GROUP_DIM
ATTN_GROUPS = ((128, 1), (512, 4), (2048, 16))
HEADS_PER_GROUP = 4
N_HEADS = HEADS_PER_GROUP * len(ATTN_GROUPS)
HEAD_DIM = D_MODEL // 8
ATTN_WIDTH = N_HEADS * HEAD_DIM
ATTN_OUT = HEADS_PER_GROUP * HEAD_DIM
Q_BLOCK = 64
NEG_INF = -1e30
N_BUCKETS = 32
MAX_DISTANCE = 1024
D_FF = ((8 * D_MODEL // 3 + 255) // 256) * 256
CONV_WIDTH = 3
EPS = 1e-6
SPLITS = [int(s) for s in np.cumsum([POOL_WIDTH, ATTN_WIDTH, ATTN_WIDTH, ATTN_WIDTH, D_MODEL])]
IN_WIDTH = POOL_WIDTH + 3 * ATTN_WIDTH + 2 * D_MODEL


def _rmsnorm(x, g):
    xf = x.astype(jnp.float32)
    y = xf * lax.rsqrt(jnp.mean(xf * xf, axis=-1, keepdims=True) + EPS)
    return (y * g.astype(jnp.float32)).astype(x.dtype)

def _t5_buckets(rel):
    n = -rel
    half = N_BUCKETS // 2
    ret = (n < 0).astype(np.int32) * half
    n = np.abs(n)
    max_exact = half // 2
    large = max_exact + (np.log(np.maximum(n, 1) / max_exact)
                         / np.log(MAX_DISTANCE / max_exact) * (half - max_exact)).astype(np.int32)
    large = np.minimum(large, half - 1)
    return (ret + np.where(n < max_exact, n, large)).astype(np.int32)

def _centred_mean(u, window):
    S = u.shape[1]
    c = jnp.pad(jnp.cumsum(u.astype(jnp.float32), axis=1), ((0, 0), (1, 0), (0, 0)))
    i = np.arange(S)
    lo = np.clip(i - window // 2, 0, S)
    hi = np.clip(i - window // 2 + window, 0, S)
    count = (hi - lo).astype(np.float32)
    return ((c[:, hi] - c[:, lo]) / count[None, :, None]).astype(u.dtype)

def _dilated_group(q, k, v, bias, window, dilation):
    B, S, H, Dh = q.shape
    half = window // (2 * dilation)
    offs = dilation * np.arange(-half, half + 1)
    pad = half * dilation
    k_pad = jnp.pad(k, ((0, 0), (pad, pad), (0, 0), (0, 0)))
    v_pad = jnp.pad(v, ((0, 0), (pad, pad), (0, 0), (0, 0)))
    t = np.arange(Q_BLOCK)
    scale = HEAD_DIM ** -0.5

    def block(q0):
        pos = q0 + t[:, None] + offs[None, :]
        valid = (pos >= 0) & (pos < S)
        idx = pos + pad
        kb = jnp.take(k_pad, idx, axis=1)
        vb = jnp.take(v_pad, idx, axis=1)
        qb = lax.dynamic_slice_in_dim(q, q0, Q_BLOCK, axis=1)
        logits = jnp.einsum('bqhd,bqkhd->bhqk', qb, kb,
                            preferred_element_type=jnp.float32) * scale
        logits = logits + bias.astype(jnp.float32)[None, :, None, :]
        logits = jnp.where(valid[None, None], logits, NEG_INF)
        lse = jax.nn.logsumexp(logits, axis=-1)
        p = jnp.exp(logits - lse[..., None]).astype(vb.dtype)
        o = jnp.einsum('bhqk,bqkhd->bqhd', p, vb)
        return o, lse

    starts = jnp.arange(S // Q_BLOCK, dtype=jnp.int32) * Q_BLOCK
    o, lse = lax.map(block, starts)
    o = o.transpose(1, 0, 2, 3, 4).reshape(B, S, H, Dh)
    lse = lse.transpose(1, 0, 3, 2).reshape(B, S, H)
    return o, lse

def _token_mixer(xn, w_in, w_pool, pool_scale, w_a, w_b, w_o, rel_bias):
    B, S, _ = xn.shape
    u, q, k, v, g_pool, g_attn = jnp.split(xn @ w_in, SPLITS, axis=-1)

    ug = u.reshape(B, S, POOL_GROUPS, POOL_GROUP_DIM)
    pooled = jnp.stack([_centred_mean(ug[:, :, gi], w) for gi, w in enumerate(POOL_WINDOWS)], axis=2) - ug
    pool_out = jnp.einsum('bsgc,gcd->bsgd', pooled, w_pool).reshape(B, S, POOL_WIDTH) * pool_scale

    q = q.reshape(B, S, N_HEADS, HEAD_DIM)
    k = k.reshape(B, S, N_HEADS, HEAD_DIM)
    v = v.reshape(B, S, N_HEADS, HEAD_DIM)
    outs, lses = [], []
    for gi, (window, dilation) in enumerate(ATTN_GROUPS):
        hs = slice(gi * HEADS_PER_GROUP, (gi + 1) * HEADS_PER_GROUP)
        half = window // (2 * dilation)
        buckets = _t5_buckets(dilation * np.arange(-half, half + 1))
        bias = rel_bias[buckets][:, hs].T
        o_g, lse_g = _dilated_group(q[:, :, hs], k[:, :, hs], v[:, :, hs], bias, window, dilation)
        outs.append(o_g)
        lses.append(lse_g)
    wts = jax.nn.softmax(jnp.stack(lses, axis=0), axis=0)
    attn = jnp.einsum('gbsh,gbshd->bshd', wts, jnp.stack(outs, axis=0).astype(jnp.float32))
    attn_out = attn.astype(xn.dtype).reshape(B, S, ATTN_OUT)

    merged = jax.nn.sigmoid(g_pool) * (pool_out @ w_a) + jax.nn.sigmoid(g_attn) * (attn_out @ w_b)
    return merged @ w_o

def _conv_ffn(xn, w_up, conv_w, conv_b, w_down):
    a, gval = jnp.split(xn @ w_up, 2, axis=-1)
    a = lax.conv_general_dilated(a, conv_w[:, None, :], window_strides=(1,),
                                 padding=((CONV_WIDTH // 2, CONV_WIDTH // 2),),
                                 dimension_numbers=('NWC', 'WIO', 'NWC'),
                                 feature_group_count=D_FF) + conv_b
    return (jax.nn.gelu(a) * gval) @ w_down

def first_inputs(seed: int = 0) -> dict:
    key = jax.random.key(seed)
    ks = jax.random.split(key, 16)
    f32 = jnp.float32

    def nrm(k, shape, scale):
        return jax.random.normal(k, shape, f32) * scale

    return {
        "x": nrm(ks[0], (BATCH, SEQ, D_MODEL), 1.0),
        "w_in": nrm(ks[1], (DEPTH, D_MODEL, IN_WIDTH), D_MODEL ** -0.5),
        "w_pool": nrm(ks[2], (DEPTH, POOL_GROUPS, POOL_GROUP_DIM, POOL_GROUP_DIM), POOL_GROUP_DIM ** -0.5),
        "pool_scale": 1.0 + nrm(ks[3], (DEPTH, POOL_WIDTH), 0.02),
        "w_a": nrm(ks[4], (DEPTH, POOL_WIDTH, D_MODEL), POOL_WIDTH ** -0.5),
        "w_b": nrm(ks[5], (DEPTH, ATTN_OUT, D_MODEL), ATTN_OUT ** -0.5),
        "w_o": nrm(ks[6], (DEPTH, D_MODEL, D_MODEL), D_MODEL ** -0.5),
        "norm1": 1.0 + nrm(ks[7], (DEPTH, D_MODEL), 0.02),
        "norm2": 1.0 + nrm(ks[8], (DEPTH, D_MODEL), 0.02),
        "w_up": nrm(ks[9], (DEPTH, D_MODEL, 2 * D_FF), D_MODEL ** -0.5),
        "conv_w": nrm(ks[10], (DEPTH, CONV_WIDTH, D_FF), CONV_WIDTH ** -0.5),
        "conv_b": nrm(ks[11], (DEPTH, D_FF), 0.01),
        "w_down": nrm(ks[12], (DEPTH, D_FF, D_MODEL), D_FF ** -0.5),
        "rel_bias": nrm(ks[13], (N_BUCKETS, N_HEADS), 0.2),
        "norm_f": 1.0 + nrm(ks[14], (D_MODEL,), 0.02),
    }

def first_block(x, w_in, w_pool, pool_scale, w_a, w_b, w_o, norm1, norm2,
              w_up, conv_w, conv_b, w_down, rel_bias, norm_f):
    h = x
    for layer in range(DEPTH):
        h = h + _token_mixer(_rmsnorm(h, norm1[layer]), w_in[layer], w_pool[layer], pool_scale[layer],
                             w_a[layer], w_b[layer], w_o[layer], rel_bias)
        h = h + _conv_ffn(_rmsnorm(h, norm2[layer]), w_up[layer], conv_w[layer], conv_b[layer], w_down[layer])
    return _rmsnorm(h, norm_f)


N_EVEN = (DEPTH + 1) // 2
N_ODD = DEPTH // 2

HGRN_DIM = D_MODEL // 2
HGRN_HEAD_DIM = 128
HGRN_HEADS = HGRN_DIM // HGRN_HEAD_DIM
HGRN_CHUNK = 64

S5_DIM = D_MODEL - HGRN_DIM
S5_GROUP = 16
S5_GROUPS = S5_DIM // S5_GROUP
S5_STATE = 64
S5_DT_MIN = 1e-3
S5_DT_MAX = 1e-1

EVEN_IN = 4 * HGRN_DIM + S5_DIM

MLA_HEADS = 8
MLA_Q_RANK = 384
MLA_KV_RANK = 256
MLA_NOPE = 128
MLA_ROPE = 64
MLA_V = 128
MLA_QK = MLA_NOPE + MLA_ROPE
ODD_IN = MLA_Q_RANK + MLA_KV_RANK + MLA_ROPE
ROPE_THETA = 10000.0
Q_BLOCK_2 = 128

D_FF_2 = 2816
CONV_W = 3


def rmsnorm(x, g):
    xf = x.astype(jnp.float32)
    y = xf * lax.rsqrt(jnp.mean(xf * xf, axis=-1, keepdims=True) + EPS)
    return (y * g.astype(jnp.float32)).astype(x.dtype)

def hgrn2(q, f, i, g, lb, norm_g):
    f32 = jnp.float32
    B_, S_, _ = q.shape
    H, Dh, C = HGRN_HEADS, HGRN_HEAD_DIM, HGRN_CHUNK
    N = S_ // C
    lb = lb.astype(f32)
    forget = lb + (1.0 - lb) * jax.nn.sigmoid(f.astype(f32))
    key_in = 1.0 - forget

    def heads(t):
        return t.astype(f32).reshape(B_, N, C, H, Dh).transpose(0, 3, 1, 2, 4)

    qh, kh, vh = heads(q), heads(key_in), heads(i)
    b = jnp.cumsum(heads(jnp.log(forget)), axis=3)
    b_last = b[:, :, :, -1:, :]
    qd = qh * jnp.exp(b)
    kd = kh * jnp.exp(-b)
    causal = jnp.tril(jnp.ones((C, C), dtype=bool))
    att = jnp.where(causal, jnp.einsum('bhntd,bhnsd->bhnts', qd, kd), 0.0)
    o_intra = jnp.einsum('bhnts,bhnsv->bhntv', att, vh)
    d_state = jnp.einsum('bhnsd,bhnsv->bhndv', kh * jnp.exp(b_last - b), vh)
    decay = jnp.exp(b_last[:, :, :, 0, :])

    def step(state, inp):
        ds_n, dec_n = inp
        return dec_n[..., None] * state + ds_n, state

    s0 = jnp.zeros((B_, H, Dh, Dh), f32)
    _, s_start = lax.scan(step, s0, (d_state.transpose(2, 0, 1, 3, 4), decay.transpose(2, 0, 1, 3)))
    s_start = s_start.transpose(1, 2, 0, 3, 4)
    o = o_intra + jnp.einsum('bhntd,bhndv->bhntv', qd, s_start)
    o = o.transpose(0, 2, 3, 1, 4).reshape(B_, S_, H, Dh)
    o = o * lax.rsqrt(jnp.mean(o * o, axis=-1, keepdims=True) + EPS) * norm_g.astype(f32).reshape(H, Dh)
    return o.reshape(B_, S_, HGRN_DIM) * jax.nn.silu(g.astype(f32))

def s5(u, a_re, a_im, log_dt, b_re, b_im, c_re, c_im, d_skip, w_glu, b_glu):
    f32 = jnp.float32
    B_, S_, _ = u.shape
    G, P, Hc = S5_GROUPS, S5_STATE, S5_GROUP
    uf = u.astype(f32).reshape(B_, S_, G, Hc)
    ar, ai = a_re.astype(f32), a_im.astype(f32)
    dt = jnp.exp(log_dt.astype(f32))[:, None]
    mag = jnp.exp(ar * dt)
    abar_re, abar_im = mag * jnp.cos(ai * dt), mag * jnp.sin(ai * dt)
    den = ar * ar + ai * ai
    xr, xi = abar_re - 1.0, abar_im
    coef_re = ((xr * ar + xi * ai) / den)[..., None]
    coef_im = ((xi * ar - xr * ai) / den)[..., None]
    br, bi = b_re.astype(f32), b_im.astype(f32)
    bb_re = coef_re * br - coef_im * bi
    bb_im = coef_re * bi + coef_im * br
    bu_re = jnp.einsum('bsgh,gph->bsgp', uf, bb_re)
    bu_im = jnp.einsum('bsgh,gph->bsgp', uf, bb_im)
    a_seq_re = jnp.broadcast_to(abar_re, (1, S_, G, P))
    a_seq_im = jnp.broadcast_to(abar_im, (1, S_, G, P))

    def combine(left, right):
        a1r, a1i, b1r, b1i = left
        a2r, a2i, b2r, b2i = right
        return (a2r * a1r - a2i * a1i, a2r * a1i + a2i * a1r,
                a2r * b1r - a2i * b1i + b2r, a2r * b1i + a2i * b1r + b2i)

    _, _, s_re, s_im = lax.associative_scan(combine, (a_seq_re, a_seq_im, bu_re, bu_im), axis=1)
    y = (jnp.einsum('bsgp,ghp->bsgh', s_re, c_re.astype(f32))
         - jnp.einsum('bsgp,ghp->bsgh', s_im, c_im.astype(f32))
         + d_skip.astype(f32).reshape(G, Hc) * uf)
    z = jax.nn.gelu(y.reshape(B_, S_, S5_DIM))
    return z * jax.nn.sigmoid(z @ w_glu.astype(f32) + b_glu.astype(f32))

def even_mixer(hn, w_in, lb, hgrn_norm_g, a_re, a_im, log_dt, b_re, b_im, c_re, c_im,
               d_skip, w_glu, b_glu, w_out):
    proj = hn @ w_in
    q, f, i, g, u = jnp.split(proj, [HGRN_DIM, 2 * HGRN_DIM, 3 * HGRN_DIM, 4 * HGRN_DIM], axis=-1)
    y_a = hgrn2(q, f, i, g, lb, hgrn_norm_g).astype(hn.dtype)
    y_b = s5(u, a_re, a_im, log_dt, b_re, b_im, c_re, c_im, d_skip, w_glu, b_glu).astype(hn.dtype)
    return jnp.concatenate([y_a, y_b], axis=-1) @ w_out

def rotate(x, cos, sin):
    x1, x2 = jnp.split(x, 2, axis=-1)
    return jnp.concatenate([x1 * cos - x2 * sin, x1 * sin + x2 * cos], axis=-1)

def mla(hn, positions, w_in, q_norm_g, w_uq, kv_norm_g, w_ukv, w_out):
    B_, S_, _ = hn.shape
    H = MLA_HEADS
    proj = hn @ w_in
    cq, ckv, k_rope = jnp.split(proj, [MLA_Q_RANK, MLA_Q_RANK + MLA_KV_RANK], axis=-1)
    q = (rmsnorm(cq, q_norm_g) @ w_uq).reshape(B_, S_, H, MLA_QK)
    kv = (rmsnorm(ckv, kv_norm_g) @ w_ukv).reshape(B_, S_, H, MLA_NOPE + MLA_V)
    q_nope, q_rope = jnp.split(q, [MLA_NOPE], axis=-1)
    k_nope, v = jnp.split(kv, [MLA_NOPE], axis=-1)
    freqs = ROPE_THETA ** (-jnp.arange(0, MLA_ROPE, 2, dtype=jnp.float32) / MLA_ROPE)
    ang = positions.astype(jnp.float32)[..., None] * freqs
    cos = jnp.cos(ang)[:, :, None, :].astype(hn.dtype)
    sin = jnp.sin(ang)[:, :, None, :].astype(hn.dtype)
    q_rope = rotate(q_rope, cos, sin)
    k_rope = rotate(k_rope[:, :, None, :], cos, sin)
    q = jnp.concatenate([q_nope, q_rope], axis=-1)
    k = jnp.concatenate([k_nope, jnp.broadcast_to(k_rope, (B_, S_, H, MLA_ROPE))], axis=-1)
    scale = MLA_QK ** -0.5
    nb = S_ // Q_BLOCK_2
    qb = q.reshape(B_, nb, Q_BLOCK_2, H, MLA_QK).transpose(1, 0, 2, 3, 4)
    kpos = jnp.arange(S_)

    def attend(args):
        q_blk, blk = args
        s = jnp.einsum('bqhd,bkhd->bhqk', q_blk, k).astype(jnp.float32) * scale
        qpos = blk * Q_BLOCK_2 + jnp.arange(Q_BLOCK_2)
        s = jnp.where(kpos[None, :] <= qpos[:, None], s, -jnp.inf)
        p = jax.nn.softmax(s, axis=-1).astype(v.dtype)
        return jnp.einsum('bhqk,bkhd->bqhd', p, v)

    o = lax.map(attend, (qb, jnp.arange(nb)))
    o = o.transpose(1, 0, 2, 3, 4).reshape(B_, S_, H * MLA_V)
    return o @ w_out

def conv_ffn(hn, w_in, conv_w, conv_b, w_out):
    a, u = jnp.split(hn @ w_in, 2, axis=-1)
    a = lax.conv_general_dilated(a, conv_w[:, None, :], window_strides=(1,),
                                 padding=[(CONV_W - 1, 0)],
                                 dimension_numbers=('NWC', 'WIO', 'NWC'),
                                 feature_group_count=D_FF_2) + conv_b
    return (jax.nn.silu(a) * u) @ w_out

def second_inputs(seed: int = 0) -> dict:
    key = jax.random.key(seed)
    ks = iter(jax.random.split(key, 40))
    nrm = lambda shape, s: jax.random.normal(next(ks), shape, jnp.float32) * s
    D = D_MODEL
    G, P, Hc = S5_GROUPS, S5_STATE, S5_GROUP
    x = nrm((BATCH, SEQ, D), 1.0)
    offset = jax.random.randint(next(ks), (BATCH, 1), 0, SEQ)
    positions = (offset + jnp.arange(SEQ)[None, :]).astype(jnp.int32)
    return {
        "x": x,
        "positions": positions,
        "norm_mix_g": 1.0 + nrm((DEPTH, D), 0.02),
        "norm_ffn_g": 1.0 + nrm((DEPTH, D), 0.02),
        "final_norm_g": 1.0 + nrm((D,), 0.02),
        "even_w_in": nrm((N_EVEN, D, EVEN_IN), D ** -0.5),
        "hgrn_lb_logits": nrm((N_EVEN + 1, HGRN_DIM), 0.1),
        "hgrn_norm_g": 1.0 + nrm((N_EVEN, HGRN_DIM), 0.02),
        "s5_a_re": -0.5 + nrm((N_EVEN, G, P), 0.01),
        "s5_a_im": jnp.pi * jnp.arange(P, dtype=jnp.float32) + nrm((N_EVEN, G, P), 0.01),
        "s5_log_dt": jax.random.uniform(next(ks), (N_EVEN, G), jnp.float32,
                                        math.log(S5_DT_MIN), math.log(S5_DT_MAX)),
        "s5_b_re": nrm((N_EVEN, G, P, Hc), (2 * Hc) ** -0.5),
        "s5_b_im": nrm((N_EVEN, G, P, Hc), (2 * Hc) ** -0.5),
        "s5_c_re": nrm((N_EVEN, G, Hc, P), (2 * P) ** -0.5),
        "s5_c_im": nrm((N_EVEN, G, Hc, P), (2 * P) ** -0.5),
        "s5_d": nrm((N_EVEN, S5_DIM), 1.0),
        "s5_w_glu": nrm((N_EVEN, S5_DIM, S5_DIM), S5_DIM ** -0.5),
        "s5_b_glu": nrm((N_EVEN, S5_DIM), 0.02),
        "even_w_out": nrm((N_EVEN, HGRN_DIM + S5_DIM, D), (HGRN_DIM + S5_DIM) ** -0.5),
        "odd_w_in": nrm((N_ODD, D, ODD_IN), D ** -0.5),
        "mla_q_norm_g": 1.0 + nrm((N_ODD, MLA_Q_RANK), 0.02),
        "mla_w_uq": nrm((N_ODD, MLA_Q_RANK, MLA_HEADS * MLA_QK), MLA_Q_RANK ** -0.5),
        "mla_kv_norm_g": 1.0 + nrm((N_ODD, MLA_KV_RANK), 0.02),
        "mla_w_ukv": nrm((N_ODD, MLA_KV_RANK, MLA_HEADS * (MLA_NOPE + MLA_V)), MLA_KV_RANK ** -0.5),
        "odd_w_out": nrm((N_ODD, MLA_HEADS * MLA_V, D), (MLA_HEADS * MLA_V) ** -0.5),
        "ffn_w_in": nrm((DEPTH, D, 2 * D_FF_2), D ** -0.5),
        "ffn_conv_w": nrm((DEPTH, CONV_W, D_FF_2), CONV_W ** -0.5),
        "ffn_conv_b": nrm((DEPTH, D_FF_2), 0.02),
        "ffn_w_out": nrm((DEPTH, D_FF_2, D), D_FF_2 ** -0.5),
    }

def second_block(x, positions, norm_mix_g, norm_ffn_g, final_norm_g,
              even_w_in, hgrn_lb_logits, hgrn_norm_g,
              s5_a_re, s5_a_im, s5_log_dt, s5_b_re, s5_b_im, s5_c_re, s5_c_im,
              s5_d, s5_w_glu, s5_b_glu, even_w_out,
              odd_w_in, mla_q_norm_g, mla_w_uq, mla_kv_norm_g, mla_w_ukv, odd_w_out,
              ffn_w_in, ffn_conv_w, ffn_conv_b, ffn_w_out):
    lower_bounds = jnp.cumsum(jax.nn.softmax(hgrn_lb_logits.astype(jnp.float32), axis=0), axis=0)
    h = x
    for layer in range(DEPTH):
        j = layer // 2
        hn = rmsnorm(h, norm_mix_g[layer])
        if layer % 2 == 0:
            mix = even_mixer(hn, even_w_in[j], lower_bounds[j], hgrn_norm_g[j],
                             s5_a_re[j], s5_a_im[j], s5_log_dt[j], s5_b_re[j], s5_b_im[j],
                             s5_c_re[j], s5_c_im[j], s5_d[j], s5_w_glu[j], s5_b_glu[j],
                             even_w_out[j])
        else:
            mix = mla(hn, positions, odd_w_in[j], mla_q_norm_g[j], mla_w_uq[j],
                      mla_kv_norm_g[j], mla_w_ukv[j], odd_w_out[j])
        h = h + mix
        h = h + conv_ffn(rmsnorm(h, norm_ffn_g[layer]), ffn_w_in[layer], ffn_conv_w[layer],
                         ffn_conv_b[layer], ffn_w_out[layer])
    return rmsnorm(h, final_norm_g)


def setup_inputs(seed=0):
    out = dict(first_inputs(seed))
    for name, value in second_inputs(seed + 1).items():
        if name != "x":
            out[name + "_2"] = value
    return out


def reference(
    x, w_in, w_pool, pool_scale, w_a, w_b, w_o, norm1, norm2, w_up, conv_w, conv_b, w_down,
    rel_bias, norm_f, positions_2, norm_mix_g_2, norm_ffn_g_2, final_norm_g_2, even_w_in_2,
    hgrn_lb_logits_2, hgrn_norm_g_2, s5_a_re_2, s5_a_im_2, s5_log_dt_2, s5_b_re_2, s5_b_im_2,
    s5_c_re_2, s5_c_im_2, s5_d_2, s5_w_glu_2, s5_b_glu_2, even_w_out_2, odd_w_in_2,
    mla_q_norm_g_2, mla_w_uq_2, mla_kv_norm_g_2, mla_w_ukv_2, odd_w_out_2, ffn_w_in_2,
    ffn_conv_w_2, ffn_conv_b_2, ffn_w_out_2,
):
    x = first_block(
        x, w_in, w_pool, pool_scale, w_a, w_b, w_o, norm1, norm2, w_up, conv_w, conv_b, w_down,
        rel_bias, norm_f,
    )
    return second_block(
        x, positions_2, norm_mix_g_2, norm_ffn_g_2, final_norm_g_2, even_w_in_2,
        hgrn_lb_logits_2, hgrn_norm_g_2, s5_a_re_2, s5_a_im_2, s5_log_dt_2, s5_b_re_2,
        s5_b_im_2, s5_c_re_2, s5_c_im_2, s5_d_2, s5_w_glu_2, s5_b_glu_2, even_w_out_2,
        odd_w_in_2, mla_q_norm_g_2, mla_w_uq_2, mla_kv_norm_g_2, mla_w_ukv_2, odd_w_out_2,
        ffn_w_in_2, ffn_conv_w_2, ffn_conv_b_2, ffn_w_out_2,
    )


_drawn_inputs = setup_inputs


def setup_inputs(seed=0):
    import zlib

    import numpy as np

    out = dict(_drawn_inputs(seed))
    spreads = {}
    factors = {'pool_scale': 2.943,
     'conv_b': 5.437,
     'norm_mix_g_2': 2.71,
     'norm_ffn_g_2': 2.87,
     'final_norm_g_2': 8.29,
     'hgrn_norm_g_2': 6.321,
     's5_a_re_2': 64.0,
     's5_a_im_2': 32.088,
     's5_log_dt_2': 31.768,
     's5_b_re_2': 43.904,
     's5_b_im_2': 45.08,
     's5_c_re_2': 44.056,
     's5_c_im_2': 44.656,
     's5_b_glu_2': 8.0,
     'mla_q_norm_g_2': 8.0,
     'mla_kv_norm_g_2': 8.0,
     'ffn_conv_b_2': 4.167}
    for name, (base, spread) in spreads.items():
        noise = np.random.default_rng([zlib.crc32(name.encode()), seed]).standard_normal(out[name].shape)
        drawn = base * np.exp(spread * noise) if base else spread * noise
        out[name] = __import__('jax').numpy.asarray(drawn.astype(out[name].dtype))
    for name, factor in factors.items():
        out[name] = (out[name] * factor).astype(out[name].dtype)
    return out
```

```python
from contextlib import ExitStack

import concourse.bass as bass
from concourse import mybir
import numpy as np

F32 = mybir.dt.float32
F32R = mybir.dt.float32r
I32 = mybir.dt.int32
ACT = mybir.ActivationFunctionType
ALU = mybir.AluOpType
AX = mybir.AxisListType

P = 128
S = 256
ST = S // P
D = 1024
DC = D // P
DH = 128
SLOTS = 4
GROUPS = 3
HEADS = SLOTS * GROUPS
DILATIONS = (1, 4, 16)
HALF = 64
BUCKETS, MAX_DISTANCE = 32, 1024
TAB = 2 * S - 1
FF = 2816
FC = FF // P
PAIRS = FF // 256
EPS = 1e-6
NEG = -1e30
PADT = 8
WIDE = 2048
RAW = 3
SPL = 2
BANK = 512
SG, SP_ = 32, 64
SC = SG * SP_ // P
NS5 = 4 * P + SC
NANG = NS5 + S
CH = 64
MH = 8
TWO_PI = float(2 * np.pi)
C1 = 6.28125
C2 = float(np.float32(0.0019350051879882812))
C3 = TWO_PI - C1 - C2
MAGIC = 12582912.0


class Block:

    def __init__(self, kind, n, ncol, kc, tiles, banks, start=True, stop=True):
        self.kind, self.n, self.ncol, self.kc, self.tiles, self.banks = kind, n, ncol, kc, tiles, banks
        self.start, self.stop, self.used = start, stop, kc * ncol


def ftiles(cols, kc, x0=0):
    return [(t * S, "f", [(c, x0 + c) for c in range(kc)], t * P, P, 0) for t in range(cols // P)]


def ttiles(cols, kc, c0=0, base=0):
    return [(base + t * cols, "t", [(c, c) for c in range(kc)], c0, cols, t) for t in range(ST)]


def make_plan():
    plan = []

    def ffn(n):
        for j in range(PAIRS):
            plan.append(Block("up_a", n, 256, DC, ftiles(256, DC), 1))
            plan.append(Block("up_g", n, 256, DC, ftiles(256, DC), 1))
        for j in range(4):
            for k, (c0, kc) in enumerate(((0, 8), (8, 8), (16, 6))):
                plan.append(Block("down", n, 256, kc, ftiles(256, kc, c0), 1, k == 0, k == 2))

    for layer in range(2):
        for kind, count in (("v", 6), ("q", 6), ("k", 6), ("u", 4), ("gp", 4), ("ga", 4)):
            tiles = ttiles(256, DC) if kind == "v" else ftiles(256, DC)
            plan += [Block(kind, layer, 256, DC, tiles, 1) for _ in range(count)]
        pool = [((2 * g + t) * S, "f", [(2 * g + c, 2 * g + c) for c in range(2)], t * P, P, 0)
                for g in range(4) for t in range(2)]
        plan.append(Block("pool", layer, 256, DC, pool, 4))
        plan += [Block("wa", layer, 256, DC, ftiles(256, DC), 1) for _ in range(4)]
        plan += [Block("wb", layer, 512, 4, ftiles(512, 4), 2) for _ in range(2)]
        plan += [Block("wo", layer, 256, DC, ftiles(256, DC), 1) for _ in range(4)]
        ffn(layer)
    for kind in ("ef", "eq", "ei", "eg", "eu"):
        tiles = ttiles(256, DC) if kind == "ei" else ftiles(256, DC)
        plan += [Block(kind, 0, 256, DC, tiles, 1) for _ in range(2)]
    plan.append(Block("glu", 0, 512, 4, ftiles(512, 4, 4), 2))
    plan += [Block("eo", 0, 256, DC, ftiles(256, DC), 1) for _ in range(4)]
    ffn(2)
    plan += [Block("mp", 0, 256, DC, ftiles(256, DC), 1) for _ in range(3)]
    plan += [Block("uq", 0, 384, 3, ftiles(384, 3), 2) for _ in range(4)]
    plan += [Block("ukv", 0, 1024, 2, [(t * S, "f", [(c, 3 + c) for c in range(2)], t * P, P, 0) for t in range(4)]
                   + [(1024 + t * 512, "t", [(c, 3 + c) for c in range(2)], 512, 512, t) for t in range(ST)], 4)
             for _ in range(2)]
    plan += [Block("mo", 0, 256, DC, ftiles(256, DC), 1) for _ in range(4)]
    ffn(3)

    out, last, turn, bank = 0, [0] * 4, 0, 0
    for b in plan:
        if b.start:
            if b.banks == 1:
                bank, turn = turn, (turn + 1) % 3
            else:
                bank, turn = 0, 0
            b.freed = max(last[bank:bank + b.banks])
        else:
            b.freed = 0
        b.bank = bank
        if b.stop:
            out += 1
            b.out = out
            for k in range(bank, bank + b.banks):
                last[k] = out
    return plan


PLAN = make_plan()
OFFSETS = [0]
for _b in PLAN:
    OFFSETS.append(OFFSETS[-1] + _b.used)


def first(kind, n=0):
    return next(i for i, b in enumerate(PLAN) if b.kind == kind and b.n == n)


def count(kind, n=0):
    return sum(b.kind == kind and b.n == n for b in PLAN)


VECTORS = ([(f"norm1.{i}", 8) for i in range(2)] + [(f"norm2.{i}", 8) for i in range(2)] + [("norm_f", 8)]
           + [(f"pool_scale.{i}", 8) for i in range(2)]
           + [(f"conv{k}.{n}", FC) for n in range(4) for k in range(3)] + [(f"convb.{n}", FC) for n in range(4)]
           + [(f"mix.{i}", 8) for i in range(2)] + [(f"ffn.{i}", 8) for i in range(2)] + [("final", 8)]
           + [("lb0", 4), ("lb1", 4), ("hgrn_g", 4), ("s5_d", 4), ("b_glu", 4), ("q_g", 3), ("kv_g", 2)])
COL, NPAR = {}, 0
for _name, _n in VECTORS:
    COL[_name] = NPAR
    NPAR += _n
FFN_NORM = ("norm2.0", "norm2.1", "ffn.0", "ffn.1")

CONSTS = (("ident", P), ("rotate", P), ("causal", P), ("inv_count", 4 * S), ("freq", 1), ("chunk_causal", CH))
CCOL, NCONST = {}, 0
for _name, _n in CONSTS:
    CCOL[_name] = NCONST
    NCONST += _n


class Side:

    def __init__(self, eng, own):
        self.eng, self.own, self.given, self.taken, self.last = eng, own, {}, {}, None

    def give(self, ins, sem=None):
        sem = sem or self.own
        ins.then_inc(sem, 1)
        self.given[sem.name] = self.given.get(sem.name, 0) + 1
        self.last = (sem, self.given[sem.name])
        return ins

    def take(self, sem, events=1):
        self.taken[sem.name] = self.taken.get(sem.name, 0) + events
        self.eng.wait_ge(sem, self.taken[sem.name])

    def settle(self):
        self.eng.wait_ge(*self.last)


def two_blocks_kernel(nc, a):
    ctx = ExitStack()
    with ctx:
        base = [(nc.sbuf_base + 31) // 32 * 32]

        def region(size):
            at = base[0]
            base[0] += size
            return at

        def tile(name, at, shape, dt=F32):
            return nc.alloc_sbuf_tensor_at(name, shape, dt, offset=at)

        K = 1024
        raw = [tile(f"raw{j}", region(8 * K), [P, WIDE]) for j in range(RAW)]
        w_hi = [tile(f"w_hi{j}", region(8 * K), [P, WIDE], F32R) for j in range(SPL)]
        w_lo = [tile(f"w_lo{j}", region(8 * K), [P, WIDE], F32R) for j in range(SPL)]
        h = tile("h", region(8 * K), [P, DC, S])
        x_hi = tile("x_hi", region(8 * K), [P, DC, S], F32R)
        x_lo = tile("x_lo", region(8 * K), [P, DC, S], F32R)
        tmp = tile("tmp", region(8 * K), [P, DC, S])
        r_bm, r_hid, r_gate, r_att = region(24 * K), region(45568), region(16 * K), region(14 * K)
        par = tile("par", region(NPAR * 4 + 31 & ~31), [P, NPAR])
        cst = tile("cst", region(NCONST * 4 + 31 & ~31), [P, NCONST])
        ones = tile("ones", region(512), [P, P])
        small = tile("small", region(256), [P, 64])
        cos_r = tile("cos_r", region(K), [P, 1, S])
        sin_r = tile("sin_r", region(K), [P, 1, S])
        s5_st = tile("s5_st", region(256), [P, 4, SC])
        bb = tile("bb", region(4 * K), [P, 2, 4, P])
        assert base[0] <= nc.sbuf_usable_end, base[0]

        bm = tile("bm", r_bm, [P, ST, SLOTS, GROUPS * S])
        qt = tile("qt", r_hid, [P, HEADS, S])
        kt = tile("kt", r_hid + 12 * K, [P, HEADS, S])
        va = tile("va", r_hid + 24 * K, [P, ST, HEADS * DH])
        ub = tile("ub", r_hid + 36 * K, [P, DC, S + 2 * PADT])
        ph = tile("ph", r_hid, [P, DC, S], F32R)
        pl = tile("pl", r_hid + 8 * K, [P, DC, S], F32R)
        gate_p = tile("gate_p", r_gate, [P, DC, S])
        gate_a = tile("gate_a", r_gate + 8 * K, [P, DC, S])
        lg = tile("lg", r_att, [P, GROUPS * S])
        pt = tile("pt", r_att + 3 * K, [P, GROUPS * ST, P])
        ao_h = tile("ao_h", r_att + 6 * K, [P, SLOTS, S], F32R)
        ao_l = tile("ao_l", r_att + 10 * K, [P, SLOTS, S], F32R)
        yh = tile("yh", r_hid, [P, FC, S], F32R)
        yl = tile("yl", r_hid + FC * K, [P, FC, S], F32R)
        cv = tile("cv", r_att, [P, 2, 2, S])
        rms = tile("rms", r_att, [P, 2 * S])
        ec = tile("ec", r_bm, [P, SC, S])
        es = tile("es", r_gate, [P, SC, S])
        etmp = tile("etmp", r_bm + 16 * K, [P, SC, P])
        names = ("fe", "key", "qb", "cum", "dd", "eb", "enb", "v2", "sg", "mask")
        fe, key, qb, cum, dd, eb, enb, v2, sgate, smask = (
            tile(n, r_hid + 4 * K * j, [P, 4 * S]) for j, n in enumerate(names))
        uu = tile("uu", r_hid + 40 * K, [P, 4 * S])
        am = tile("am", r_bm + 16 * K, [P, 8, P])
        ket = tile("ket", r_bm + 20 * K, [P, 8, P])
        st = tile("st", r_att + 2 * K, [P, 3, 4, P])
        cc = tile("cc", r_att + 8 * K, [P, 2, SC, 32])
        t_s5 = [tile(f"t_s5_{j}", r_hid + 4 * K * j, [P, 4 * S]) for j in range(10)]
        c6 = tile("c6", r_hid, [P, 6, S])
        qn = tile("qn", r_hid + 6 * K, [P, MH, S])
        rx = tile("rx", r_hid + 14 * K, [P, 4, S])
        kn = tile("kn", r_hid + 18 * K, [P, MH, S])
        v3 = tile("v3", r_hid + 26 * K, [P, ST, MH * DH])
        qr = tile("qr", r_hid + 34 * K, [P, 4, S])
        kr = tile("kr", r_hid + 38 * K, [P, 1, S])
        lm = tile("lm", r_gate, [P, 2, 3, P])
        pm = tile("pm", r_gate + 3 * K, [P, 3 * P])
        NB = NANG * 4 + 31 & ~31
        ang = [tile(f"ang{j}", r_bm + NB * j if j < 7 else r_hid + 13 * K + NB * (j - 7), [P, NANG]) for j in range(10)]
        s5x = [tile(f"s5x{j}", r_hid + 2112 * j, [P, NS5]) for j in range(6)]
        relw = tile("relw", r_hid + 24 * K, [BUCKETS + 1, HEADS, P])
        pos_i = tile("pos_i", r_hid + 30 * K, [P, S], I32)
        tab = tile("tab", r_gate, [P, 2, SLOTS, TAB + 1])
        hot = tile("hot", r_att + 2 * K, [BUCKETS + 1, GROUPS * (TAB + 1)])
        relb = tile("relb", r_att + 8 * K, [BUCKETS + 1, HEADS])
        s5b = tile("s5b", r_att + 9 * K, [P, 2, 4 * P])
        assert 7 * NB <= 24 * K and 13 * K + 3 * NB <= 24 * K
        tab_dram = nc.dram_tensor("bias_table", (HEADS, P, TAB + 1), F32, kind="Internal").ap()

        pool_w = [tile(f"pool_w{j}", region(2176), [P, 2, S + 2 * PADT]) for j in range(2)]
        assert base[0] <= nc.sbuf_usable_end, base[0]

        G = ctx.enter_context(nc.psum_tensor("gemm", [P, 4 * BANK], F32))
        A = ctx.enter_context(nc.psum_tensor("aux", [P, 4 * BANK], F32))
        ident = cst[:, CCOL["ident"]:CCOL["ident"] + P]
        rotate = cst[:, CCOL["rotate"]:CCOL["rotate"] + P]
        causal = cst[:, CCOL["causal"]:CCOL["causal"] + P]
        freq = cst[:, CCOL["freq"]:CCOL["freq"] + 1]
        ccausal = cst[:, CCOL["chunk_causal"]:CCOL["chunk_causal"] + CH].bitcast(I32)
        eps = small[:, 0:1]
        lb, omlb, nbglu = small[:, 4:8], small[:, 8:12], small[:, 12:16]
        lbt = small[:, 16:28]
        mx, nm, sums, rs = small[:, 28:30], small[:, 30:32], small[:, 32:34], small[:, 34:36]

        def vec(name, c):
            return par[:, COL[name] + c:COL[name] + c + 1]

        def inv_count(g):
            return cst[:, CCOL["inv_count"] + g * S:CCOL["inv_count"] + (g + 1) * S]

        def sem(name):
            return ctx.enter_context(nc.semaphore(name))

        x_in, par_in, cst_in = sem("x_in"), sem("par_in"), sem("cst_in")
        s5_in, s5b_in, pos_in, hot_in, cc_in = sem("s5_in"), sem("s5b_in"), sem("pos_in"), sem("hot_in"), sem("cc_in")
        relb_in, bm_in = sem("relb_in"), sem("bm_in")
        tab_out = [sem(f"tab_out{j}") for j in range(GROUPS)]
        raw_in = [sem(f"raw_in{j}") for j in range(RAW)]
        out_done = sem("out_done")
        w_hi_ready, w_lo_ready = sem("w_hi_ready"), sem("w_lo_ready")
        mm_done = sem("mm_done")
        read_out = sem("read_out")
        act_own, dve_own, pool_own = sem("act_own"), sem("dve_own"), sem("pool_own")
        ones_ready = sem("ones_ready")
        x_f32, x_hi_ready, x_ready = sem("x_f32"), sem("x_hi_ready"), sem("x_ready")
        sq_ready, ms_ready, rms_ready, hf_ready = sem("sq_ready"), sem("ms_ready"), sem("rms_ready"), sem("hf_ready")
        relb_ready, tab_ready, tab_copied = sem("relb_ready"), sem("tab_ready"), sem("tab_copied")
        dt_ready, th_ready, mag_ready, red_ready = sem("dt_ready"), sem("th_ready"), sem("mag_ready"), sem("red_ready")
        trig_ready, den_ready, bb_ready, ndt_ready = sem("trig_ready"), sem("den_ready"), sem("bb_ready"), sem("ndt_ready")
        rope_kept = sem("rope_kept")
        qkv_ready, scores_ready, scores_read = sem("qkv_ready"), sem("scores_ready"), sem("scores_read")
        lg_ready, exp_ready, prob_ready = sem("lg_ready"), sem("exp_ready"), sem("prob_ready")
        tr_ready, pt_ready = sem("tr_ready"), sem("pt_ready")
        pv_ready, pv_hi, pv_read = sem("pv_ready"), sem("pv_hi"), sem("pv_read")
        u_zero, u_ready, pooled = sem("u_zero"), sem("u_ready"), sem("pooled")
        gate_exp = sem("gate_exp")
        conv_mid, act_ready, prod_ready, y_hi, y_ready = (sem("conv_mid"), sem("act_ready"), sem("prod_ready"),
                                                           sem("y_hi"), sem("y_ready"))
        e_ready, smask_ready, am_zero, cc_ready = sem("e_ready"), sem("smask_ready"), sem("am_zero"), sem("cc_ready")
        rden_ready, lbd_ready, lbe_ready = sem("rden_ready"), sem("lbd_ready"), sem("lbe_ready")
        f_ready, ln_ready, cum_ready, eb_ready, qd_ready = (sem("f_ready"), sem("ln_ready"), sem("cum_ready"),
                                                            sem("eb_ready"), sem("qd_ready"))
        att_ready, am_ready, ket_psum, ket_ready = sem("att_ready"), sem("am_ready"), sem("ket_psum"), sem("ket_ready")
        ds_ready, st_ready, o_ready = sem("ds_ready"), sem("st_ready"), sem("o_ready")
        bu_ready, bu_read, z_ready, z_read, s_ready, ys_ready = (sem("bu_ready"), sem("bu_read"), sem("z_ready"),
                                                                 sem("z_read"), sem("s_ready"), sem("ys_ready"))
        yd_ready, zg_ready, s5_free = sem("yd_ready"), sem("zg_ready"), sem("s5_free")
        rx_ready, rot_ready, rope_ready = sem("rx_ready"), sem("rot_ready"), sem("rope_ready")
        final_ready = sem("final_ready")

        block = ctx.enter_context(nc.Block())
        N = len(PLAN)

        @block.sync
        def _(sp):
            def load(dst, src, s):
                sp.dma_start(dst, src).then_inc(s, 16)

            load(h[:, :, :], a["x"].rearrange("(c p) s -> p c s", p=P), x_in)
            load(par[:, :], a["params"], par_in)
            load(cst[:, :], a["consts"], cst_in)
            load(relb[0:BUCKETS, :], a["rel_bias"], relb_in)
            load(hot[:, :], a["onehot"], hot_in)

            def weights(i):
                b = PLAN[i]
                if i >= RAW:
                    sp.wait_ge(w_lo_ready, i - RAW + 1)
                load(raw[i % RAW][:, 0:b.used],
                     a["weights"][OFFSETS[i] * P:OFFSETS[i + 1] * P].rearrange("(p n) -> p n", p=P), raw_in[i % RAW])

            for i in range(RAW):
                weights(i)
            for j in range(3):
                load(ang[j][:, 0:NS5], a["s5_abt"][j], s5_in)
            load(s5b[:, :, :], a["s5_b"], s5b_in)
            load(pos_i[:, :], a["positions"].to_broadcast([P, S]), pos_in)

            def store_table(g):
                sp.wait_ge(tab_copied, g + 1)
                load(tab_dram[g * SLOTS:(g + 1) * SLOTS].rearrange("h p n -> p h n"), tab[:, g % 2, :, :], tab_out[g])

            def load_bias():
                for s_ in tab_out:
                    sp.wait_ge(s_, 16)
                sp.wait_ge(bb_ready, 1)
                for q in range(ST):
                    for s in range(SLOTS):
                        src = bass.AP(tab_dram.tensor, s * P * (TAB + 1) + S - 1 - q * P,
                                      [[TAB, P], [SLOTS * P * (TAB + 1), GROUPS], [1, S]])
                        load(bm[:, q, s, :].rearrange("p (g n) -> p g n", g=GROUPS), src, bm_in)

            for i in range(RAW, N):
                weights(i)
                if 4 <= i < 4 + GROUPS:
                    store_table(i - 4)
                if i == first("q", 0) + 3:
                    load_bias()
                if i == first("down", 1) + 6:
                    load(cc[:, :, :, :], a["s5_c"], cc_in)
            sp.wait_ge(final_ready, 1)
            load(a["out"].rearrange("(c p) s -> p c s", p=P), tmp[:, :, :], out_done)
            sp.wait_ge(out_done, 16)

        @block.tensor
        def _(pe):
            me = Side(pe, None)

            def gemm(i, hi, lo, chunks_at=()):
                b = PLAN[i]
                wh = w_hi[i % SPL][:, 0:b.used].rearrange("p (c n) -> p c n", c=b.kc)
                wl = w_lo[i % SPL][:, 0:b.used].rearrange("p (c n) -> p c n", c=b.kc)
                pe.wait_ge(w_lo_ready, i + 1)
                if b.freed:
                    pe.wait_ge(read_out, b.freed)
                todo = dict(chunks_at)
                mm = None
                for at, (off, kind, pairs, c0, n, t) in enumerate(b.tiles):
                    o = b.bank * BANK + off
                    for k, (wc, xc) in enumerate(pairs):
                        if xc in todo:
                            me.take(*todo.pop(xc))
                        fresh = b.start and k == 0 and (at == 0 or b.stop)
                        end = b.stop and k == len(pairs) - 1
                        if kind == "f":
                            out = G[:, o:o + S]
                            two = [(wh[:, wc, c0:c0 + P], hi[:, xc, :]), (wh[:, wc, c0:c0 + P], lo[:, xc, :]),
                                   (wl[:, wc, c0:c0 + P], hi[:, xc, :])]
                        else:
                            out = G[:, o:o + n]
                            tok = slice(t * P, (t + 1) * P)
                            two = [(hi[:, xc, tok], wh[:, wc, c0:c0 + n]), (hi[:, xc, tok], wl[:, wc, c0:c0 + n]),
                                   (lo[:, xc, tok], wh[:, wc, c0:c0 + n])]
                        for m, (lhs, rhs) in enumerate(two):
                            mm = pe.matmul(out, lhs, rhs, start=fresh and m == 0, stop=end and m == 2,
                                           skip_group_check=True)
                me.give(mm, mm_done)

            def mean_square(chunks, outs):
                me.take(sq_ready)
                mm = None
                for cs, o in zip(chunks, outs):
                    for k, c in enumerate(cs):
                        mm = pe.matmul(A[:, o:o + S], ones[:, :], tmp[:, c, :], start=k == 0, stop=k == len(cs) - 1,
                                       skip_group_check=True)
                me.give(mm, ms_ready)

            def norm():
                mean_square([range(DC)], [0])

            HALVES = {0: (x_ready, 1), 4: (x_ready, 1)}

            def ffn(n):
                norm()
                i = first("up_a", n)
                for j in range(2 * PAIRS):
                    gemm(i + j, x_hi, x_lo, HALVES if j == 0 else ())
                i += 2 * PAIRS
                for j in range(12):
                    wait = {0: {0: (y_ready, 4)}, 1: {8: (y_ready, 4)}, 2: {16: (y_ready, 3)}}.get(j, ())
                    gemm(i + j, yh, yl, wait)

            def scores(u):
                s, q = divmod(u, ST)
                me.take(scores_read) if u else None
                mm = None
                for g in range(GROUPS):
                    hd = g * SLOTS + s
                    mm = pe.matmul(A[:, g * S:(g + 1) * S], qt[:, hd, q * P:(q + 1) * P], kt[:, hd, :],
                                   start=True, stop=True, skip_group_check=True)
                me.give(mm, scores_ready)

            def turn(u):
                me.take(prob_ready)
                mm = None
                for k in range(GROUPS * ST):
                    mm = pe.transpose(A[:, 2 * BANK + k * P:2 * BANK + (k + 1) * P], lg[:, k * P:(k + 1) * P], ident)
                me.give(mm, tr_ready)

            def pv(u, layer):
                s, q = divmod(u, ST)
                me.take(pt_ready)
                if u:
                    me.take(pv_read)
                mm = None
                for k in range(GROUPS * ST):
                    hd = (k // ST) * SLOTS + s
                    mm = pe.matmul(G[:, 3 * BANK:3 * BANK + P], va[:, k % ST, hd * DH:(hd + 1) * DH], pt[:, k, :],
                                   start=k == 0, stop=k == GROUPS * ST - 1, skip_group_check=True)
                me.give(mm, pv_ready)

            def mixer(layer):
                norm()
                i = first("v", layer)
                for j in range(18):
                    gemm(i + j, x_hi, x_lo, HALVES if j == 0 else ())
                me.take(qkv_ready)
                for j in range(12):
                    gemm(i + 18 + j, x_hi, x_lo)
                    if j < 8:
                        scores(j)
                    if 2 <= j < 10:
                        pv(j - 2, layer)
                    if 1 <= j < 9:
                        turn(j - 1)
                me.take(pv_read)
                me.take(scores_read)
                gemm(first("pool", layer), x_hi, x_lo, {0: (x_ready, 1)})
                for j in range(4):
                    gemm(first("wa", layer) + j, ph, pl, HALVES if j == 0 else ())
                for j in range(2):
                    gemm(first("wb", layer) + j, ao_h, ao_l)
                for j in range(4):
                    gemm(first("wo", layer) + j, x_hi, x_lo, HALVES if j == 0 else ())
                ffn(layer)

            pe.wait_ge(hot_in, 16)
            me.take(relb_ready)
            for g in range(GROUPS):
                if g:
                    me.take(tab_copied)
                for s in range(SLOTS):
                    mm = pe.matmul(A[:, s * BANK:(s + 1) * BANK], relw[:, g * SLOTS + s, :],
                                   hot[:, g * (TAB + 1):(g + 1) * (TAB + 1)], start=True, stop=True)
                me.give(mm, tab_ready)
            me.take(tab_copied)
            me.take(ones_ready)
            pe.wait_ge(cst_in, 16)
            for layer in range(2):
                mixer(layer)

            norm()
            norm()
            i = first("ef")
            for j in range(10):
                gemm(i + j, x_hi, x_lo, HALVES if j == 0 else ())
            me.take(qd_ready)
            q4 = qb.rearrange("p (c s) -> p c s", c=4)
            k4 = enb.rearrange("p (c s) -> p c s", c=4)
            ke4 = dd.rearrange("p (c s) -> p c s", c=4)
            v24 = v2.rearrange("p (t n) -> p t n", t=ST)
            for c in range(4):
                for n in range(4):
                    r, o = CH * (n % 2), (2 * c + n // 2) * CH
                    mm = pe.matmul(A[r:r + CH, o:o + CH], k4[:, c, n * CH:(n + 1) * CH], q4[:, c, n * CH:(n + 1) * CH],
                                   start=True, stop=True, skip_group_check=True)
            me.give(mm, att_ready)
            for c in range(4):
                for t in range(ST):
                    o = BANK + (2 * c + t) * P
                    mm = pe.transpose(A[:, o:o + P], ke4[:, c, t * P:(t + 1) * P], ident)
            me.give(mm, ket_psum)
            me.take(ket_ready)
            for n in range(3):
                if n:
                    me.take(st_ready)
                r, t = CH * (n % 2), n // 2
                for c in range(4):
                    mm = pe.matmul(A[:, 3 * BANK + c * P:3 * BANK + (c + 1) * P], ket[r:r + CH, 2 * c + t, :],
                                   v24[r:r + CH, t, c * P:(c + 1) * P], start=True, stop=True, skip_group_check=True)
                me.give(mm, ds_ready)
            me.take(am_ready)
            me.take(st_ready)
            for c in range(4):
                for t in range(ST):
                    o = BANK + c * S + t * P
                    mm = pe.matmul(A[:, o:o + P], v24[:, t, c * P:(c + 1) * P], am[:, 2 * c + t, :],
                                   start=True, stop=False, skip_group_check=True)
                    for n in range(2 * t, 2 * t + 2):
                        if n:
                            oo = o + (n % 2) * CH
                            mm = pe.matmul(A[:, oo:oo + CH], st[:, n - 1, c, :], q4[:, c, n * CH:(n + 1) * CH],
                                           start=False, stop=n % 2 == 1, skip_group_check=True)
            me.give(mm, o_ready)
            mean_square([[0], [1], [2], [3]], [0, S, 3 * BANK, 3 * BANK + S])
            me.take(cc_ready)
            me.take(bb_ready)
            me.take(s5_free)
            u4 = uu.rearrange("p (c s) -> p c s", c=4)

            def s5_in_mm(g):
                if g:
                    me.take(bu_read)
                m = None
                for part in range(2):
                    for k in range(4):
                        o = k * BANK + part * S
                        m = pe.matmul(A[:, o:o + S], bb[32 * k:32 * k + 32, part, g, :], u4[32 * k:32 * k + 32, g, :],
                                      start=True, stop=True, skip_group_check=True, tile_position=(32 * k, 0))
                me.give(m, bu_ready)

            def s5_out_mm(g):
                me.take(s_ready)
                m = None
                sre = t_s5[6].rearrange("p (c s) -> p c s", c=4)
                sim = t_s5[8].rearrange("p (c s) -> p c s", c=4)
                for k in range(4):
                    o = G[32 * k:32 * k + 32, g * BANK:g * BANK + S]
                    pe.matmul(o, cc[:, 0, 4 * g + k, :], sre[:, k, :], start=True, stop=False, skip_group_check=True,
                              tile_position=(0, 32 * k))
                    m = pe.matmul(o, cc[:, 1, 4 * g + k, :], sim[:, k, :], start=False, stop=True,
                                  skip_group_check=True, tile_position=(0, 32 * k))
                me.give(m, ys_ready)

            pe.wait_ge(read_out, PLAN[first("eu") + 1].out)
            s5_in_mm(0)
            for g in range(4):
                if g < 3:
                    s5_in_mm(g + 1)
                s5_out_mm(g)
            me.take(x_ready)
            pe.wait_ge(yd_ready, 4)
            gemm(first("glu"), x_hi, x_lo, {4: (x_ready, 1)})
            for j in range(4):
                gemm(first("eo") + j, x_hi, x_lo, {4: (x_ready, 1)} if j == 0 else ())
            ffn(2)

            norm()
            for j in range(3):
                gemm(first("mp") + j, x_hi, x_lo, HALVES if j == 0 else ())
            mean_square([[0, 1, 2], [3, 4]], [0, S])
            for j in range(4):
                gemm(first("uq") + j, x_hi, x_lo, {0: (x_ready, 1)} if j == 0 else ())
            for j in range(2):
                gemm(first("ukv") + j, x_hi, x_lo)
            me.take(rx_ready)
            rxf = rx.rearrange("p c s -> p (c s)")
            for k in range(2):
                pe.matmul(A[:, k * BANK:(k + 1) * BANK], rotate, rxf[:, k * BANK:(k + 1) * BANK], start=True, stop=True)
            mm = pe.matmul(A[:, 2 * BANK:2 * BANK + S], rotate, c6[:, 5, :], start=True, stop=True)
            me.give(mm, rot_ready)
            me.take(rope_ready)

            def m_scores(hd):
                if hd >= 2:
                    me.take(scores_read)
                b0, r = (hd % 2) * BANK, 64 * (hd % 2)
                m = None
                for q in range(ST):
                    nk = (q + 1) * P
                    o = A[:, b0 + q * P:b0 + q * P + nk]
                    pe.matmul(o, qn[:, hd, q * P:(q + 1) * P], kn[:, hd, 0:nk], start=True, stop=False,
                              skip_group_check=True)
                    m = pe.matmul(o, qr[r:r + 64, hd // 2, q * P:(q + 1) * P], kr[r:r + 64, 0, 0:nk], start=False,
                                  stop=True, skip_group_check=True)
                me.give(m, scores_ready)

            for j in range(MH + 2):
                if j < MH:
                    m_scores(j)
                if j >= 2:
                    hd = j - 2
                    me.take(pt_ready)
                    if hd:
                        me.take(pv_read)
                    o = 3 * BANK
                    pe.matmul(A[:, o:o + S], v3[:, 0, hd * DH:(hd + 1) * DH], pm[:, 0:S], start=True, stop=False,
                              skip_group_check=True)
                    mm = pe.matmul(A[:, o + P:o + S], v3[:, 1, hd * DH:(hd + 1) * DH], pm[:, S:S + P], start=False,
                                   stop=True, skip_group_check=True)
                    me.give(mm, pv_ready)
                if 1 <= j <= MH:
                    me.take(prob_ready)
                    for k in range(3):
                        mm = pe.transpose(A[:, 2 * BANK + k * P:2 * BANK + (k + 1) * P], lm[:, (j - 1) % 2, k, :], ident)
                    me.give(mm, tr_ready)
            me.take(scores_read, 2)
            me.take(pv_read)
            for j in range(4):
                gemm(first("mo") + j, x_hi, x_lo)
            ffn(3)
            norm()

        @block.scalar
        def _(act):
            me = Side(act, act_own)

            def split(i):
                if i >= N:
                    return
                n = PLAN[i].used
                act.wait_ge(raw_in[i % RAW], 16 * (i // RAW + 1))
                if i >= SPL:
                    act.wait_ge(mm_done, i - SPL + 1)
                me.give(act.activation(w_hi[i % SPL][:, 0:n], raw[i % RAW][:, 0:n], ACT.Copy), w_hi_ready)

            def split_all(i, n):
                for k in range(n):
                    split(i + k + SPL)

            def hi(dst, src):
                me.take(x_f32)
                me.give(act.activation(dst, src, ACT.Copy), x_hi_ready)

            def root(outs):
                me.take(ms_ready)
                for k, (dst, off, width, count_) in enumerate(outs):
                    ins = act.activation(dst, A[:, off:off + width], ACT.Sqrt, bias=eps, scale=1.0 / count_)
                me.give(ins, rms_ready)

            def norm(split_it=True):
                me.give(act.activation(tmp[:, :, :], h[:, :, :], ACT.Square), sq_ready)
                root([(rms[:, 0:S], 0, S, D)])
                if split_it:
                    for k in (0, 4):
                        hi(x_hi[:, k:k + 4, :], tmp[:, k:k + 4, :])

            def after(kind, n):
                i = first(kind, n) + count(kind, n) - 1
                act.wait_ge(read_out, PLAN[i].out)

            def psum(i):
                b = PLAN[i]
                act.wait_ge(mm_done, i + 1)
                return G[:, b.bank * BANK:(b.bank + b.banks) * BANK]

            def ffn(n):
                norm()
                i = first("up_a", n)
                centre = 1 if n < 2 else 2
                func = ACT.Gelu_apprx_tanh if n < 2 else ACT.Silu
                for j in range(PAIRS):
                    ia, c = i + 2 * j, cv[:, j % 2, :, :]
                    p = psum(ia)
                    if j >= 2:
                        act.wait_ge(y_ready, n * PAIRS + j - 1)
                    for t in range(2):
                        ins = act.activation(c[:, t, :], p[:, t * S:(t + 1) * S], ACT.Identity,
                                             bias=vec(f"convb.{n}", 2 * j + t), scale=vec(f"conv{centre}.{n}", 2 * j + t))
                    me.give(ins, conv_mid)
                    split(ia + 2)
                    act.wait_ge(read_out, PLAN[ia].out)
                    me.give(act.activation(c, c, func), act_ready)
                    split(ia + 3)
                    me.take(prod_ready)
                    me.give(act.activation(yh[:, 2 * j:2 * j + 2, :], c, ACT.Copy), y_hi)
                split_all(first("down", n), 12)

            def pv_half(u):
                s, q = divmod(u, ST)
                me.take(pv_ready)
                me.give(act.activation(ao_h[:, s, q * P:(q + 1) * P], G[:, 3 * BANK:3 * BANK + P], ACT.Copy), pv_hi)

            def mixer(layer):
                norm()
                i = first("v", layer)
                split_all(i, 18)
                for j in range(12):
                    ib = i + 18 + j
                    if j >= 4:
                        g = gate_p if j < 8 else gate_a
                        c = 2 * ((j - 4) % 4)
                        me.give(act.activation(g[:, c:c + 2, :].rearrange("p c s -> p (c s)"), psum(ib), ACT.Exp,
                                               scale=-1.0), gate_exp)
                    split(ib + 2)
                    if j < 8:
                        me.take(lg_ready)
                        me.give(act.activation(lg[:, :], lg[:, :], ACT.Exp, bias=nm[:, 0:1], accum_out=sums[:, 0:1]),
                                exp_ready)
                    if 2 <= j < 10:
                        pv_half(j - 2)
                    if 1 <= j < 9:
                        me.take(tr_ready)
                        ptf = pt.rearrange("p k n -> p (k n)")
                        act.activation(ptf[:, 0:BANK], A[:, 2 * BANK:3 * BANK], ACT.Copy)
                        me.give(act.activation(ptf[:, BANK:6 * P], A[:, 3 * BANK:3 * BANK + 2 * P], ACT.Copy), pt_ready)
                me.take(pooled, 4)
                hi(x_hi[:, :, :], tmp[:, :, :])
                ip = first("pool", layer)
                p = psum(ip)
                for k in range(DC):
                    ins = act.activation(ph[:, k, :], p[:, k * S:(k + 1) * S], ACT.Copy,
                                         scale=vec(f"pool_scale.{layer}", k))
                    if k % 4 == 3:
                        me.give(ins, x_hi_ready)
                split(ip + 2)
                split_all(ip + 1, 4)
                for j in range(2):
                    split(first("wb", layer) + j + 2)
                    hi(x_hi[:, 4 * j:4 * j + 4, :], tmp[:, 4 * j:4 * j + 4, :])
                split_all(first("wo", layer), 4)
                after("wo", layer)
                ffn(layer)
                after("down", layer)

            split(0)
            act.wait_ge(x_in, 16)
            split(1)
            act.wait_ge(s5_in, 48)
            dt, mag, theta = ang[3], ang[4], ang[5]
            me.give(act.activation(dt[:, 0:NS5], ang[2][:, 0:NS5], ACT.Exp), dt_ready)
            me.take(ndt_ready)
            me.give(act.activation(mag[:, 0:NS5], mag[:, 0:NS5], ACT.Exp), mag_ready)
            act.wait_ge(par_in, 16)
            me.take(lbd_ready)
            me.give(act.activation(lbt[:, 0:8], lbt[:, 0:8], ACT.Exp), lbe_ready)
            me.take(red_ready)
            act.activation(ang[7][:, :], ang[7][:, :], ACT.Sin)
            me.give(act.activation(ang[8][:, :], ang[8][:, :], ACT.Sin), trig_ready)
            for g in range(GROUPS):
                me.take(tab_ready)
                if g == 2:
                    act.wait_ge(tab_out[0], 16)
                me.give(act.activation(tab[:, g % 2, :, :].rearrange("p h n -> p (h n)"), A[:, :], ACT.Copy), tab_copied)
            act.wait_ge(ones_ready, 1)
            for layer in range(2):
                mixer(layer)
            norm(False)
            me.take(hf_ready)
            norm()
            i = first("ef")
            for j in range(2):
                me.give(act.activation(fe[:, j * BANK:(j + 1) * BANK], psum(i + j), ACT.Exp, scale=-1.0), gate_exp)
                split(i + j + 2)
            split(i + 4)
            me.take(f_ready)
            me.give(act.activation(fe[:, :], fe[:, :], ACT.Ln), ln_ready)
            split(i + 5)
            me.take(cum_ready)
            act.activation(eb[:, :], cum[:, :], ACT.Exp)
            act.activation(enb[:, :], cum[:, :], ACT.Exp, scale=-1.0)
            me.give(act.activation(dd[:, :], dd[:, :], ACT.Exp), eb_ready)
            split_all(i + 4, 2)
            for j in range(2):
                me.give(act.activation(sgate[:, j * BANK:(j + 1) * BANK], psum(i + 6 + j), ACT.Exp, scale=-1.0), gate_exp)
                split(i + 8 + j)
            split_all(i + 8, 2)
            me.take(ket_psum)
            me.give(act.activation(ket.rearrange("p k n -> p (k n)"), A[:, BANK:3 * BANK], ACT.Copy), ket_ready)
            me.take(o_ready)
            me.give(act.activation(tmp[:, 0:4, :].rearrange("p c s -> p (c s)"), A[:, BANK:3 * BANK], ACT.Square),
                    sq_ready)
            root([(fe[:, 0:BANK], 0, BANK, DH), (fe[:, BANK:2 * BANK], 3 * BANK, BANK, DH)])
            hi(x_hi[:, 0:4, :], tmp[:, 0:4, :])
            for g in range(4):
                me.take(yd_ready)
                me.give(act.activation(tmp[:, 4 + g, :], tmp[:, 4 + g, :], ACT.Gelu_apprx_tanh), zg_ready)
            me.settle()
            me.give(act.activation(x_hi[:, 4:8, :], tmp[:, 4:8, :], ACT.Copy), x_hi_ready)
            ig = first("glu")
            p = psum(ig)
            for k in range(4):
                ins = act.activation(t_s5[0][:, k * S:(k + 1) * S], p[:, k * S:(k + 1) * S], ACT.Exp, bias=nbglu[:, k:k + 1],
                                     scale=-1.0)
            me.give(ins, gate_exp)
            split(ig + 2)
            hi(x_hi[:, 4:8, :], tmp[:, 4:8, :])
            split_all(first("eo"), 4)
            after("eo", 0)
            ffn(2)
            after("down", 2)
            norm()
            split_all(first("mp"), 3)
            act.wait_ge(read_out, PLAN[first("mp") + 2].out)
            me.give(act.activation(tmp[:, 0:5, :], c6[:, 0:5, :], ACT.Square), sq_ready)
            root([(rms[:, 0:S], 0, S, 384), (rms[:, S:2 * S], S, S, 256)])
            hi(x_hi[:, 0:5, :], tmp[:, 0:5, :])
            split_all(first("uq"), 6)
            for j in range(MH + 2):
                if j < MH:
                    me.take(lg_ready)
                    l = lm[:, j % 2, :, :].rearrange("p k n -> p (k n)")
                    act.activation(l[:, 0:P], l[:, 0:P], ACT.Exp, bias=nm[:, 0:1], accum_out=sums[:, 0:1])
                    me.give(act.activation(l[:, P:3 * P], l[:, P:3 * P], ACT.Exp, bias=nm[:, 1:2],
                                           accum_out=sums[:, 1:2]), exp_ready)
                if j >= 2:
                    me.take(pv_ready)
                    me.give(act.activation(x_hi[:, j - 2, :], A[:, 3 * BANK:3 * BANK + S], ACT.Copy), pv_hi)
                if 1 <= j <= MH:
                    me.take(tr_ready)
                    me.give(act.activation(pm[:, :], A[:, 2 * BANK:2 * BANK + 3 * P], ACT.Copy), pt_ready)
            split_all(first("mo"), 4)
            after("mo", 0)
            ffn(3)
            after("down", 3)
            norm(False)

        @block.vector
        def _(v):
            me = Side(v, dve_own)

            def split(i):
                if i >= N:
                    return
                n = PLAN[i].used
                me.taken[w_hi_ready.name] = i
                me.take(w_hi_ready)
                me.give(v.tensor_tensor(w_lo[i % SPL][:, 0:n], raw[i % RAW][:, 0:n],
                                        w_hi[i % SPL][:, 0:n].bitcast(F32), ALU.subtract), w_lo_ready)

            def lo(dst, src, hi_, signal=x_ready):
                me.take(x_hi_ready)
                me.give(v.tensor_tensor(dst, src, hi_.bitcast(F32), ALU.subtract), signal)

            def psum(i):
                b = PLAN[i]
                v.wait_ge(mm_done, i + 1)
                return G[:, b.bank * BANK:(b.bank + b.banks) * BANK]

            def norm(name, dst=tmp, split_it=True, signal=None):
                me.take(rms_ready)
                me.give(v.reciprocal(rms[:, 0:S], rms[:, 0:S]))
                me.settle()
                for c in range(DC):
                    ins = v.scalar_tensor_tensor(out=dst[:, c, :], in0=h[:, c, :], scalar=vec(name, c),
                                                 in1=rms[:, 0:S], op0=ALU.mult, op1=ALU.mult)
                    if split_it and c % 4 == 3:
                        me.give(ins, x_f32)
                if not split_it:
                    me.give(ins, signal)
                    return
                for k in (0, 4):
                    lo(x_lo[:, k:k + 4, :], tmp[:, k:k + 4, :], x_hi[:, k:k + 4, :])

            def add_h(i, j):
                hh = h[:, 2 * j:2 * j + 2, :].rearrange("p c s -> p (c s)")
                me.give(v.tensor_tensor(hh, hh, psum(i), ALU.add), read_out)

            def ffn(n):
                norm(FFN_NORM[n])
                i = first("up_a", n)
                centre = 1 if n < 2 else 2
                for j in range(PAIRS):
                    ia, c = i + 2 * j, cv[:, j % 2, :, :]
                    p = psum(ia)
                    me.take(conv_mid)
                    taps = [k for k in range(3) if k != centre]
                    for k in taps:
                        sh = k - centre
                        o0, o1 = max(0, -sh), S - max(0, sh)
                        for t in range(2):
                            ins = v.scalar_tensor_tensor(out=c[:, t, o0:o1], in0=p[:, t * S + o0 + sh:t * S + o1 + sh],
                                                         scalar=vec(f"conv{k}.{n}", 2 * j + t), in1=c[:, t, o0:o1],
                                                         op0=ALU.mult, op1=ALU.add)
                        if k == taps[0]:
                            me.give(ins)
                            me.settle()
                    me.give(ins, read_out)
                    split(ia + 2)
                    p = psum(ia + 1)
                    me.take(act_ready)
                    cf = c.rearrange("p c s -> p (c s)")
                    me.give(v.tensor_tensor(cf, cf, p, ALU.mult), read_out)
                    me.give(v.tensor_copy(small[:, 40:41], small[:, 0:1]), prod_ready)
                    split(ia + 3)
                    me.take(y_hi)
                    me.give(v.tensor_tensor(yl[:, 2 * j:2 * j + 2, :], c, yh[:, 2 * j:2 * j + 2, :].bitcast(F32),
                                            ALU.subtract), y_ready)
                i = first("down", n)
                for j in range(12):
                    if j % 3 == 2:
                        add_h(i + j, j // 3)
                    split(i + j + 2)

            def soft_a(u):
                s, q = divmod(u, ST)
                if u:
                    me.take(tr_ready)
                me.take(scores_ready)
                v.tensor_tensor(lg[:, 0:BANK], A[:, 0:BANK], bm[:, q, s, 0:BANK], ALU.add)
                me.give(v.tensor_tensor(lg[:, BANK:3 * S], A[:, BANK:BANK + S], bm[:, q, s, BANK:3 * S], ALU.add),
                        scores_read)
                me.settle()
                me.give(v.tensor_reduce(mx[:, 0:1], lg[:, :], AX.X, ALU.max))
                me.settle()
                me.give(v.tensor_scalar(nm[:, 0:1], mx[:, 0:1], -1.0, None, ALU.mult), lg_ready)

            def soft_b():
                me.take(exp_ready)
                me.give(v.reciprocal(rs[:, 0:1], sums[:, 0:1]))
                me.settle()
                me.give(v.tensor_scalar(lg[:, :], lg[:, :], rs[:, 0:1], None, ALU.mult), prob_ready)

            def sigmoid(g):
                me.take(gate_exp)
                me.give(v.tensor_scalar(g, g, 1.0, None, ALU.add), read_out)
                me.settle()
                me.give(v.reciprocal(g, g))

            def mixer(layer):
                norm(f"norm1.{layer}")
                i = first("v", layer)
                for j in range(18):
                    p = psum(i + j)
                    k = 2 * (j % 6)
                    if layer == 0 and j == 6:
                        v.wait_ge(bb_ready, 1)
                    if j < 6:
                        ins = v.tensor_copy(va[:, :, j * S:(j + 1) * S], p.rearrange("p (t n) -> p t n", t=ST))
                    elif j < 12:
                        ins = v.tensor_scalar(qt[:, k:k + 2, :].rearrange("p c s -> p (c s)"), p, DH ** -0.5, None,
                                              ALU.mult)
                    else:
                        ins = v.tensor_copy(kt[:, k:k + 2, :].rearrange("p c s -> p (c s)"), p)
                    me.give(ins, read_out)
                    split(i + j + 2)
                me.settle()
                me.give(v.tensor_copy(small[:, 41:42], small[:, 0:1]), qkv_ready)
                me.take(u_zero)
                v.wait_ge(bm_in, 16 * ST * SLOTS)
                for j in range(12):
                    ib = i + 18 + j
                    if j < 4:
                        p = psum(ib)
                        me.give(v.tensor_copy(ub[:, 2 * j:2 * j + 2, PADT:PADT + S],
                                              p.rearrange("p (c s) -> p c s", c=2)), read_out)
                    else:
                        g = gate_p if j < 8 else gate_a
                        c = 2 * ((j - 4) % 4)
                        sigmoid(g[:, c:c + 2, :])
                    split(ib + 2)
                    if j < 8:
                        soft_a(j)
                    if 2 <= j < 10:
                        s, q = divmod(j - 2, ST)
                        me.take(pv_hi)
                        me.give(v.tensor_tensor(ao_l[:, s, q * P:(q + 1) * P], G[:, 3 * BANK:3 * BANK + P],
                                                ao_h[:, s, q * P:(q + 1) * P].bitcast(F32), ALU.subtract), pv_read)
                    if j < 8:
                        soft_b()
                me.take(tr_ready)
                me.take(pooled, 4)
                v.wait_ge(mm_done, i + 30)
                me.give(v.tensor_copy(small[:, 42:43], small[:, 0:1]), x_f32)
                lo(x_lo[:, :, :], tmp[:, :, :], x_hi[:, :, :])
                ip = first("pool", layer)
                p = psum(ip)
                for k in range(DC):
                    if k % 4 == 0:
                        me.take(x_hi_ready)
                    ins = v.scalar_tensor_tensor(out=pl[:, k, :], in0=p[:, k * S:(k + 1) * S],
                                                 scalar=vec(f"pool_scale.{layer}", k), in1=ph[:, k, :].bitcast(F32),
                                                 op0=ALU.mult, op1=ALU.subtract)
                    if k % 4 == 3:
                        me.give(ins, x_ready)
                me.settle()
                me.give(v.tensor_copy(small[:, 43:44], small[:, 0:1]), read_out)
                split(ip + 2)
                for j in range(4):
                    p = psum(ip + 1 + j)
                    g = gate_p[:, 2 * j:2 * j + 2, :].rearrange("p c s -> p (c s)")
                    me.give(v.tensor_tensor(g, g, p, ALU.mult), read_out)
                    split(ip + j + 3)
                ib = first("wb", layer)
                for j in range(2):
                    p = psum(ib + j)
                    g = gate_a[:, 4 * j:4 * j + 4, :].rearrange("p c s -> p (c s)")
                    me.give(v.tensor_tensor(g, g, p, ALU.mult), read_out)
                    me.settle()
                    me.give(v.tensor_tensor(tmp[:, 4 * j:4 * j + 4, :], gate_a[:, 4 * j:4 * j + 4, :],
                                            gate_p[:, 4 * j:4 * j + 4, :], ALU.add), x_f32)
                    split(ib + j + 2)
                    lo(x_lo[:, 4 * j:4 * j + 4, :], tmp[:, 4 * j:4 * j + 4, :], x_hi[:, 4 * j:4 * j + 4, :])
                io = first("wo", layer)
                for j in range(4):
                    add_h(io + j, j)
                    split(io + j + 2)
                me.settle()
                ffn(layer)
                me.settle()

            me.give(v.memset(relb[BUCKETS:BUCKETS + 1, :], 1.0))
            v.wait_ge(relb_in, 16)
            me.settle()
            me.give(v.tensor_copy(relw[:, :, :], relb[:, :].rearrange("p (h o) -> p h o", o=1)
                                  .to_broadcast([BUCKETS + 1, HEADS, P])), relb_ready)
            v.memset(ones[:, :], 1.0)
            v.memset(small[:, 0:1], EPS)
            me.give(v.memset(small[:, 1:4], 0.0), ones_ready)
            v.wait_ge(par_in, 16)
            me.settle()
            l0, l1 = par[:, COL["lb0"]:COL["lb0"] + 4], par[:, COL["lb1"]:COL["lb1"] + 4]
            me.give(v.tensor_tensor(lbt[:, 8:12], l0, l1, ALU.max))
            me.settle()
            v.tensor_tensor(lbt[:, 0:4], l0, lbt[:, 8:12], ALU.subtract)
            v.tensor_scalar(nbglu, par[:, COL["b_glu"]:COL["b_glu"] + 4], -1.0, None, ALU.mult)
            me.give(v.tensor_tensor(lbt[:, 4:8], l1, lbt[:, 8:12], ALU.subtract), lbd_ready)
            split(0)
            split(1)
            v.wait_ge(pos_in, 16)
            v.wait_ge(cst_in, 16)
            theta, red = ang[5], ang[6]
            me.give(v.tensor_copy(theta[:, NS5:NANG], pos_i[:, :]))
            me.settle()
            me.give(v.tensor_scalar(theta[:, NS5:NANG], theta[:, NS5:NANG], freq, None, ALU.mult))
            me.settle()
            me.take(th_ready)
            k = ang[9]
            me.give(v.tensor_scalar(k[:, :], theta[:, :], 1.0 / TWO_PI, MAGIC, ALU.mult, ALU.add))
            me.settle()
            me.give(v.tensor_scalar(k[:, :], k[:, :], MAGIC, None, ALU.subtract))
            me.settle()
            src = theta
            for c in (C1, C2, C3):
                me.give(v.scalar_tensor_tensor(out=red[:, :], in0=k[:, :], scalar=-c, in1=src[:, :], op0=ALU.mult,
                                               op1=ALU.add))
                me.settle()
                src = red
            lim = 3.1415925
            me.give(v.tensor_scalar(ang[7][:, :], red[:, :], lim, -lim, ALU.min, ALU.max))
            me.settle()
            me.give(v.scalar_tensor_tensor(out=ang[8][:, :], in0=ang[7][:, :], scalar=-1.0, in1=ang[7][:, :],
                                           op0=ALU.mult, op1=ALU.max))
            me.settle()
            me.give(v.tensor_scalar(ang[8][:, :], ang[8][:, :], -1.0, float(np.pi / 2), ALU.mult, ALU.add), red_ready)
            me.take(trig_ready)
            v.tensor_copy(sin_r[:, 0, :], ang[7][:, NS5:NANG])
            me.give(v.tensor_copy(cos_r[:, 0, :], ang[8][:, NS5:NANG]), rope_kept)
            me.take(lbe_ready)
            me.give(v.tensor_tensor(lbt[:, 8:12], lbt[:, 0:4], lbt[:, 4:8], ALU.add))
            me.settle()
            me.give(v.reciprocal(lbt[:, 8:12], lbt[:, 8:12]))
            me.settle()
            v.tensor_tensor(lb, lbt[:, 0:4], lbt[:, 8:12], ALU.mult)
            me.give(v.tensor_tensor(omlb, lbt[:, 4:8], lbt[:, 8:12], ALU.mult))
            me.take(den_ready)
            me.give(v.reciprocal(s5x[0][:, :], s5x[0][:, :]), rden_ready)
            v.wait_ge(x_in, 16)
            for layer in range(2):
                mixer(layer)
            norm("norm_f", dst=h, split_it=False, signal=hf_ready)
            me.settle()
            norm("mix.0")
            i = first("ef")
            for j in range(2):
                f = fe[:, j * BANK:(j + 1) * BANK]
                sigmoid(f)
                me.settle()
                for c in range(2):
                    fc = fe[:, j * BANK + c * S:j * BANK + (c + 1) * S]
                    ins = v.tensor_scalar(fc, fc, omlb[:, 2 * j + c:2 * j + c + 1], lb[:, 2 * j + c:2 * j + c + 1],
                                          ALU.mult, ALU.add)
                me.give(ins)
                me.settle()
                me.give(v.tensor_scalar(key[:, j * BANK:(j + 1) * BANK], f, -1.0, 1.0, ALU.mult, ALU.add),
                        f_ready if j else None)
                split(i + j + 2)
            me.give(v.tensor_copy(qb[:, 0:BANK], psum(i + 2)), read_out)
            split(i + 4)
            me.take(ln_ready)
            me.take(smask_ready)
            me.give(v.tensor_tensor_scan(cum[:, :], smask[:, :], fe[:, :], 0.0, ALU.mult, ALU.add))
            me.settle()
            c16 = cum.rearrange("p (c s) -> p c s", s=CH)
            last = c16[:, :, CH - 1:CH].to_broadcast([P, 16, CH])
            me.give(v.tensor_tensor(dd.rearrange("p (c s) -> p c s", s=CH), last, c16, ALU.subtract), cum_ready)
            me.give(v.tensor_copy(qb[:, BANK:2 * BANK], psum(i + 3)), read_out)
            split(i + 5)
            me.settle()
            me.take(eb_ready)
            v.tensor_tensor(qb[:, :], qb[:, :], eb[:, :], ALU.mult)
            v.tensor_tensor(enb[:, :], enb[:, :], key[:, :], ALU.mult)
            me.give(v.tensor_tensor(dd[:, :], dd[:, :], key[:, :], ALU.mult), qd_ready)
            v24 = v2.rearrange("p (t n) -> p t n", t=ST)
            for j in range(2):
                me.give(v.tensor_copy(v24[:, :, j * S:(j + 1) * S], psum(i + 4 + j).rearrange("p (t n) -> p t n", t=ST)),
                        read_out)
                split(i + 6 + j)
            for j in range(2):
                g = sgate[:, j * BANK:(j + 1) * BANK]
                me.take(gate_exp)
                me.give(v.tensor_scalar(g, g, 1.0, None, ALU.add))
                me.settle()
                me.give(v.reciprocal(g, g))
                me.settle()
                me.give(v.tensor_tensor(g, g, psum(i + 6 + j), ALU.mult), read_out)
                split(i + 8 + j)
            for j in range(2):
                me.give(v.tensor_copy(uu[:, j * BANK:(j + 1) * BANK], psum(i + 8 + j)), read_out)
                split(i + 10 + j)
            me.take(att_ready)
            me.take(am_zero)
            att = A[:, 0:BANK].rearrange("p (k n) -> p k n", n=CH)
            for r in (0, CH):
                ins = v.copy_predicated(am[r:r + CH, :, r:r + CH],
                                        ccausal[r:r + CH, :].rearrange("p (o n) -> p o n", o=1).to_broadcast([CH, 8, CH]),
                                        att[r:r + CH, :, :])
            me.give(ins, am_ready)
            for n in range(3):
                me.take(ds_ready)
                if n == 0:
                    me.give(v.tensor_copy(st[:, 0, :, :].rearrange("p c n -> p (c n)"), A[:, 3 * BANK:4 * BANK]), st_ready)
                else:
                    me.settle()
                    for c in range(4):
                        e = c * S + n * CH + CH - 1
                        ins = v.scalar_tensor_tensor(out=st[:, n, c, :], in0=st[:, n - 1, c, :], scalar=eb[:, e:e + 1],
                                                     in1=A[:, 3 * BANK + c * P:3 * BANK + (c + 1) * P],
                                                     op0=ALU.mult, op1=ALU.add)
                    me.give(ins, st_ready)
            me.take(rms_ready)
            me.give(v.reciprocal(fe[:, :], fe[:, :]))
            me.settle()
            for c in range(4):
                cs = slice(c * S, (c + 1) * S)
                ins = v.scalar_tensor_tensor(out=key[:, cs], in0=A[:, BANK + c * S:BANK + (c + 1) * S],
                                             scalar=vec("hgrn_g", c), in1=fe[:, cs], op0=ALU.mult, op1=ALU.mult)
            me.give(ins)
            me.settle()
            me.give(v.tensor_tensor(tmp[:, 0:4, :].rearrange("p c s -> p (c s)"), key[:, :], sgate[:, :], ALU.mult),
                    x_f32)
            lo(x_lo[:, 0:4, :], tmp[:, 0:4, :], x_hi[:, 0:4, :])
            me.settle()
            me.give(v.tensor_copy(small[:, 44:45], small[:, 0:1]), s5_free)
            me.take(e_ready)
            t1, t2, t3, t4, zr, zi = t_s5[0:6]

            def s5_states(g):
                gs = slice(4 * g, 4 * g + 4)
                ecg, esg = ec[:, gs, :], es[:, gs, :]
                bu = A[:, :].rearrange("p (k n) -> p k n", k=4)
                re, im = bu[:, :, 0:S], bu[:, :, S:2 * S]
                u1, u2, u3, u4 = (t.rearrange("p (k n) -> p k n", k=4) for t in (t1, t2, t3, t4))
                me.take(bu_ready)
                v.tensor_tensor(u1, ecg, re, ALU.mult)
                v.tensor_tensor(u2, esg, im, ALU.mult)
                v.tensor_tensor(u3, ecg, im, ALU.mult)
                me.give(v.tensor_tensor(u4, esg, re, ALU.mult), bu_read)
                me.settle()
                v.tensor_tensor(t1[:, :], t1[:, :], t2[:, :], ALU.add)
                me.give(v.tensor_tensor(t3[:, :], t3[:, :], t4[:, :], ALU.subtract))
                me.settle()
                if g:
                    me.take(z_read)
                for k in range(4):
                    m = s5_st[:, 0, 4 * g + k:4 * g + k + 1].to_broadcast([P, S])
                    ks = slice(k * S, (k + 1) * S)
                    v.tensor_tensor_scan(zr[:, ks], m, t1[:, ks], 0.0, ALU.mult, ALU.add)
                    ins = v.tensor_tensor_scan(zi[:, ks], m, t3[:, ks], 0.0, ALU.mult, ALU.add)
                me.give(ins, z_ready)
                me.settle()

            def s5_y(g):
                me.take(ys_ready)
                me.give(v.scalar_tensor_tensor(out=tmp[:, 4 + g, :], in0=uu[:, g * S:(g + 1) * S], scalar=vec("s5_d", g),
                                               in1=G[:, g * BANK:g * BANK + S], op0=ALU.mult, op1=ALU.add), yd_ready)

            for g in range(4):
                s5_states(g)
                if g:
                    s5_y(g - 1)
            s5_y(3)
            me.take(zg_ready, 4)
            lo(x_lo[:, 4:8, :], tmp[:, 4:8, :], x_hi[:, 4:8, :])
            ig = first("glu")
            sigmoid(t1[:, :])
            me.settle()
            z = tmp[:, 4:8, :].rearrange("p c s -> p (c s)")
            me.give(v.tensor_tensor(z, z, t1[:, :], ALU.mult), x_f32)
            split(ig + 2)
            lo(x_lo[:, 4:8, :], tmp[:, 4:8, :], x_hi[:, 4:8, :])
            for j in range(4):
                add_h(first("eo") + j, j)
                split(first("eo") + j + 2)
            me.settle()
            ffn(2)
            me.settle()
            norm("mix.1")
            i = first("mp")
            for j in range(3):
                me.give(v.tensor_copy(c6[:, 2 * j:2 * j + 2, :].rearrange("p c s -> p (c s)"), psum(i + j)), read_out)
                split(i + j + 2)
            me.settle()
            me.take(rms_ready)
            me.give(v.reciprocal(rms[:, :], rms[:, :]))
            me.settle()
            for c in range(5):
                g, r = (vec("q_g", c), rms[:, 0:S]) if c < 3 else (vec("kv_g", c - 3), rms[:, S:2 * S])
                ins = v.scalar_tensor_tensor(out=tmp[:, c, :], in0=c6[:, c, :], scalar=g, in1=r, op0=ALU.mult,
                                             op1=ALU.mult)
            me.give(ins, x_f32)
            lo(x_lo[:, 0:5, :], tmp[:, 0:5, :], x_hi[:, 0:5, :])
            i = first("uq")
            for j in range(4):
                p = psum(i + j)
                v.tensor_copy(qn[:, 2 * j:2 * j + 2, :].rearrange("p c s -> p (c s)"), p[:, 0:2 * S])
                me.give(v.tensor_copy(rx[:, j, :], p[:, 2 * S:3 * S]), read_out)
                split(i + j + 2)
            i = first("ukv")
            for j in range(2):
                p = psum(i + j)
                v.tensor_copy(kn[:, 4 * j:4 * j + 4, :].rearrange("p c s -> p (c s)"), p[:, 0:2 * BANK])
                me.give(v.tensor_copy(v3[:, :, j * 512:(j + 1) * 512],
                                      p[:, 2 * BANK:4 * BANK].rearrange("p (t n) -> p t n", t=ST)), read_out)
                split(i + j + 2)
            me.settle()
            me.give(v.tensor_copy(small[:, 45:46], small[:, 0:1]), rx_ready)
            cb = cos_r[:, :, :].to_broadcast([P, 4, S])
            sb_ = sin_r[:, :, :].to_broadcast([P, 4, S])
            v.tensor_tensor(tmp[:, 0:4, :], rx[:, :, :], cb, ALU.mult)
            v.tensor_tensor(tmp[:, 4, :], c6[:, 5, :], cos_r[:, 0, :], ALU.mult)
            me.take(rot_ready)
            v.tensor_tensor(qr[:, :, :], sb_, A[:, 0:2 * BANK].rearrange("p (c s) -> p c s", c=4), ALU.mult)
            me.give(v.tensor_tensor(kr[:, 0, :], sin_r[:, 0, :], A[:, 2 * BANK:2 * BANK + S], ALU.mult))
            me.settle()
            v.tensor_tensor(qr[:, :, :], qr[:, :, :], tmp[:, 0:4, :], ALU.add)
            me.give(v.tensor_tensor(kr[:, 0, :], kr[:, 0, :], tmp[:, 4, :], ALU.add), rope_ready)
            scale = 192 ** -0.5
            cz = causal.rearrange("p (o n) -> p o n", o=1).to_broadcast([P, 2, P])
            for j in range(MH + 2):
                if j < MH:
                    if j >= 2:
                        me.take(tr_ready)
                    me.take(scores_ready)
                    l = lm[:, j % 2, :, :]
                    ps = A[:, (j % 2) * BANK:(j % 2) * BANK + 3 * P].rearrange("p (k n) -> p k n", k=3)
                    v.tensor_scalar(l[:, 1, :], ps[:, 1, :], scale, None, ALU.mult)
                    me.give(v.scalar_tensor_tensor(out=l[:, 0:3:2, :], in0=ps[:, 0:3:2, :], scalar=scale, in1=cz,
                                                   op0=ALU.mult, op1=ALU.add), scores_read)
                    me.settle()
                    lf = l.rearrange("p k n -> p (k n)")
                    v.tensor_reduce(mx[:, 0:1], lf[:, 0:P], AX.X, ALU.max)
                    me.give(v.tensor_reduce(mx[:, 1:2], lf[:, P:3 * P], AX.X, ALU.max))
                    me.settle()
                    me.give(v.tensor_scalar(nm[:, :], mx[:, :], -1.0, None, ALU.mult), lg_ready)
                if j >= 2:
                    me.take(pv_hi)
                    me.give(v.tensor_tensor(x_lo[:, j - 2, :], A[:, 3 * BANK:3 * BANK + S],
                                            x_hi[:, j - 2, :].bitcast(F32), ALU.subtract), pv_read)
                if j < MH:
                    me.take(exp_ready)
                    me.give(v.reciprocal(rs[:, :], sums[:, :]))
                    me.settle()
                    v.tensor_scalar(lf[:, 0:P], lf[:, 0:P], rs[:, 0:1], None, ALU.mult)
                    me.give(v.tensor_scalar(lf[:, P:3 * P], lf[:, P:3 * P], rs[:, 1:2], None, ALU.mult), prob_ready)
            for j in range(4):
                add_h(first("mo") + j, j)
                split(first("mo") + j + 2)
            me.settle()
            ffn(3)
            me.settle()
            norm("final", split_it=False, signal=final_ready)

        @block.gpsimd
        def _(g):
            me = Side(g, pool_own)

            def tt(out, x, y, op, s=None):
                me.give(g.tensor_tensor(out, x, y, op), s)
                me.settle()

            W = slice(0, NS5)
            ar, ai, dt, mag, theta = (ang[j][:, W] for j in (0, 1, 3, 4, 5))
            g.wait_ge(s5_in, 48)
            me.take(dt_ready)
            tt(mag, ar, dt, ALU.mult, ndt_ready)
            tt(theta, ai, dt, ALU.mult, th_ready)
            den, xr, cr, ci, u1, u2 = (s5x[j][:, :] for j in range(6))
            tt(den, ar, ar, ALU.mult)
            tt(u1, ai, ai, ALU.mult)
            tt(den, den, u1, ALU.add, den_ready)
            me.take(trig_ready)
            g.wait_ge(mag_ready, 1)
            sin, cos = ang[7][:, W], ang[8][:, W]
            xi = u2
            for k, x in enumerate((ang[4], ang[8], ang[7])):
                me.give(g.tensor_copy(s5_st[:, k, :], x[:, 4 * P:NS5]))
            tt(xr, mag, cos, ALU.mult)
            tt(xi, mag, sin, ALU.mult)
            me.give(g.tensor_scalar(xr, xr, -1.0, None, ALU.add))
            me.settle()
            tt(cr, xr, ar, ALU.mult)
            tt(u1, xi, ai, ALU.mult)
            tt(cr, cr, u1, ALU.add)
            tt(ci, xi, ar, ALU.mult)
            tt(u1, xr, ai, ALU.mult)
            tt(ci, ci, u1, ALU.subtract)
            me.take(rden_ready)
            tt(cr, cr, den, ALU.mult)
            tt(ci, ci, den, ALU.mult)
            g.wait_ge(s5b_in, 16)
            cr, ci, u1 = cr[:, 0:4 * P], ci[:, 0:4 * P], u1[:, 0:4 * P]
            br, bi = s5b[:, 0, :], s5b[:, 1, :]
            bbr, bbi = (bb[:, j, :, :].rearrange("p c n -> p (c n)") for j in range(2))
            tt(bbr, cr, br, ALU.mult)
            tt(u1, ci, bi, ALU.mult)
            tt(bbr, bbr, u1, ALU.subtract)
            tt(bbi, cr, bi, ALU.mult)
            tt(u1, ci, br, ALU.mult)
            g.wait_ge(rope_kept, 1)
            tt(bbi, bbi, u1, ALU.add, bb_ready)

            for layer in range(2):
                if layer:
                    g.wait_ge(read_out, PLAN[first("down", 0) + 11].out)
                me.give(g.memset(ub[:, :, :], 0.0), u_zero)
                for j in range(4):
                    g.wait_ge(read_out, PLAN[first("u", layer) + j].out)
                    src, length = ub[:, 2 * j:2 * j + 2, :], S + 2 * PADT
                    for k in range(j + 1):
                        step = 1 << k
                        length -= step
                        dst = pool_w[k % 2]
                        me.give(g.tensor_tensor(dst[:, :, 0:length], src[:, :, 0:length], src[:, :, step:step + length],
                                                ALU.add))
                        me.settle()
                        src = dst
                    o = PADT - (1 << j)
                    if j == 0:
                        g.wait_ge(mm_done, first("v", layer) + 1)
                    for c in range(2):
                        me.give(g.tensor_tensor(tmp[:, 2 * j + c, :], src[:, c, o:o + S], inv_count(j), ALU.mult))
                    me.settle()
                    me.give(g.tensor_tensor(tmp[:, 2 * j:2 * j + 2, :], tmp[:, 2 * j:2 * j + 2, :],
                                            ub[:, 2 * j:2 * j + 2, PADT:PADT + S], ALU.subtract), pooled)
            g.wait_ge(read_out, PLAN[first("wo", 1) + 3].out)
            g.memset(ec[:, :, 0:1], 1.0)
            g.memset(es[:, :, 0:1], 0.0)
            g.tensor_copy(ec[:, :, 1:2], s5_st[:, 1, :].rearrange("p (c o) -> p c o", o=1))
            me.give(g.tensor_copy(es[:, :, 1:2], s5_st[:, 2, :].rearrange("p (c o) -> p c o", o=1)))
            me.settle()
            w = 1
            while w < S:
                n = min(w, S - 1 - w)
                if n:
                    dc, ds = ec[:, :, w + 1:w + 1 + n], es[:, :, w + 1:w + 1 + n]
                    sc, ss = ec[:, :, 1:1 + n], es[:, :, 1:1 + n]
                    ew = ec[:, :, w:w + 1].to_broadcast([P, SC, n])
                    fw = es[:, :, w:w + 1].to_broadcast([P, SC, n])
                    sx = etmp[:, :, 0:n]
                    tt(dc, sc, ew, ALU.mult)
                    tt(sx, ss, fw, ALU.mult)
                    tt(dc, dc, sx, ALU.subtract)
                    tt(ds, ss, ew, ALU.mult)
                    tt(sx, sc, fw, ALU.mult)
                    tt(ds, ds, sx, ALU.add, e_ready if w + n >= S - 1 else None)
                w *= 2
            g.wait_ge(read_out, PLAN[first("down", 1) + 11].out)
            me.give(g.memset(smask[:, :], 1.0))
            me.settle()
            me.give(g.memset(smask.rearrange("p (c s) -> p c s", s=CH)[:, :, 0:1], 0.0), smask_ready)
            me.give(g.memset(am[:, :, :], 0.0), am_zero)
            g.wait_ge(cc_in, 16)
            me.give(g.tensor_scalar(cc[:, 1, :, :], cc[:, 1, :, :], -1.0, None, ALU.mult), cc_ready)
            zr, zi, u1, u2, u3, u4 = (t_s5[j] for j in (4, 5, 6, 7, 8, 9))
            for k in range(4):
                gs = slice(4 * k, 4 * k + 4)
                ecg = ec[:, gs, :].rearrange("p c s -> p (c s)")
                esg = es[:, gs, :].rearrange("p c s -> p (c s)")
                me.take(z_ready)
                if k:
                    me.take(ys_ready)
                g.tensor_tensor(u1[:, :], zr[:, :], ecg, ALU.mult)
                g.tensor_tensor(u2[:, :], zi[:, :], esg, ALU.mult)
                g.tensor_tensor(u3[:, :], zr[:, :], esg, ALU.mult)
                me.give(g.tensor_tensor(u4[:, :], zi[:, :], ecg, ALU.mult), z_read)
                me.settle()
                g.tensor_tensor(u1[:, :], u1[:, :], u2[:, :], ALU.subtract)
                me.give(g.tensor_tensor(u3[:, :], u3[:, :], u4[:, :], ALU.add), s_ready)
                me.settle()


def _buckets(rel):
    n = -rel
    half = BUCKETS // 2
    ret = (n < 0).astype(np.int32) * half
    n = np.abs(n)
    exact = half // 2
    large = exact + (np.log(np.maximum(n, 1) / exact) / np.log(MAX_DISTANCE / exact) * (half - exact)).astype(np.int32)
    return (ret + np.where(n < exact, n, np.minimum(large, half - 1))).astype(np.int32)


def _constants():
    p = np.arange(P)
    rotate = np.zeros((P, P), np.float32)
    for m in range(P):
        if m % 64 < 32:
            rotate[m + 32, m] = -1.0
        else:
            rotate[m - 32, m] = 1.0
    inv = np.zeros((4, S), np.float32)
    i = np.arange(S)
    for g in range(4):
        w = 2 << g
        inv[g] = np.float32(1) / (np.clip(i - w // 2 + w, 0, S) - np.clip(i - w // 2, 0, S)).astype(np.float32)
    freq = (np.float32(10000.0) ** (-np.arange(0, 64, 2, dtype=np.float32) / np.float32(64))).astype(np.float32)
    parts = {
        "ident": np.eye(P, dtype=np.float32), "rotate": rotate,
        "causal": np.where(p[None, :] > p[:, None], NEG, 0.0).astype(np.float32),
        "inv_count": np.broadcast_to(inv.reshape(1, -1), (P, 4 * S)),
        "freq": freq[p % 32][:, None],
        "chunk_causal": ((p % CH)[:, None] <= np.arange(CH)[None, :]).astype(np.float32),
    }
    consts = np.concatenate([parts[n] for n, _ in CONSTS], axis=1).astype(np.float32)
    hot = np.zeros((BUCKETS + 1, GROUPS, TAB + 1), np.float32)
    rel = np.arange(TAB) - (S - 1)
    for g, d in enumerate(DILATIONS):
        ok = (np.abs(rel) <= HALF * d) & (rel % d == 0)
        hot[_buckets(rel)[ok], g, np.nonzero(ok)[0]] = 1.0
        hot[BUCKETS, g, np.nonzero(~ok)[0]] = NEG
        hot[BUCKETS, g, TAB] = NEG
    return np.ascontiguousarray(consts), hot.reshape(BUCKETS + 1, -1)


def _weights(a):
    out = []
    seen = {}
    w_in, e_in = a["w_in"], a["even_w_in_2"][0]
    mla = a["odd_w_in_2"][0]
    mla = np.concatenate([mla[:, :640], mla[:, 640:], mla[:, 640:]], axis=1)
    uq = a["mla_w_uq_2"][0].reshape(384, MH, 192)
    ukv = a["mla_w_ukv_2"][0].reshape(256, MH, 256)
    base = {"u": 0, "q": 1024, "k": 2560, "v": 4096, "gp": 5632, "ga": 6656}
    even = {"ef": 512, "eq": 0, "ei": 1024, "eg": 1536, "eu": 2048}
    for b in PLAN:
        j = seen.get((b.kind, b.n), 0)
        seen[(b.kind, b.n)] = j + 1
        n, cols = b.n, slice(j * b.ncol, (j + 1) * b.ncol)
        if b.kind in base:
            w = w_in[n][:, base[b.kind] + j * 256:base[b.kind] + (j + 1) * 256]
        elif b.kind == "pool":
            w = a["w_pool"][n].reshape(D, 256)
        elif b.kind == "wa":
            w = a["w_a"][n][:, cols]
        elif b.kind == "wb":
            w = a["w_b"][n][:, cols]
        elif b.kind == "wo":
            w = a["w_o"][n][:, cols]
        elif b.kind in even:
            w = e_in[:, even[b.kind] + j * 256:even[b.kind] + (j + 1) * 256]
        elif b.kind == "glu":
            w = a["s5_w_glu_2"][0]
        elif b.kind == "eo":
            w = a["even_w_out_2"][0][:, cols]
        elif b.kind == "mp":
            w = mla[:, cols]
        elif b.kind == "uq":
            two = uq[:, 2 * j:2 * j + 2]
            w = np.concatenate([two[:, 0, :128], two[:, 1, :128], two[:, 0, 128:], two[:, 1, 128:]], axis=1)
        elif b.kind == "ukv":
            four = ukv[:, 4 * j:4 * j + 4]
            w = np.concatenate([four[:, :, :128].reshape(256, 512), four[:, :, 128:].reshape(256, 512)], axis=1)
        elif b.kind == "mo":
            w = a["odd_w_out_2"][0][:, cols]
        elif b.kind in ("up_a", "up_g"):
            up = a["w_up"][n] if n < 2 else a["ffn_w_in_2"][n - 2]
            c0 = j * 256 + (FF if b.kind == "up_g" else 0)
            w = up[:, c0:c0 + 256]
        else:
            down = a["w_down"][n] if n < 2 else a["ffn_w_out_2"][n - 2]
            r0 = (j % 3) * 1024
            w = down[r0:r0 + b.kc * P, (j // 3) * 256:(j // 3 + 1) * 256]
        assert w.shape == (b.kc * P, b.ncol), (b.kind, w.shape)
        out.append(np.ascontiguousarray(w.reshape(b.kc, P, b.ncol).transpose(1, 0, 2)).reshape(-1))
    return np.concatenate(out)


def _layouts(a):
    vectors = {"norm_f": a["norm_f"], "final": a["final_norm_g_2"], "lb0": a["hgrn_lb_logits_2"][0],
               "lb1": a["hgrn_lb_logits_2"][1], "hgrn_g": a["hgrn_norm_g_2"][0], "s5_d": a["s5_d_2"][0],
               "b_glu": a["s5_b_glu_2"][0], "q_g": a["mla_q_norm_g_2"][0], "kv_g": a["mla_kv_norm_g_2"][0]}
    for i in range(2):
        vectors |= {f"norm1.{i}": a["norm1"][i], f"norm2.{i}": a["norm2"][i], f"pool_scale.{i}": a["pool_scale"][i],
                    f"mix.{i}": a["norm_mix_g_2"][i], f"ffn.{i}": a["norm_ffn_g_2"][i],
                    f"convb.{i}": a["conv_b"][i], f"convb.{i + 2}": a["ffn_conv_b_2"][i]}
        for k in range(3):
            vectors |= {f"conv{k}.{i}": a["conv_w"][i, k], f"conv{k}.{i + 2}": a["ffn_conv_w_2"][i, k]}
    params = np.concatenate([vectors[n].reshape(-1, P).T for n, _ in VECTORS], axis=1)
    row, c4, col = np.meshgrid(np.arange(P), np.arange(4), np.arange(P), indexing="ij")
    chunk = 4 * c4 + row // 32
    group, state = 2 * chunk + col // SP_, col % SP_
    srow, sc = np.meshgrid(np.arange(P), np.arange(SC), indexing="ij")
    sgroup, sstate = 2 * sc + srow // SP_, srow % SP_
    abt = []
    for x in (a["s5_a_re_2"][0], a["s5_a_im_2"][0], np.broadcast_to(a["s5_log_dt_2"][0][:, None], (SG, SP_))):
        abt.append(np.concatenate([x[group, state].reshape(P, -1), x[sgroup, sstate]], axis=1))
    own = (row % 32) // 16 == col // SP_
    s5_b = np.zeros((P, 2, 4, P), np.float32)
    s5_c = np.zeros((P, 2, SC, 32), np.float32)
    for j, (b, c) in enumerate(((a["s5_b_re_2"][0], a["s5_c_re_2"][0]), (a["s5_b_im_2"][0], a["s5_c_im_2"][0]))):
        s5_b[:, j][own] = b[group, state, row % 16][own]
        for g in range(SG):
            r, f = SP_ * (g % 2), 16 * (g % 2)
            s5_c[r:r + SP_, j, g // 2, f:f + 16] = c[g].T
    consts, hot = _constants()
    return {
        "x": np.ascontiguousarray(a["x"][0].T), "params": np.ascontiguousarray(params), "consts": consts,
        "rel_bias": a["rel_bias"], "onehot": hot, "weights": _weights(a), "s5_abt": np.stack(abt),
        "s5_b": s5_b.reshape(P, 2, 4 * P), "s5_c": s5_c, "positions": a["positions_2"],
    }


def kernel(**inputs):
    import concourse.bacc as bacc
    from concourse.bass_utils import run_bass_kernel_spmd

    arrays = _layouts({k: np.asarray(v) for k, v in inputs.items()})
    nc = bacc.Bacc("TRN2", target_bir_lowering=False, num_devices=1)
    aps = {n: nc.dram_tensor(f"in_{n}", x.shape, mybir.dt.from_np(x.dtype), kind="ExternalInput").ap()
           for n, x in arrays.items()}
    aps["out"] = nc.dram_tensor("out_y", (D, S), F32, kind="ExternalOutput").ap()
    two_blocks_kernel(nc, aps)
    r = run_bass_kernel_spmd(nc, [{f"in_{n}": x for n, x in arrays.items()}], core_ids=[0])
    return np.ascontiguousarray(r.results[0]["out_y"].T)[None]
```

```python
from contextlib import ExitStack

import concourse.bass as bass
from concourse import mybir
import numpy as np

F32 = mybir.dt.float32
F32R = mybir.dt.float32r
I32 = mybir.dt.int32
ACT = mybir.ActivationFunctionType
ALU = mybir.AluOpType
AX = mybir.AxisListType

P = 128
S = 256
ST = S // P
D = 1024
DC = D // P
DH = 128
SLOTS = 4
GROUPS = 3
HEADS = SLOTS * GROUPS
DILATIONS = (1, 4, 16)
HALF = 64
BUCKETS, MAX_DISTANCE = 32, 1024
TAB = 2 * S - 1
FF = 2816
FC = FF // P
PAIRS = FF // 256
EPS = 1e-6
NEG = -1e30
PADT = 8
WIDE = 2048
RAW = 3
SPL = 2
BANK = 512
SG, SP_ = 32, 64
SC = SG * SP_ // P
NS5 = 4 * P + SC
NANG = NS5 + S
CH = 64
MH = 8
TWO_PI = float(2 * np.pi)
C1 = 6.28125
C2 = float(np.float32(0.0019350051879882812))
C3 = TWO_PI - C1 - C2
MAGIC = 12582912.0


class Block:

    def __init__(self, kind, n, ncol, kc, tiles, banks, start=True, stop=True):
        self.kind, self.n, self.ncol, self.kc, self.tiles, self.banks = kind, n, ncol, kc, tiles, banks
        self.start, self.stop, self.used = start, stop, kc * ncol


def ftiles(cols, kc, x0=0):
    return [(t * S, "f", [(c, x0 + c) for c in range(kc)], t * P, P, 0) for t in range(cols // P)]


def ttiles(cols, kc, c0=0, base=0):
    return [(base + t * cols, "t", [(c, c) for c in range(kc)], c0, cols, t) for t in range(ST)]


def make_plan():
    plan = []

    def ffn(n):
        for j in range(PAIRS):
            plan.append(Block("up_a", n, 256, DC, ftiles(256, DC), 1))
            plan.append(Block("up_g", n, 256, DC, ftiles(256, DC), 1))
        for j in range(4):
            for k, (c0, kc) in enumerate(((0, 8), (8, 8), (16, 6))):
                plan.append(Block("down", n, 256, kc, ftiles(256, kc, c0), 1, k == 0, k == 2))

    for layer in range(2):
        for kind in "vqkug":
            tiles = ttiles(256, DC) if kind == "v" else ftiles(256, DC)
            plan += [Block(kind, layer, 256, DC, tiles, 1) for _ in range({"v": 6, "q": 6, "k": 6, "u": 4, "g": 6}[kind])]
        pool = [((2 * g + t) * S, "f", [(2 * g + c, 2 * g + c) for c in range(2)], t * P, P, 0)
                for g in range(4) for t in range(2)]
        plan.append(Block("pool", layer, 256, DC, pool, 0))
        plan += [Block("g", layer, 256, DC, ftiles(256, DC), 1) for _ in range(2)]
        plan += [Block("wb", layer, 512, 4, ftiles(512, 4), 2) for _ in range(2)]
        plan += [Block("wa", layer, 256, DC, ftiles(256, DC), 1) for _ in range(4)]
        plan += [Block("wo", layer, 256, DC, ftiles(256, DC), 1) for _ in range(4)]
        ffn(layer)
    for kind in ("ef", "eq", "ei", "eg", "eu"):
        tiles = ttiles(256, DC) if kind == "ei" else ftiles(256, DC)
        plan += [Block(kind, 0, 256, DC, tiles, 1) for _ in range(2)]
    plan.append(Block("glu", 0, 512, 4, ftiles(512, 4, 4), 2))
    plan += [Block("eo", 0, 256, DC, ftiles(256, DC), 1) for _ in range(4)]
    ffn(2)
    plan += [Block("mp", 0, 256, DC, ftiles(256, DC), 1) for _ in range(3)]
    plan += [Block("uq", 0, 384, 3, ftiles(384, 3), 2) for _ in range(4)]
    plan += [Block("ukv", 0, 1024, 2, [(t * S, "f", [(c, 3 + c) for c in range(2)], t * P, P, 0) for t in range(4)]
                   + [(1024 + t * 512, "t", [(c, 3 + c) for c in range(2)], 512, 512, t) for t in range(ST)], 4)
             for _ in range(2)]
    plan += [Block("mo", 0, 256, DC, ftiles(256, DC), 1) for _ in range(4)]
    ffn(3)

    out, last, turn, bank = 0, [0] * 4, 0, 0
    for b in plan:
        b.freed = 0
        if b.start and b.banks:
            if b.banks == 1:
                bank, turn = turn, (turn + 1) % 3
            else:
                bank, turn = 0, 0
            b.freed = max(last[bank:bank + b.banks])
        b.bank = bank
        if b.stop and b.banks:
            out += 1
            b.out = out
            for k in range(bank, bank + b.banks):
                last[k] = out
    return plan


PLAN = make_plan()
OFFSETS = [0]
for _b in PLAN:
    OFFSETS.append(OFFSETS[-1] + _b.used)


def last(kind, n=0):
    return max(i for i, b in enumerate(PLAN) if b.kind == kind and b.n == n)


def first(kind, n=0):
    return next(i for i, b in enumerate(PLAN) if b.kind == kind and b.n == n)


VECTORS = ([(f"norm1.{i}", 8) for i in range(2)] + [(f"norm2.{i}", 8) for i in range(2)] + [("norm_f", 8)]
           + [(f"pool_scale.{i}", 8) for i in range(2)]
           + [(f"conv{k}.{n}", FC) for n in range(4) for k in range(3)] + [(f"convb.{n}", FC) for n in range(4)]
           + [(f"mix.{i}", 8) for i in range(2)] + [(f"ffn.{i}", 8) for i in range(2)] + [("final", 8)]
           + [("lb0", 4), ("lb1", 4), ("hgrn_g", 4), ("s5_d", 4), ("b_glu", 4), ("q_g", 3), ("kv_g", 2)])
COL, NPAR = {}, 0
for _name, _n in VECTORS:
    COL[_name] = NPAR
    NPAR += _n
FFN_NORM = ("norm2.0", "norm2.1", "ffn.0", "ffn.1")

CONSTS = (("ident", P), ("rotate", P), ("causal", P), ("inv_count", 4 * S), ("freq", 1), ("chunk_causal", CH))
CCOL, NCONST = {}, 0
for _name, _n in CONSTS:
    CCOL[_name] = NCONST
    NCONST += _n


class Side:

    def __init__(self, eng, own):
        self.eng, self.own, self.given, self.taken, self.last = eng, own, {}, {}, None

    def give(self, ins, sem=None):
        sem = sem or self.own
        ins.then_inc(sem, 1)
        self.given[sem.name] = self.given.get(sem.name, 0) + 1
        self.last = (sem, self.given[sem.name])
        return ins

    def take(self, sem, events=1):
        self.taken[sem.name] = self.taken.get(sem.name, 0) + events
        self.eng.wait_ge(sem, self.taken[sem.name])

    def settle(self):
        self.eng.wait_ge(*self.last)


def two_blocks_kernel(nc, a):
    ctx = ExitStack()
    with ctx:
        base = [(nc.sbuf_base + 31) // 32 * 32]

        def region(size):
            at = base[0]
            base[0] += size
            return at

        def tile(name, at, shape, dt=F32):
            return nc.alloc_sbuf_tensor_at(name, shape, dt, offset=at)

        K = 1024
        raw = [tile(f"raw{j}", region(8 * K), [P, WIDE]) for j in range(RAW)]
        w_hi = [tile(f"w_hi{j}", region(8 * K), [P, WIDE], F32R) for j in range(SPL)]
        w_lo = [tile(f"w_lo{j}", region(8 * K), [P, WIDE], F32R) for j in range(SPL)]
        h = tile("h", region(8 * K), [P, DC, S])
        x_hi = tile("x_hi", region(8 * K), [P, DC, S], F32R)
        x_lo = tile("x_lo", region(8 * K), [P, DC, S], F32R)
        tmp = tile("tmp", region(8 * K), [P, DC, S])
        r_bm, r_hid, r_gate, r_att = region(24 * K), region(45568), region(16 * K), region(14 * K)
        par = tile("par", region(NPAR * 4 + 31 & ~31), [P, NPAR])
        cst = tile("cst", region(NCONST * 4 + 31 & ~31), [P, NCONST])
        ones = tile("ones", region(512), [P, P])
        small = tile("small", region(256), [P, 64])
        rstd = tile("rstd", region(2080), [P, 2 * S + 2])
        gg = tile("gg", region(32), [P, DC])
        cos_r = tile("cos_r", region(K), [P, 1, S])
        sin_r = tile("sin_r", region(K), [P, 1, S])
        s5_st = tile("s5_st", region(256), [P, 4, SC])
        bb = tile("bb", region(4 * K), [P, 2, 4, P])
        assert base[0] <= nc.sbuf_usable_end, base[0]

        bm = tile("bm", r_bm, [P, ST, SLOTS, GROUPS * S])
        qt = tile("qt", r_hid, [P, HEADS, S])
        kt = tile("kt", r_hid + 12 * K, [P, HEADS, S])
        va = tile("va", r_hid + 24 * K, [P, ST, HEADS * DH])
        ub = tile("ub", r_hid + 36 * K, [P, DC, S + 2 * PADT])
        ph = tile("ph", r_hid, [P, DC, S], F32R)
        pl = tile("pl", r_hid + 8 * K, [P, DC, S], F32R)
        po_h = tile("po_h", r_hid + 16 * K, [P, DC, S], F32R)
        po_l = tile("po_l", r_hid + 36 * K, [P, DC, S], F32R)
        gate_p = tile("gate_p", r_gate, [P, DC, S])
        gate_a = tile("gate_a", r_gate + 8 * K, [P, DC, S])
        lg = tile("lg", r_att, [P, GROUPS * S])
        pt = tile("pt", r_att + 3 * K, [P, GROUPS * ST, P])
        ao_h = tile("ao_h", r_att + 6 * K, [P, SLOTS, S], F32R)
        ao_l = tile("ao_l", r_att + 10 * K, [P, SLOTS, S], F32R)
        yh = tile("yh", r_hid, [P, FC, S], F32R)
        yl = tile("yl", r_hid + FC * K, [P, FC, S], F32R)
        cv = tile("cv", r_att, [P, 2, 2, S])
        ar = tile("ar", r_att + 4 * K, [P, 2, 2, S])
        xb_hi = tile("xb_hi", r_gate, [P, DC, S], F32R)
        xb_lo = tile("xb_lo", r_gate + 8 * K, [P, DC, S], F32R)
        ec = tile("ec", r_bm, [P, SC, S])
        es = tile("es", r_gate, [P, SC, S])
        etmp = tile("etmp", r_bm + 16 * K, [P, SC, P])
        sq2 = tile("sq2", r_bm + 16 * K, [P, DC, S])
        rf = tile("rf", r_att, [P, S + 2])
        rf2 = tile("rf2", r_att + 1056, [P, S + 2])
        names = ("fe", "key", "qb", "cum", "dd", "eb", "enb", "v2", "sg", "mask")
        fe, key, qb, cum, dd, eb, enb, v2, sgate, smask = (
            tile(n, r_hid + 4 * K * j, [P, 4 * S]) for j, n in enumerate(names))
        uu = tile("uu", r_hid + 40 * K, [P, 4 * S])
        am = tile("am", r_bm + 16 * K, [P, 8, P])
        ket = tile("ket", r_bm + 20 * K, [P, 8, P])
        st = tile("st", r_att + 2 * K, [P, 3, 4, P])
        cc = tile("cc", r_att + 8 * K, [P, 2, SC, 32])
        t_s5 = [tile(f"t_s5_{j}", r_hid + 4 * K * j, [P, 4 * S]) for j in range(10)]
        c6 = tile("c6", r_hid, [P, 6, S])
        qn = tile("qn", r_hid + 6 * K, [P, MH, S])
        rx = tile("rx", r_hid + 14 * K, [P, 4, S])
        kn = tile("kn", r_hid + 18 * K, [P, MH, S])
        v3 = tile("v3", r_hid + 26 * K, [P, ST, MH * DH])
        qr = tile("qr", r_hid + 34 * K, [P, 4, S])
        kr = tile("kr", r_hid + 38 * K, [P, 1, S])
        lm = tile("lm", r_att, [P, 2, 3, P])
        pm = tile("pm", r_att + 3 * K, [P, 3 * P])
        sqm = tile("sqm", r_att + 5 * K, [P, 5, S])
        NB = NANG * 4 + 31 & ~31
        ang = [tile(f"ang{j}", r_bm + NB * j if j < 7 else r_hid + 13 * K + NB * (j - 7), [P, NANG]) for j in range(10)]
        s5x = [tile(f"s5x{j}", r_hid + 2112 * j, [P, NS5]) for j in range(6)]
        relw = tile("relw", r_hid + 36 * K, [BUCKETS + 1, HEADS, P])
        pos_i = tile("pos_i", r_hid + 42 * K, [P, S], I32)
        tab = tile("tab", r_gate, [P, 2, SLOTS, TAB + 1])
        hot = tile("hot", r_att + 2 * K, [BUCKETS + 1, GROUPS * (TAB + 1)])
        relb = tile("relb", r_att + 8 * K, [BUCKETS + 1, HEADS])
        s5b = tile("s5b", r_att + 9 * K, [P, 2, 4 * P])
        assert 7 * NB <= 24 * K and 13 * K + 3 * NB <= 24 * K
        tab_dram = nc.dram_tensor("bias_table", (HEADS, P, TAB + 1), F32, kind="Internal").ap()

        pool_w = [tile(f"pool_w{j}", region(2176), [P, 2, S + 2 * PADT]) for j in range(2)]
        assert base[0] <= nc.sbuf_usable_end, base[0]

        G = ctx.enter_context(nc.psum_tensor("gemm", [P, 4 * BANK], F32))
        A = ctx.enter_context(nc.psum_tensor("aux", [P, 4 * BANK], F32))
        ident = cst[:, CCOL["ident"]:CCOL["ident"] + P]
        rotate = cst[:, CCOL["rotate"]:CCOL["rotate"] + P]
        causal = cst[:, CCOL["causal"]:CCOL["causal"] + P]
        freq = cst[:, CCOL["freq"]:CCOL["freq"] + 1]
        ccausal = cst[:, CCOL["chunk_causal"]:CCOL["chunk_causal"] + CH].bitcast(I32)
        eps = small[:, 0:1]
        lb, omlb, nbglu = small[:, 4:8], small[:, 8:12], small[:, 12:16]
        lbt = small[:, 16:28]
        mx, nm, sums, rs = small[:, 28:30], small[:, 30:32], small[:, 32:34], small[:, 34:36]

        def vec(name, c):
            return par[:, COL[name] + c:COL[name] + c + 1]

        def inv_count(g):
            return cst[:, CCOL["inv_count"] + g * S:CCOL["inv_count"] + (g + 1) * S]

        def sem(name):
            return ctx.enter_context(nc.semaphore(name))

        x_in, par_in, cst_in = sem("x_in"), sem("par_in"), sem("cst_in")
        s5_in, s5b_in, pos_in, hot_in, cc_in = sem("s5_in"), sem("s5b_in"), sem("pos_in"), sem("hot_in"), sem("cc_in")
        relb_in, bm_in = sem("relb_in"), sem("bm_in")
        tab_out = [sem(f"tab_out{j}") for j in range(GROUPS)]
        raw_in = [sem(f"raw_in{j}") for j in range(RAW)]
        out_done = sem("out_done")
        w_hi_ready, w_lo_ready = sem("w_hi_ready"), sem("w_lo_ready")
        mm_done = sem("mm_done")
        read_out = sem("read_out")
        act_own, dve_own, pool_own = sem("act_own"), sem("dve_own"), sem("pool_own")
        ones_ready = sem("ones_ready")
        x_f32, x_hi_ready, x_ready = sem("x_f32"), sem("x_hi_ready"), sem("x_ready")
        sq_ready, ms_ready, rms_ready, hf_ready = sem("sq_ready"), sem("ms_ready"), sem("rms_ready"), sem("hf_ready")
        relb_ready, tab_ready, tab_copied = sem("relb_ready"), sem("tab_ready"), sem("tab_copied")
        dt_ready, th_ready, mag_ready, red_ready = sem("dt_ready"), sem("th_ready"), sem("mag_ready"), sem("red_ready")
        trig_ready, den_ready, bb_ready, ndt_ready = sem("trig_ready"), sem("den_ready"), sem("bb_ready"), sem("ndt_ready")
        rope_kept = sem("rope_kept")
        qkv_ready, scores_ready, scores_read = sem("qkv_ready"), sem("scores_ready"), sem("scores_read")
        lg_ready, exp_ready, prob_ready = sem("lg_ready"), sem("exp_ready"), sem("prob_ready")
        tr_ready, pt_ready = sem("tr_ready"), sem("pt_ready")
        pv_ready, pv_hi, pv_read = sem("pv_ready"), sem("pv_hi"), sem("pv_read")
        u_zero, u_ready, pooled = sem("u_zero"), sem("u_ready"), sem("pooled")
        gate_exp = sem("gate_exp")
        conv_mid, conv_done, act_ready, act_scaled, y_hi, y_ready = (
            sem("conv_mid"), sem("conv_done"), sem("act_ready"), sem("act_scaled"), sem("y_hi"), sem("y_ready"))
        gate_in, rf_ready, rstd_ready, ms2_ready = sem("gate_in"), sem("rf_ready"), sem("rstd_ready"), sem("ms2_ready")
        e_ready, smask_ready, am_zero, cc_ready = sem("e_ready"), sem("smask_ready"), sem("am_zero"), sem("cc_ready")
        rden_ready, lbd_ready, lbe_ready = sem("rden_ready"), sem("lbd_ready"), sem("lbe_ready")
        f_ready, ln_ready, cum_ready, eb_ready, qd_ready = (sem("f_ready"), sem("ln_ready"), sem("cum_ready"),
                                                            sem("eb_ready"), sem("qd_ready"))
        att_ready, am_ready, ket_psum, ket_ready = sem("att_ready"), sem("am_ready"), sem("ket_psum"), sem("ket_ready")
        ds_ready, st_ready, o_ready = sem("ds_ready"), sem("st_ready"), sem("o_ready")
        bu_ready, bu_read, z_ready, z_read, s_ready, ys_ready = (sem("bu_ready"), sem("bu_read"), sem("z_ready"),
                                                                 sem("z_read"), sem("s_ready"), sem("ys_ready"))
        yd_ready, zg_ready, s5_free = sem("yd_ready"), sem("zg_ready"), sem("s5_free")
        rx_ready, rot_ready, rope_ready = sem("rx_ready"), sem("rot_ready"), sem("rope_ready")
        final_ready = sem("final_ready")

        block = ctx.enter_context(nc.Block())
        N = len(PLAN)

        @block.sync
        def _(sp):
            def load(dst, src, s):
                sp.dma_start(dst, src).then_inc(s, 16)

            load(h[:, :, :], a["x"].rearrange("(c p) s -> p c s", p=P), x_in)
            load(par[:, :], a["params"], par_in)

            def weights(i):
                b = PLAN[i]
                if i >= RAW:
                    sp.wait_ge(w_lo_ready, i - RAW + 1)
                load(raw[i % RAW][:, 0:b.used],
                     a["weights"][OFFSETS[i] * P:OFFSETS[i + 1] * P].rearrange("(p n) -> p n", p=P), raw_in[i % RAW])

            for i in range(RAW):
                weights(i)
            load(relb[0:BUCKETS, :], a["rel_bias"], relb_in)
            load(cst[:, :], a["consts"], cst_in)
            load(hot[:, :], a["onehot"], hot_in)
            for j in range(3):
                load(ang[j][:, 0:NS5], a["s5_abt"][j], s5_in)
            load(s5b[:, :, :], a["s5_b"], s5b_in)
            load(pos_i[:, :], a["positions"].to_broadcast([P, S]), pos_in)

            def store_table(g):
                sp.wait_ge(tab_copied, g + 1)
                load(tab_dram[g * SLOTS:(g + 1) * SLOTS].rearrange("h p n -> p h n"), tab[:, g % 2, :, :], tab_out[g])

            def load_bias():
                for s_ in tab_out:
                    sp.wait_ge(s_, 16)
                sp.wait_ge(bb_ready, 1)
                for q in range(ST):
                    for s in range(SLOTS):
                        src = bass.AP(tab_dram.tensor, s * P * (TAB + 1) + S - 1 - q * P,
                                      [[TAB, P], [SLOTS * P * (TAB + 1), GROUPS], [1, S]])
                        load(bm[:, q, s, :].rearrange("p (g n) -> p g n", g=GROUPS), src, bm_in)

            for i in range(RAW, N):
                weights(i)
                if i in (7, 9, 11):
                    store_table((i - 7) // 2)
                if i == first("k", 0):
                    load_bias()
                if i == first("down", 1) + 6:
                    load(cc[:, :, :, :], a["s5_c"], cc_in)
            sp.wait_ge(final_ready, 1)
            load(a["out"].rearrange("(c p) s -> p c s", p=P), tmp[:, :, :], out_done)
            sp.wait_ge(out_done, 16)

        @block.tensor
        def _(pe):
            me = Side(pe, None)

            def gemm(i, hi, lo, chunks_at=(), dst=G):
                b = PLAN[i]
                wh = w_hi[i % SPL][:, 0:b.used].rearrange("p (c n) -> p c n", c=b.kc)
                wl = w_lo[i % SPL][:, 0:b.used].rearrange("p (c n) -> p c n", c=b.kc)
                pe.wait_ge(w_lo_ready, i + 1)
                if b.freed:
                    pe.wait_ge(read_out, b.freed)
                todo = dict(chunks_at)
                mm = None
                for at, (off, kind, pairs, c0, n, t) in enumerate(b.tiles):
                    o = (b.bank * BANK if b.banks else 0) + off
                    for k, (wc, xc) in enumerate(pairs):
                        if xc in todo:
                            me.take(*todo.pop(xc))
                        fresh = b.start and k == 0 and (at == 0 or b.stop)
                        end = b.stop and k == len(pairs) - 1
                        if kind == "f":
                            out = dst[:, o:o + S]
                            two = [(wh[:, wc, c0:c0 + P], hi[:, xc, :]), (wh[:, wc, c0:c0 + P], lo[:, xc, :]),
                                   (wl[:, wc, c0:c0 + P], hi[:, xc, :])]
                        else:
                            out = dst[:, o:o + n]
                            tok = slice(t * P, (t + 1) * P)
                            two = [(hi[:, xc, tok], wh[:, wc, c0:c0 + n]), (hi[:, xc, tok], wl[:, wc, c0:c0 + n]),
                                   (lo[:, xc, tok], wh[:, wc, c0:c0 + n])]
                        for m, (lhs, rhs) in enumerate(two):
                            mm = pe.matmul(out, lhs, rhs, start=fresh and m == 0, stop=end and m == 2,
                                           skip_group_check=True)
                me.give(mm, mm_done)

            def mean_square(chunks, outs):
                me.take(sq_ready)
                mm = None
                for cs, o in zip(chunks, outs):
                    for k, c in enumerate(cs):
                        mm = pe.matmul(A[:, o:o + S], ones[:, :], tmp[:, c, :], start=k == 0, stop=k == len(cs) - 1,
                                       skip_group_check=True)
                me.give(mm, ms_ready)

            def norm(bank=0, src=tmp, tokens=True, pairs=4, ready=ms_ready):
                o = bank * BANK
                mm = None
                for c in range(DC):
                    if c % (DC // pairs) == 0:
                        me.take(sq_ready)
                    mm = pe.matmul(A[:, o:o + S], ones[:, :], src[:, c, :], start=c == 0, stop=c == DC - 1,
                                   skip_group_check=True)
                for t in range(ST if tokens else 0):
                    for c in range(DC):
                        mm = pe.matmul(A[:, o + S + t:o + S + t + 1], src[:, c, t * P:(t + 1) * P], ones[:, 0:1],
                                       start=c == 0, stop=c == DC - 1, skip_group_check=True)
                me.give(mm, ready)

            BY_PAIR = {c: (x_ready, 1) for c in (0, 2, 4, 6)}

            def ffn(n):
                i = first("up_a", n)
                xh, xl = (x_hi, x_lo) if n < 2 else (xb_hi, xb_lo)
                for j in range(2 * PAIRS):
                    gemm(i + j, xh, xl, BY_PAIR if j == 0 else ())
                    if j == 0:
                        norm(tokens=False)
                i += 2 * PAIRS
                for j in range(12):
                    wait = {0: {0: (y_ready, 4)}, 1: {8: (y_ready, 4)}, 2: {16: (y_ready, 3)}}.get(j, ())
                    gemm(i + j, yh, yl, wait)

            def scores(u):
                s, q = divmod(u, ST)
                me.take(scores_read) if u else None
                mm = None
                for g in range(GROUPS):
                    hd = g * SLOTS + s
                    mm = pe.matmul(A[:, g * S:(g + 1) * S], qt[:, hd, q * P:(q + 1) * P], kt[:, hd, :],
                                   start=True, stop=True, skip_group_check=True)
                me.give(mm, scores_ready)

            def turn(u):
                me.take(prob_ready)
                mm = None
                for k in range(GROUPS * ST):
                    mm = pe.transpose(A[:, 2 * BANK + k * P:2 * BANK + (k + 1) * P], lg[:, k * P:(k + 1) * P], ident)
                me.give(mm, tr_ready)

            def pv(u, layer):
                s, q = divmod(u, ST)
                me.take(pt_ready)
                if u:
                    me.take(pv_read)
                mm = None
                for k in range(GROUPS * ST):
                    hd = (k // ST) * SLOTS + s
                    mm = pe.matmul(G[:, 3 * BANK:3 * BANK + P], va[:, k % ST, hd * DH:(hd + 1) * DH], pt[:, k, :],
                                   start=k == 0, stop=k == GROUPS * ST - 1, skip_group_check=True)
                me.give(mm, pv_ready)

            def table(g):
                if g:
                    me.take(tab_copied)
                mm = None
                for s in range(SLOTS):
                    mm = pe.matmul(A[:, s * BANK:(s + 1) * BANK], relw[:, g * SLOTS + s, :],
                                   hot[:, g * (TAB + 1):(g + 1) * (TAB + 1)], start=True, stop=True)
                me.give(mm, tab_ready)

            def mixer(layer):
                i = first("v", layer)
                for j in range(18):
                    gemm(i + j, x_hi, x_lo, BY_PAIR if j == 0 else ())
                    if j == 0:
                        if layer == 0:
                            me.take(ones_ready)
                        norm()
                    if layer == 0 and j in (3, 5, 7):
                        if j == 3:
                            pe.wait_ge(hot_in, 16)
                            me.take(relb_ready)
                            pe.wait_ge(rstd_ready, 1)
                        table((j - 3) // 2)
                if layer == 0:
                    me.take(tab_copied)
                    pe.wait_ge(cst_in, 16)
                me.take(qkv_ready)
                for j in range(10):
                    gemm(i + 18 + j, x_hi, x_lo)
                    if j < 8:
                        scores(j)
                    if 2 <= j:
                        pv(j - 2, layer)
                    if 1 <= j < 9:
                        turn(j - 1)
                me.take(scores_read)
                gemm(first("pool", layer), ph, pl, {0: (x_ready, 1)}, dst=A)
                for j in range(2):
                    gemm(first("pool", layer) + 1 + j, x_hi, x_lo)
                me.take(pv_read)
                for j in range(2):
                    gemm(first("wb", layer) + j, ao_h, ao_l)
                for j in range(4):
                    gemm(first("wa", layer) + j, po_h, po_l, {0: (x_ready, 1), 4: (x_ready, 1)} if j == 0 else ())
                for j in range(4):
                    gemm(first("wo", layer) + j, ph, pl, BY_PAIR if j == 0 else ())
                ffn(layer)

            for layer in range(2):
                mixer(layer)

            i = first("ef")
            for j in range(10):
                gemm(i + j, x_hi, x_lo, BY_PAIR if j == 0 else ())
                if j == 0:
                    norm()
                    norm(bank=1, src=sq2, pairs=1, ready=ms2_ready)
            me.take(qd_ready)
            q4 = qb.rearrange("p (c s) -> p c s", c=4)
            k4 = enb.rearrange("p (c s) -> p c s", c=4)
            ke4 = dd.rearrange("p (c s) -> p c s", c=4)
            v24 = v2.rearrange("p (t n) -> p t n", t=ST)
            for c in range(4):
                for n in range(4):
                    r, o = CH * (n % 2), (2 * c + n // 2) * CH
                    mm = pe.matmul(A[r:r + CH, o:o + CH], k4[:, c, n * CH:(n + 1) * CH], q4[:, c, n * CH:(n + 1) * CH],
                                   start=True, stop=True, skip_group_check=True)
            me.give(mm, att_ready)
            for c in range(4):
                for t in range(ST):
                    o = BANK + (2 * c + t) * P
                    mm = pe.transpose(A[:, o:o + P], ke4[:, c, t * P:(t + 1) * P], ident)
            me.give(mm, ket_psum)
            me.take(ket_ready)
            for n in range(3):
                if n:
                    me.take(st_ready)
                r, t = CH * (n % 2), n // 2
                for c in range(4):
                    mm = pe.matmul(A[:, 3 * BANK + c * P:3 * BANK + (c + 1) * P], ket[r:r + CH, 2 * c + t, :],
                                   v24[r:r + CH, t, c * P:(c + 1) * P], start=True, stop=True, skip_group_check=True)
                me.give(mm, ds_ready)
            me.take(am_ready)
            me.take(st_ready)
            for c in range(4):
                for t in range(ST):
                    o = BANK + c * S + t * P
                    mm = pe.matmul(A[:, o:o + P], v24[:, t, c * P:(c + 1) * P], am[:, 2 * c + t, :],
                                   start=True, stop=False, skip_group_check=True)
                    for n in range(2 * t, 2 * t + 2):
                        if n:
                            oo = o + (n % 2) * CH
                            mm = pe.matmul(A[:, oo:oo + CH], st[:, n - 1, c, :], q4[:, c, n * CH:(n + 1) * CH],
                                           start=False, stop=n % 2 == 1, skip_group_check=True)
            me.give(mm, o_ready)
            mean_square([[0], [1], [2], [3]], [0, S, 3 * BANK, 3 * BANK + S])
            me.take(cc_ready)
            me.take(bb_ready)
            me.take(s5_free)
            u4 = uu.rearrange("p (c s) -> p c s", c=4)

            def s5_in_mm(g):
                if g:
                    me.take(bu_read)
                m = None
                for part in range(2):
                    for k in range(4):
                        o = k * BANK + part * S
                        m = pe.matmul(A[:, o:o + S], bb[32 * k:32 * k + 32, part, g, :], u4[32 * k:32 * k + 32, g, :],
                                      start=True, stop=True, skip_group_check=True, tile_position=(32 * k, 0))
                me.give(m, bu_ready)

            def s5_out_mm(g):
                me.take(s_ready)
                m = None
                sre = t_s5[6].rearrange("p (c s) -> p c s", c=4)
                sim = t_s5[8].rearrange("p (c s) -> p c s", c=4)
                for k in range(4):
                    o = G[32 * k:32 * k + 32, g * BANK:g * BANK + S]
                    pe.matmul(o, cc[:, 0, 4 * g + k, :], sre[:, k, :], start=True, stop=False, skip_group_check=True,
                              tile_position=(0, 32 * k))
                    m = pe.matmul(o, cc[:, 1, 4 * g + k, :], sim[:, k, :], start=False, stop=True,
                                  skip_group_check=True, tile_position=(0, 32 * k))
                me.give(m, ys_ready)

            pe.wait_ge(read_out, PLAN[first("eu") + 1].out)
            s5_in_mm(0)
            for g in range(4):
                if g < 3:
                    s5_in_mm(g + 1)
                s5_out_mm(g)
            me.take(x_ready)
            pe.wait_ge(yd_ready, 4)
            gemm(first("glu"), x_hi, x_lo, {4: (x_ready, 1)})
            for j in range(4):
                gemm(first("eo") + j, x_hi, x_lo, {4: (x_ready, 1)} if j == 0 else ())
            ffn(2)

            for j in range(3):
                gemm(first("mp") + j, x_hi, x_lo, BY_PAIR if j == 0 else ())
                if j == 0:
                    norm(tokens=False)
            for j in range(4):
                gemm(first("uq") + j, xb_hi, xb_lo, {0: (x_ready, 1), 2: (x_ready, 1)} if j == 0 else ())
                if j == 0:
                    me.take(sq_ready)
                    for o, cs in ((0, (0, 1, 2)), (S, (3, 4))):
                        for c in cs:
                            pe.matmul(A[:, o:o + S], ones[:, :], sqm[:, c, :], start=c == cs[0], stop=c == cs[-1],
                                      skip_group_check=True)
                    for t in range(ST):
                        for c in (3, 4):
                            mm = pe.matmul(A[:, 2 * S + t:2 * S + t + 1], sqm[:, c, t * P:(t + 1) * P], ones[:, 0:1],
                                           start=c == 3, stop=c == 4, skip_group_check=True)
                    me.give(mm, ms_ready)
            for j in range(2):
                gemm(first("ukv") + j, xb_hi, xb_lo, {3: (x_ready, 1)} if j == 0 else ())
            me.take(rx_ready)
            rxf = rx.rearrange("p c s -> p (c s)")
            for k in range(2):
                pe.matmul(A[:, k * BANK:(k + 1) * BANK], rotate, rxf[:, k * BANK:(k + 1) * BANK], start=True, stop=True)
            mm = pe.matmul(A[:, 2 * BANK:2 * BANK + S], rotate, c6[:, 5, :], start=True, stop=True)
            me.give(mm, rot_ready)
            me.take(rope_ready)

            def m_scores(hd):
                if hd >= 2:
                    me.take(scores_read)
                b0, r = (hd % 2) * BANK, 64 * (hd % 2)
                m = None
                for q in range(ST):
                    nk = (q + 1) * P
                    o = A[:, b0 + q * P:b0 + q * P + nk]
                    pe.matmul(o, qn[:, hd, q * P:(q + 1) * P], kn[:, hd, 0:nk], start=True, stop=False,
                              skip_group_check=True)
                    m = pe.matmul(o, qr[r:r + 64, hd // 2, q * P:(q + 1) * P], kr[r:r + 64, 0, 0:nk], start=False,
                                  stop=True, skip_group_check=True)
                me.give(m, scores_ready)

            for j in range(MH + 2):
                if j < MH:
                    m_scores(j)
                if j >= 2:
                    hd = j - 2
                    me.take(pt_ready)
                    if hd:
                        me.take(pv_read)
                    o = 3 * BANK
                    pe.matmul(A[:, o:o + S], v3[:, 0, hd * DH:(hd + 1) * DH], pm[:, 0:S], start=True, stop=False,
                              skip_group_check=True)
                    mm = pe.matmul(A[:, o + P:o + S], v3[:, 1, hd * DH:(hd + 1) * DH], pm[:, S:S + P], start=False,
                                   stop=True, skip_group_check=True)
                    me.give(mm, pv_ready)
                if 1 <= j <= MH:
                    me.take(prob_ready)
                    for k in range(3):
                        mm = pe.transpose(A[:, 2 * BANK + k * P:2 * BANK + (k + 1) * P], lm[:, (j - 1) % 2, k, :], ident)
                    me.give(mm, tr_ready)
            me.take(scores_read, 2)
            me.take(pv_read)
            for j in range(4):
                gemm(first("mo") + j, x_hi, x_lo)
            ffn(3)
            norm(tokens=False)

        @block.scalar
        def _(act):
            me = Side(act, act_own)

            def split(i):
                if i >= N:
                    return
                n = PLAN[i].used
                act.wait_ge(raw_in[i % RAW], 16 * (i // RAW + 1))
                if i >= SPL:
                    act.wait_ge(mm_done, i - SPL + 1)
                me.give(act.activation(w_hi[i % SPL][:, 0:n], raw[i % RAW][:, 0:n], ACT.Copy), w_hi_ready)

            def split_all(i, n):
                for k in range(n):
                    split(i + k + SPL)

            def hi(dst, src):
                me.take(x_f32)
                me.give(act.activation(dst, src, ACT.Copy), x_hi_ready)

            def root(outs):
                me.take(ms_ready)
                for k, (dst, off, width, count_) in enumerate(outs):
                    ins = act.activation(dst, A[:, off:off + width], ACT.Sqrt, bias=eps, scale=1.0 / count_)
                me.give(ins, rms_ready)

            def feed(j, g, xh=x_hi, x=h, sq=tmp):
                for c in (2 * j, 2 * j + 1):
                    ins = act.activation(xh[:, c, :], x[:, c, :], ACT.Copy, scale=g(c))
                me.give(ins, x_hi_ready)
                me.give(act.activation(sq[:, 2 * j:2 * j + 2, :], x[:, 2 * j:2 * j + 2, :], ACT.Square), sq_ready)

            def named(name):
                return lambda c: vec(name, c)

            def feed_after(i, g, xh=x_hi, step=1):
                for j in range(4):
                    for k in range(step - 1):
                        split(i + step * j + k + 2)
                    act.wait_ge(read_out, PLAN[i + step * j + step - 1].out)
                    feed(j, g, xh)
                    split(i + step * j + step + 1)

            def tokens_root():
                root([(rstd[:, 0:S + 2], 0, S + 2, D)])

            def psum(i):
                b = PLAN[i]
                act.wait_ge(mm_done, i + 1)
                return G[:, b.bank * BANK:(b.bank + b.banks) * BANK]

            def ffn(n, then, xh=x_hi):
                i = first("up_a", n)
                centre = 1 if n < 2 else 2
                func = ACT.Gelu_apprx_tanh if n < 2 else ACT.Silu
                split(i + 2)
                root([(rstd[:, 0:S], 0, S, D)])
                for j in range(PAIRS):
                    ia, c, x = i + 2 * j, cv[:, j % 2, :, :], ar[:, j % 2, :, :]
                    if j >= 2:
                        act.wait_ge(y_ready, n * PAIRS + j - 1)
                    act.wait_ge(read_out, PLAN[ia].out)
                    for t in range(2):
                        ins = act.activation(c[:, t, :], x[:, t, :], ACT.Identity, bias=vec(f"convb.{n}", 2 * j + t),
                                             scale=vec(f"conv{centre}.{n}", 2 * j + t))
                    me.give(ins, conv_mid)
                    if j:
                        split(ia + 2)
                    me.take(conv_done)
                    me.give(act.activation(c, c, func), act_ready)
                    split(ia + 3)
                    act.wait_ge(read_out, PLAN[ia + 1].out)
                    me.give(act.activation(yh[:, 2 * j:2 * j + 2, :], c, ACT.Copy), y_hi)
                then(first("down", n))

            def pv_half(u):
                s, q = divmod(u, ST)
                me.take(pv_ready)
                me.give(act.activation(ao_h[:, s, q * P:(q + 1) * P], G[:, 3 * BANK:3 * BANK + P], ACT.Copy), pv_hi)

            def gate(layer, j):
                act.wait_ge(gate_in, 8 * layer + j + 1)
                g = (gate_p if j < 4 else gate_a)[:, 2 * (j % 4):2 * (j % 4) + 2, :]
                me.give(act.activation(g, g, ACT.Exp, scale=-1.0), gate_exp)

            def mixer(layer):
                i = first("v", layer)
                split(i + 2)
                tokens_root()
                for j in range(1, 18):
                    split(i + j + 2)
                    if layer == 0:
                        setup.get(j, lambda: None)()
                for j in range(10):
                    ib = i + 18 + j
                    split(ib + 2)
                    if j >= 4:
                        gate(layer, j - 4)
                    if j < 8:
                        me.take(lg_ready)
                        me.give(act.activation(lg[:, :], lg[:, :], ACT.Exp, bias=nm[:, 0:1], accum_out=sums[:, 0:1]),
                                exp_ready)
                    if 2 <= j:
                        pv_half(j - 2)
                    if 1 <= j < 9:
                        me.take(tr_ready)
                        ptf = pt.rearrange("p k n -> p (k n)")
                        act.activation(ptf[:, 0:BANK], A[:, 2 * BANK:3 * BANK], ACT.Copy)
                        me.give(act.activation(ptf[:, BANK:6 * P], A[:, 3 * BANK:3 * BANK + 2 * P], ACT.Copy), pt_ready)
                    if j == 8:
                        me.take(pooled, 4)
                        me.give(act.activation(ph[:, :, :], tmp[:, :, :], ACT.Copy), x_hi_ready)
                ip = first("pool", layer)
                act.wait_ge(mm_done, ip + 1)
                for k in range(DC):
                    ins = act.activation(po_h[:, k, :], A[:, k * S:(k + 1) * S], ACT.Copy,
                                         scale=vec(f"pool_scale.{layer}", k))
                    if k % 4 == 3:
                        me.give(ins, x_hi_ready)
                split(ip + 2)
                for j in range(2):
                    split(ip + 3 + j)
                    gate(layer, 6 + j)
                split_all(first("wb", layer), 2)
                for j in range(4):
                    split(first("wa", layer) + j + 2)
                    hi(ph[:, 2 * j:2 * j + 2, :], tmp[:, 2 * j:2 * j + 2, :])
                feed_after(first("wo", layer), named(f"norm2.{layer}"))

            act.wait_ge(par_in, 16)
            act.wait_ge(x_in, 16)
            for j in range(4):
                feed(j, named("norm1.0"))
                if j in (0, 3):
                    split(0 if j == 0 else 1)

            dt, mag = ang[3], ang[4]

            def setup_dt():
                act.wait_ge(s5_in, 48)
                me.give(act.activation(dt[:, 0:NS5], ang[2][:, 0:NS5], ACT.Exp), dt_ready)
                me.take(lbd_ready)
                me.give(act.activation(lbt[:, 0:8], lbt[:, 0:8], ACT.Exp), lbe_ready)

            def setup_mag():
                me.take(ndt_ready)
                me.give(act.activation(mag[:, 0:NS5], mag[:, 0:NS5], ACT.Exp), mag_ready)

            def setup_trig():
                me.take(red_ready)
                act.activation(ang[7][:, :], ang[7][:, :], ACT.Sin)
                me.give(act.activation(ang[8][:, :], ang[8][:, :], ACT.Sin), trig_ready)

            def setup_table(g):
                me.take(tab_ready)
                if g == 2:
                    act.wait_ge(tab_out[0], 16)
                me.give(act.activation(tab[:, g % 2, :, :].rearrange("p h n -> p (h n)"), A[:, :], ACT.Copy), tab_copied)

            setup = {1: setup_dt, 2: setup_mag, 3: setup_trig, 4: lambda: setup_table(0), 6: lambda: setup_table(1),
                     8: lambda: setup_table(2)}
            mixer(0)
            ffn(0, lambda i: feed_after(i, named("norm1.1"), step=3))
            mixer(1)

            def feed_two(i):
                feed_after(i, lambda c: gg[:, c:c + 1], step=3)
                act.wait_ge(e_ready, 1)
                for c in range(DC):
                    ins = act.activation(sq2[:, c, :], h[:, c, :], ACT.Square, scale=vec("norm_f", c))
                me.give(ins, sq_ready)

            ffn(1, feed_two)
            i = first("ef")
            split(i + 2)
            root([(rf[:, :], 0, S + 2, D)])
            me.take(rf_ready)
            me.give(act.activation(rstd[:, 0:S + 2], rstd[:, 0:S + 2], ACT.Sqrt, bias=eps, scale=1.0 / D), rms_ready)
            for j in range(2):
                act.wait_ge(gate_in, 17 + j)
                f = fe[:, j * BANK:(j + 1) * BANK]
                me.give(act.activation(f, f, ACT.Exp, scale=-1.0), gate_exp)
                if j:
                    split(i + 3)
            split(i + 4)
            me.take(f_ready)
            me.give(act.activation(fe[:, :], fe[:, :], ACT.Ln), ln_ready)
            split(i + 5)
            me.take(cum_ready)
            act.activation(eb[:, :], cum[:, :], ACT.Exp)
            act.activation(enb[:, :], cum[:, :], ACT.Exp, scale=-1.0)
            me.give(act.activation(dd[:, :], dd[:, :], ACT.Exp), eb_ready)
            split_all(i + 4, 2)
            for j in range(2):
                act.wait_ge(gate_in, 19 + j)
                me.give(act.activation(sgate[:, j * BANK:(j + 1) * BANK], fe[:, j * BANK:(j + 1) * BANK], ACT.Exp,
                                       scale=-1.0), gate_exp)
                split(i + 8 + j)
            split_all(i + 8, 2)
            me.take(ket_psum)
            me.give(act.activation(ket.rearrange("p k n -> p (k n)"), A[:, BANK:3 * BANK], ACT.Copy), ket_ready)
            me.take(o_ready)
            me.give(act.activation(tmp[:, 0:4, :].rearrange("p c s -> p (c s)"), A[:, BANK:3 * BANK], ACT.Square),
                    sq_ready)
            root([(fe[:, 0:BANK], 0, BANK, DH), (fe[:, BANK:2 * BANK], 3 * BANK, BANK, DH)])
            hi(x_hi[:, 0:4, :], tmp[:, 0:4, :])
            for g in range(4):
                me.take(yd_ready)
                me.give(act.activation(tmp[:, 4 + g, :], tmp[:, 4 + g, :], ACT.Gelu_apprx_tanh), zg_ready)
            me.settle()
            me.give(act.activation(x_hi[:, 4:8, :], tmp[:, 4:8, :], ACT.Copy), x_hi_ready)
            ig = first("glu")
            p = psum(ig)
            for k in range(4):
                ins = act.activation(t_s5[0][:, k * S:(k + 1) * S], p[:, k * S:(k + 1) * S], ACT.Exp, bias=nbglu[:, k:k + 1],
                                     scale=-1.0)
            me.give(ins, gate_exp)
            split(ig + 2)
            hi(x_hi[:, 4:8, :], tmp[:, 4:8, :])
            feed_after(first("eo"), named("ffn.0"), xb_hi)
            ffn(2, lambda i: feed_after(i, named("mix.1"), step=3))
            i = first("mp")
            split(i + 2)
            root([(rstd[:, 0:S], 0, S, D)])
            for j in range(3):
                act.wait_ge(read_out, PLAN[i + j].out)
                cs = range(2 * j, min(2 * j + 2, 5))
                for c in cs:
                    ins = act.activation(xb_hi[:, c, :], c6[:, c, :], ACT.Copy,
                                         scale=vec("q_g", c) if c < 3 else vec("kv_g", c - 3))
                me.give(ins, x_hi_ready)
                ins = act.activation(sqm[:, cs[0]:cs[-1] + 1, :], c6[:, cs[0]:cs[-1] + 1, :], ACT.Square)
                if j == 2:
                    me.give(ins, sq_ready)
                else:
                    split(i + 3 + j)
            split(first("uq") + 2)
            root([(rstd[:, 0:S], 0, S, 384), (rstd[:, S:2 * S + 2], S, S + 2, 256)])
            split_all(first("uq") + 1, 5)
            for j in range(MH + 2):
                if j < MH:
                    me.take(lg_ready)
                    l = lm[:, j % 2, :, :].rearrange("p k n -> p (k n)")
                    act.activation(l[:, 0:P], l[:, 0:P], ACT.Exp, bias=nm[:, 0:1], accum_out=sums[:, 0:1])
                    me.give(act.activation(l[:, P:3 * P], l[:, P:3 * P], ACT.Exp, bias=nm[:, 1:2],
                                           accum_out=sums[:, 1:2]), exp_ready)
                if j >= 2:
                    me.take(pv_ready)
                    me.give(act.activation(x_hi[:, j - 2, :], A[:, 3 * BANK:3 * BANK + S], ACT.Copy), pv_hi)
                if 1 <= j <= MH:
                    me.take(tr_ready)
                    me.give(act.activation(pm[:, :], A[:, 2 * BANK:2 * BANK + 3 * P], ACT.Copy), pt_ready)
            feed_after(first("mo"), named("ffn.1"), xb_hi)

            def squares(i):
                for j in range(4):
                    split_all(i + 3 * j, 3)
                    act.wait_ge(read_out, PLAN[i + 3 * j + 2].out)
                    me.give(act.activation(tmp[:, 2 * j:2 * j + 2, :], h[:, 2 * j:2 * j + 2, :], ACT.Square), sq_ready)

            ffn(3, squares)
            root([(rstd[:, 0:S], 0, S, D)])

        @block.vector
        def _(v):
            me = Side(v, dve_own)

            def split(i):
                if i >= N:
                    return
                n = PLAN[i].used
                me.taken[w_hi_ready.name] = i
                me.take(w_hi_ready)
                me.give(v.tensor_tensor(w_lo[i % SPL][:, 0:n], raw[i % RAW][:, 0:n],
                                        w_hi[i % SPL][:, 0:n].bitcast(F32), ALU.subtract), w_lo_ready)

            def lo(dst, src, hi_, signal=x_ready):
                me.take(x_hi_ready)
                me.give(v.tensor_tensor(dst, src, hi_.bitcast(F32), ALU.subtract), signal)

            def psum(i):
                b = PLAN[i]
                v.wait_ge(mm_done, i + 1)
                return G[:, b.bank * BANK:(b.bank + b.banks) * BANK]

            def feed(j, g, xh=x_hi, xl=x_lo, x=h):
                me.take(x_hi_ready)
                for c in (2 * j, 2 * j + 1):
                    ins = v.scalar_tensor_tensor(out=xl[:, c, :], in0=x[:, c, :], scalar=g(c), in1=xh[:, c, :].bitcast(F32),
                                                 op0=ALU.mult, op1=ALU.subtract)
                me.give(ins, x_ready)

            def named(name):
                return lambda c: vec(name, c)

            def add_feed(i, g, xh=x_hi, xl=x_lo, step=1):
                for j in range(4):
                    for k in range(step - 1):
                        split(i + step * j + k + 2)
                    add_h(i + step * j + step - 1, j)
                    me.settle()
                    if g is not None:
                        feed(j, g, xh, xl)
                    split(i + step * j + step + 1)

            def root(width=S):
                me.take(rms_ready)
                me.give(v.reciprocal(rstd[:, 0:width], rstd[:, 0:width]), rstd_ready)
                me.settle()

            def by_token(dst, i, chunks=2, r=0):
                scale = rstd[:, r:r + S].rearrange("p (o s) -> p o s", o=1).to_broadcast([P, chunks, S])
                me.give(v.tensor_tensor(dst, scale, psum(i)[:, 0:chunks * S].rearrange("p (c s) -> p c s", c=chunks),
                                        ALU.mult), read_out)

            def add_h(i, j):
                hh = h[:, 2 * j:2 * j + 2, :].rearrange("p c s -> p (c s)")
                me.give(v.tensor_tensor(hh, hh, psum(i), ALU.add), read_out)

            def ffn(n, g, xh=x_hi, xl=x_lo):
                i = first("up_a", n)
                centre = 1 if n < 2 else 2
                split(i + 2)
                root()
                for j in range(PAIRS):
                    ia, c, x = i + 2 * j, cv[:, j % 2, :, :], ar[:, j % 2, :, :]
                    by_token(x, ia)
                    if j:
                        split(ia + 2)
                    me.take(conv_mid)
                    taps = [k for k in range(3) if k != centre]
                    for k in taps:
                        sh = k - centre
                        o0, o1 = max(0, -sh), S - max(0, sh)
                        for t in range(2):
                            ins = v.scalar_tensor_tensor(out=c[:, t, o0:o1], in0=x[:, t, o0 + sh:o1 + sh],
                                                         scalar=vec(f"conv{k}.{n}", 2 * j + t), in1=c[:, t, o0:o1],
                                                         op0=ALU.mult, op1=ALU.add)
                        me.give(ins, None if k == taps[0] else conv_done)
                        if k == taps[0]:
                            me.settle()
                    me.take(act_scaled)
                    cf = c.rearrange("p c s -> p (c s)")
                    me.give(v.tensor_tensor(cf, cf, psum(ia + 1), ALU.mult), read_out)
                    split(ia + 3)
                add_feed(first("down", n), g, xh, xl, step=3)

            def soft_a(u):
                s, q = divmod(u, ST)
                if u:
                    me.take(tr_ready)
                me.take(scores_ready)
                v.tensor_tensor(lg[:, 0:BANK], A[:, 0:BANK], bm[:, q, s, 0:BANK], ALU.add)
                me.give(v.tensor_tensor(lg[:, BANK:3 * S], A[:, BANK:BANK + S], bm[:, q, s, BANK:3 * S], ALU.add),
                        scores_read)
                me.settle()
                me.give(v.tensor_reduce(mx[:, 0:1], lg[:, :], AX.X, ALU.max))
                me.settle()
                me.give(v.tensor_scalar(nm[:, 0:1], mx[:, 0:1], -1.0, None, ALU.mult), lg_ready)

            def soft_b():
                me.take(exp_ready)
                me.give(v.reciprocal(rs[:, 0:1], sums[:, 0:1]))
                me.settle()
                me.give(v.tensor_scalar(lg[:, :], lg[:, :], rs[:, 0:1], None, ALU.mult), prob_ready)

            def sigmoid(g, signal=None):
                me.take(gate_exp)
                me.give(v.tensor_scalar(g, g, 1.0, None, ALU.add), signal)
                me.settle()
                me.give(v.reciprocal(g, g))

            def gate_of(j):
                return (gate_p if j < 4 else gate_a)[:, 2 * (j % 4):2 * (j % 4) + 2, :]

            def gate_scaled(i, j):
                me.give(v.tensor_tensor(gate_of(j), rstd[:, 0:S].rearrange("p (o s) -> p o s", o=1).to_broadcast([P, 2, S]),
                                        psum(i).rearrange("p (c s) -> p c s", c=2), ALU.mult), read_out)

            def mixer(layer):
                i = first("v", layer)
                split(i + 2)
                root(S + 2)
                for j in range(18):
                    k = 2 * (j % 6)
                    if layer == 0 and j == 6:
                        v.wait_ge(bb_ready, 1)
                    if j < 6:
                        p = psum(i + j)
                        for t in range(ST):
                            ins = v.tensor_scalar(va[:, t, j * S:(j + 1) * S], p[:, t * S:(t + 1) * S],
                                                  rstd[:, S + t:S + t + 1], None, ALU.mult)
                        me.give(ins, read_out)
                    elif j < 12:
                        scale = rstd[:, 0:S].rearrange("p (o s) -> p o s", o=1).to_broadcast([P, 2, S])
                        me.give(v.scalar_tensor_tensor(out=qt[:, k:k + 2, :], in0=psum(i + j).rearrange("p (c s) -> p c s", c=2),
                                                       scalar=DH ** -0.5, in1=scale, op0=ALU.mult, op1=ALU.mult),
                                read_out)
                    else:
                        by_token(kt[:, k:k + 2, :], i + j)
                    if j:
                        split(i + j + 2)
                    if layer == 0:
                        setup.get(j, lambda: None)()
                me.settle()
                me.give(v.tensor_copy(small[:, 41:42], small[:, 0:1]), qkv_ready)
                me.take(u_zero)
                if layer == 0:
                    v.wait_ge(bm_in, 16 * ST * SLOTS)

                def gate_done(j):
                    sigmoid(gate_of(j))

                for j in range(10):
                    ib = i + 18 + j
                    if j < 4:
                        by_token(ub[:, 2 * j:2 * j + 2, PADT:PADT + S], ib)
                    else:
                        by_token(gate_of(j - 4), ib)
                        me.settle()
                        me.give(v.tensor_copy(small[:, 42:43], small[:, 0:1]), gate_in)
                    split(ib + 2)
                    if j >= 5:
                        gate_done(j - 5)
                    if j < 8:
                        soft_a(j)
                    if 2 <= j:
                        s, q = divmod(j - 2, ST)
                        me.take(pv_hi)
                        me.give(v.tensor_tensor(ao_l[:, s, q * P:(q + 1) * P], G[:, 3 * BANK:3 * BANK + P],
                                                ao_h[:, s, q * P:(q + 1) * P].bitcast(F32), ALU.subtract), pv_read)
                    if j < 8:
                        soft_b()
                    if j == 8:
                        me.take(tr_ready)
                        lo(pl[:, :, :], tmp[:, :, :], ph[:, :, :])
                gate_done(5)
                ip = first("pool", layer)
                v.wait_ge(mm_done, ip + 1)
                for k in range(DC):
                    if k % 4 == 0:
                        me.take(x_hi_ready)
                    ins = v.scalar_tensor_tensor(out=po_l[:, k, :], in0=A[:, k * S:(k + 1) * S],
                                                 scalar=vec(f"pool_scale.{layer}", k), in1=po_h[:, k, :].bitcast(F32),
                                                 op0=ALU.mult, op1=ALU.subtract)
                    if k % 4 == 3:
                        me.give(ins, x_ready)
                split(ip + 2)
                for j in range(2):
                    by_token(gate_of(6 + j), ip + 1 + j)
                    me.settle()
                    me.give(v.tensor_copy(small[:, 42:43], small[:, 0:1]), gate_in)
                    split(ip + 3 + j)
                    gate_done(6 + j)
                me.settle()
                for j in range(2):
                    g = gate_a[:, 4 * j:4 * j + 4, :].rearrange("p c s -> p (c s)")
                    me.give(v.tensor_tensor(g, g, psum(first("wb", layer) + j), ALU.mult), read_out)
                    split(first("wb", layer) + j + 2)
                ia = first("wa", layer)
                for j in range(4):
                    g = gate_p[:, 2 * j:2 * j + 2, :].rearrange("p c s -> p (c s)")
                    me.give(v.tensor_tensor(g, g, psum(ia + j), ALU.mult), read_out)
                    me.settle()
                    me.give(v.tensor_tensor(tmp[:, 2 * j:2 * j + 2, :], gate_a[:, 2 * j:2 * j + 2, :],
                                            gate_p[:, 2 * j:2 * j + 2, :], ALU.add), x_f32)
                    lo(pl[:, 2 * j:2 * j + 2, :], tmp[:, 2 * j:2 * j + 2, :], ph[:, 2 * j:2 * j + 2, :])
                    split(ia + j + 2)
                add_feed(first("wo", layer), named(f"norm2.{layer}"))

            v.memset(ones[:, :], 1.0)
            v.memset(small[:, 0:1], EPS)
            me.give(v.memset(small[:, 1:4], 0.0), ones_ready)
            v.wait_ge(par_in, 16)
            v.wait_ge(x_in, 16)
            for j in range(4):
                feed(j, named("norm1.0"))
                if j in (0, 3):
                    split(0 if j == 0 else 1)
            theta, red = ang[5], ang[6]

            def setup_bounds():
                v.wait_ge(relb_in, 16)
                me.give(v.memset(relb[BUCKETS:BUCKETS + 1, :], 1.0))
                me.settle()
                me.give(v.tensor_copy(relw[:, :, :], relb[:, :].rearrange("p (h o) -> p h o", o=1)
                                      .to_broadcast([BUCKETS + 1, HEADS, P])), relb_ready)
                v.tensor_tensor(gg[:, :], par[:, COL["norm_f"]:COL["norm_f"] + 8], par[:, COL["mix.0"]:COL["mix.0"] + 8],
                                ALU.mult)
                l0, l1 = par[:, COL["lb0"]:COL["lb0"] + 4], par[:, COL["lb1"]:COL["lb1"] + 4]
                me.give(v.tensor_tensor(lbt[:, 8:12], l0, l1, ALU.max))
                me.settle()
                v.tensor_tensor(lbt[:, 0:4], l0, lbt[:, 8:12], ALU.subtract)
                v.tensor_scalar(nbglu, par[:, COL["b_glu"]:COL["b_glu"] + 4], -1.0, None, ALU.mult)
                me.give(v.tensor_tensor(lbt[:, 4:8], l1, lbt[:, 8:12], ALU.subtract), lbd_ready)

            def setup_angles():
                v.wait_ge(pos_in, 16)
                v.wait_ge(cst_in, 16)
                me.give(v.tensor_copy(theta[:, NS5:NANG], pos_i[:, :]))
                me.settle()
                me.give(v.tensor_scalar(theta[:, NS5:NANG], theta[:, NS5:NANG], freq, None, ALU.mult))
                me.settle()
                me.take(th_ready)
                k = ang[9]
                me.give(v.tensor_scalar(k[:, :], theta[:, :], 1.0 / TWO_PI, MAGIC, ALU.mult, ALU.add))
                me.settle()
                me.give(v.tensor_scalar(k[:, :], k[:, :], MAGIC, None, ALU.subtract))
                me.settle()
                src = theta
                for c in (C1, C2, C3):
                    me.give(v.scalar_tensor_tensor(out=red[:, :], in0=k[:, :], scalar=-c, in1=src[:, :], op0=ALU.mult,
                                                   op1=ALU.add))
                    me.settle()
                    src = red
                lim = 3.1415925
                me.give(v.tensor_scalar(ang[7][:, :], red[:, :], lim, -lim, ALU.min, ALU.max))
                me.settle()
                me.give(v.scalar_tensor_tensor(out=ang[8][:, :], in0=ang[7][:, :], scalar=-1.0, in1=ang[7][:, :],
                                               op0=ALU.mult, op1=ALU.max))
                me.settle()
                me.give(v.tensor_scalar(ang[8][:, :], ang[8][:, :], -1.0, float(np.pi / 2), ALU.mult, ALU.add), red_ready)

            def setup_kept():
                me.take(trig_ready)
                v.tensor_copy(sin_r[:, 0, :], ang[7][:, NS5:NANG])
                me.give(v.tensor_copy(cos_r[:, 0, :], ang[8][:, NS5:NANG]), rope_kept)
                me.take(lbe_ready)
                me.give(v.tensor_tensor(lbt[:, 8:12], lbt[:, 0:4], lbt[:, 4:8], ALU.add))
                me.settle()
                me.give(v.reciprocal(lbt[:, 8:12], lbt[:, 8:12]))
                me.settle()
                v.tensor_tensor(lb, lbt[:, 0:4], lbt[:, 8:12], ALU.mult)
                me.give(v.tensor_tensor(omlb, lbt[:, 4:8], lbt[:, 8:12], ALU.mult))
                me.take(den_ready)
                me.give(v.reciprocal(s5x[0][:, :], s5x[0][:, :]), rden_ready)

            setup = {0: setup_bounds, 2: setup_angles, 3: setup_kept}
            mixer(0)
            ffn(0, named("norm1.1"))
            mixer(1)
            ffn(1, lambda c: gg[:, c:c + 1])
            i = first("ef")
            split(i + 2)
            me.take(rms_ready)
            me.give(v.reciprocal(rf[:, :], rf[:, :]))
            me.settle()
            me.give(v.tensor_tensor(rf2[:, :], rf[:, :], rf[:, :], ALU.mult))
            me.settle()
            me.take(ms2_ready)
            me.give(v.tensor_tensor(rstd[:, 0:S + 2], rf2[:, :], A[:, BANK:BANK + S + 2], ALU.mult), rf_ready)
            me.take(rms_ready)
            me.give(v.reciprocal(rstd[:, 0:S + 2], rstd[:, 0:S + 2]))
            me.settle()
            me.give(v.tensor_tensor(rstd[:, 0:S + 2], rstd[:, 0:S + 2], rf[:, :], ALU.mult), rstd_ready)
            me.settle()
            for j in range(2):
                f = fe[:, j * BANK:(j + 1) * BANK]
                by_token(f.rearrange("p (c s) -> p c s", c=2), i + j)
                me.settle()
                me.give(v.tensor_copy(small[:, 42:43], small[:, 0:1]), gate_in)
                if j:
                    split(i + 3)
                sigmoid(f)
                me.settle()
                for c in range(2):
                    fc = fe[:, j * BANK + c * S:j * BANK + (c + 1) * S]
                    ins = v.tensor_scalar(fc, fc, omlb[:, 2 * j + c:2 * j + c + 1], lb[:, 2 * j + c:2 * j + c + 1],
                                          ALU.mult, ALU.add)
                me.give(ins)
                me.settle()
                me.give(v.tensor_scalar(key[:, j * BANK:(j + 1) * BANK], f, -1.0, 1.0, ALU.mult, ALU.add),
                        f_ready if j else None)
            for c in range(DC):
                ins = v.scalar_tensor_tensor(out=h[:, c, :], in0=h[:, c, :], scalar=vec("norm_f", c), in1=rf[:, 0:S],
                                             op0=ALU.mult, op1=ALU.mult)
            me.give(ins)
            by_token(qb[:, 0:BANK].rearrange("p (c s) -> p c s", c=2), i + 2)
            split(i + 4)
            me.take(ln_ready)
            me.take(smask_ready)
            me.give(v.tensor_tensor_scan(cum[:, :], smask[:, :], fe[:, :], 0.0, ALU.mult, ALU.add))
            me.settle()
            c16 = cum.rearrange("p (c s) -> p c s", s=CH)
            last = c16[:, :, CH - 1:CH].to_broadcast([P, 16, CH])
            me.give(v.tensor_tensor(dd.rearrange("p (c s) -> p c s", s=CH), last, c16, ALU.subtract), cum_ready)
            by_token(qb[:, BANK:2 * BANK].rearrange("p (c s) -> p c s", c=2), i + 3)
            split(i + 5)
            me.settle()
            me.take(eb_ready)
            v.tensor_tensor(qb[:, :], qb[:, :], eb[:, :], ALU.mult)
            v.tensor_tensor(enb[:, :], enb[:, :], key[:, :], ALU.mult)
            me.give(v.tensor_tensor(dd[:, :], dd[:, :], key[:, :], ALU.mult), qd_ready)
            v24 = v2.rearrange("p (t n) -> p t n", t=ST)
            for j in range(2):
                p = psum(i + 4 + j)
                for t in range(ST):
                    ins = v.tensor_scalar(v24[:, t, j * S:(j + 1) * S], p[:, t * S:(t + 1) * S], rstd[:, S + t:S + t + 1],
                                          None, ALU.mult)
                me.give(ins, read_out)
                split(i + 6 + j)
            for j in range(2):
                g = sgate[:, j * BANK:(j + 1) * BANK]
                f = fe[:, j * BANK:(j + 1) * BANK]
                by_token(f.rearrange("p (c s) -> p c s", c=2), i + 6 + j)
                me.settle()
                me.give(v.tensor_copy(small[:, 42:43], small[:, 0:1]), gate_in)
                split(i + 8 + j)
                me.take(gate_exp)
                me.give(v.tensor_scalar(g, g, 1.0, None, ALU.add))
                me.settle()
                me.give(v.reciprocal(g, g))
                me.settle()
                me.give(v.tensor_tensor(g, g, f, ALU.mult))
            for j in range(2):
                by_token(uu[:, j * BANK:(j + 1) * BANK].rearrange("p (c s) -> p c s", c=2), i + 8 + j)
                split(i + 10 + j)
            me.take(att_ready)
            me.take(am_zero)
            att = A[:, 0:BANK].rearrange("p (k n) -> p k n", n=CH)
            for r in (0, CH):
                ins = v.copy_predicated(am[r:r + CH, :, r:r + CH],
                                        ccausal[r:r + CH, :].rearrange("p (o n) -> p o n", o=1).to_broadcast([CH, 8, CH]),
                                        att[r:r + CH, :, :])
            me.give(ins, am_ready)
            for n in range(3):
                me.take(ds_ready)
                if n == 0:
                    me.give(v.tensor_copy(st[:, 0, :, :].rearrange("p c n -> p (c n)"), A[:, 3 * BANK:4 * BANK]), st_ready)
                else:
                    me.settle()
                    for c in range(4):
                        e = c * S + n * CH + CH - 1
                        ins = v.scalar_tensor_tensor(out=st[:, n, c, :], in0=st[:, n - 1, c, :], scalar=eb[:, e:e + 1],
                                                     in1=A[:, 3 * BANK + c * P:3 * BANK + (c + 1) * P],
                                                     op0=ALU.mult, op1=ALU.add)
                    me.give(ins, st_ready)
            me.take(rms_ready)
            me.give(v.reciprocal(fe[:, :], fe[:, :]))
            me.settle()
            for c in range(4):
                cs = slice(c * S, (c + 1) * S)
                ins = v.scalar_tensor_tensor(out=key[:, cs], in0=A[:, BANK + c * S:BANK + (c + 1) * S],
                                             scalar=vec("hgrn_g", c), in1=fe[:, cs], op0=ALU.mult, op1=ALU.mult)
            me.give(ins)
            me.settle()
            me.give(v.tensor_tensor(tmp[:, 0:4, :].rearrange("p c s -> p (c s)"), key[:, :], sgate[:, :], ALU.mult),
                    x_f32)
            lo(x_lo[:, 0:4, :], tmp[:, 0:4, :], x_hi[:, 0:4, :])
            me.settle()
            me.give(v.tensor_copy(small[:, 44:45], small[:, 0:1]), s5_free)
            me.take(e_ready)
            t1, t2, t3, t4, zr, zi = t_s5[0:6]

            def s5_states(g):
                gs = slice(4 * g, 4 * g + 4)
                ecg, esg = ec[:, gs, :], es[:, gs, :]
                bu = A[:, :].rearrange("p (k n) -> p k n", k=4)
                re, im = bu[:, :, 0:S], bu[:, :, S:2 * S]
                u1, u2, u3, u4 = (t.rearrange("p (k n) -> p k n", k=4) for t in (t1, t2, t3, t4))
                me.take(bu_ready)
                v.tensor_tensor(u1, ecg, re, ALU.mult)
                v.tensor_tensor(u2, esg, im, ALU.mult)
                v.tensor_tensor(u3, ecg, im, ALU.mult)
                me.give(v.tensor_tensor(u4, esg, re, ALU.mult), bu_read)
                me.settle()
                v.tensor_tensor(t1[:, :], t1[:, :], t2[:, :], ALU.add)
                me.give(v.tensor_tensor(t3[:, :], t3[:, :], t4[:, :], ALU.subtract))
                me.settle()
                if g:
                    me.take(z_read)
                for k in range(4):
                    m = s5_st[:, 0, 4 * g + k:4 * g + k + 1].to_broadcast([P, S])
                    ks = slice(k * S, (k + 1) * S)
                    v.tensor_tensor_scan(zr[:, ks], m, t1[:, ks], 0.0, ALU.mult, ALU.add)
                    ins = v.tensor_tensor_scan(zi[:, ks], m, t3[:, ks], 0.0, ALU.mult, ALU.add)
                me.give(ins, z_ready)
                me.settle()

            def s5_y(g):
                me.take(ys_ready)
                me.give(v.scalar_tensor_tensor(out=tmp[:, 4 + g, :], in0=uu[:, g * S:(g + 1) * S], scalar=vec("s5_d", g),
                                               in1=G[:, g * BANK:g * BANK + S], op0=ALU.mult, op1=ALU.add), yd_ready)

            for g in range(4):
                s5_states(g)
                if g:
                    s5_y(g - 1)
            s5_y(3)
            me.take(zg_ready, 4)
            lo(x_lo[:, 4:8, :], tmp[:, 4:8, :], x_hi[:, 4:8, :])
            ig = first("glu")
            sigmoid(t1[:, :], read_out)
            me.settle()
            z = tmp[:, 4:8, :].rearrange("p c s -> p (c s)")
            me.give(v.tensor_tensor(z, z, t1[:, :], ALU.mult), x_f32)
            split(ig + 2)
            lo(x_lo[:, 4:8, :], tmp[:, 4:8, :], x_hi[:, 4:8, :])
            add_feed(first("eo"), named("ffn.0"), xb_hi, xb_lo)
            ffn(2, named("mix.1"))
            i = first("mp")
            split(i + 2)
            root()
            for j in range(3):
                by_token(c6[:, 2 * j:2 * j + 2, :], i + j)
                if j:
                    split(i + j + 2)
                me.take(x_hi_ready)
                for c in range(2 * j, min(2 * j + 2, 5)):
                    ins = v.scalar_tensor_tensor(out=xb_lo[:, c, :], in0=c6[:, c, :],
                                                 scalar=vec("q_g", c) if c < 3 else vec("kv_g", c - 3),
                                                 in1=xb_hi[:, c, :].bitcast(F32), op0=ALU.mult, op1=ALU.subtract)
                me.give(ins, x_ready)
            i = first("uq")
            split(i + 2)
            root(2 * S + 2)
            for j in range(4):
                p = psum(i + j)
                me.give(v.tensor_tensor(qn[:, 2 * j:2 * j + 2, :],
                                        rstd[:, 0:S].rearrange("p (o s) -> p o s", o=1).to_broadcast([P, 2, S]),
                                        p[:, 0:2 * S].rearrange("p (c s) -> p c s", c=2), ALU.mult))
                me.give(v.tensor_tensor(rx[:, j, :], rstd[:, 0:S], p[:, 2 * S:3 * S], ALU.mult), read_out)
                if j:
                    split(i + j + 2)
            i = first("ukv")
            for j in range(2):
                p = psum(i + j)
                me.give(v.tensor_tensor(kn[:, 4 * j:4 * j + 4, :],
                                        rstd[:, S:2 * S].rearrange("p (o s) -> p o s", o=1).to_broadcast([P, 4, S]),
                                        p[:, 0:2 * BANK].rearrange("p (c s) -> p c s", c=4), ALU.mult))
                for t in range(ST):
                    ins = v.tensor_scalar(v3[:, t, j * 512:(j + 1) * 512], p[:, (2 + t) * BANK:(3 + t) * BANK],
                                          rstd[:, 2 * S + t:2 * S + t + 1], None, ALU.mult)
                me.give(ins, read_out)
                split(i + j + 2)
            me.settle()
            me.give(v.tensor_copy(small[:, 45:46], small[:, 0:1]), rx_ready)
            cb = cos_r[:, :, :].to_broadcast([P, 4, S])
            sb_ = sin_r[:, :, :].to_broadcast([P, 4, S])
            v.tensor_tensor(tmp[:, 0:4, :], rx[:, :, :], cb, ALU.mult)
            v.tensor_tensor(tmp[:, 4, :], c6[:, 5, :], cos_r[:, 0, :], ALU.mult)
            me.take(rot_ready)
            v.tensor_tensor(qr[:, :, :], sb_, A[:, 0:2 * BANK].rearrange("p (c s) -> p c s", c=4), ALU.mult)
            me.give(v.tensor_tensor(kr[:, 0, :], sin_r[:, 0, :], A[:, 2 * BANK:2 * BANK + S], ALU.mult))
            me.settle()
            v.tensor_tensor(qr[:, :, :], qr[:, :, :], tmp[:, 0:4, :], ALU.add)
            me.give(v.tensor_tensor(kr[:, 0, :], kr[:, 0, :], tmp[:, 4, :], ALU.add), rope_ready)
            scale = 192 ** -0.5
            cz = causal.rearrange("p (o n) -> p o n", o=1).to_broadcast([P, 2, P])
            for j in range(MH + 2):
                if j < MH:
                    if j >= 2:
                        me.take(tr_ready)
                    me.take(scores_ready)
                    l = lm[:, j % 2, :, :]
                    ps = A[:, (j % 2) * BANK:(j % 2) * BANK + 3 * P].rearrange("p (k n) -> p k n", k=3)
                    v.tensor_scalar(l[:, 1, :], ps[:, 1, :], scale, None, ALU.mult)
                    me.give(v.scalar_tensor_tensor(out=l[:, 0:3:2, :], in0=ps[:, 0:3:2, :], scalar=scale, in1=cz,
                                                   op0=ALU.mult, op1=ALU.add), scores_read)
                    me.settle()
                    lf = l.rearrange("p k n -> p (k n)")
                    v.tensor_reduce(mx[:, 0:1], lf[:, 0:P], AX.X, ALU.max)
                    me.give(v.tensor_reduce(mx[:, 1:2], lf[:, P:3 * P], AX.X, ALU.max))
                    me.settle()
                    me.give(v.tensor_scalar(nm[:, :], mx[:, :], -1.0, None, ALU.mult), lg_ready)
                if j >= 2:
                    me.take(pv_hi)
                    me.give(v.tensor_tensor(x_lo[:, j - 2, :], A[:, 3 * BANK:3 * BANK + S],
                                            x_hi[:, j - 2, :].bitcast(F32), ALU.subtract), pv_read)
                if j < MH:
                    me.take(exp_ready)
                    me.give(v.reciprocal(rs[:, :], sums[:, :]))
                    me.settle()
                    v.tensor_scalar(lf[:, 0:P], lf[:, 0:P], rs[:, 0:1], None, ALU.mult)
                    me.give(v.tensor_scalar(lf[:, P:3 * P], lf[:, P:3 * P], rs[:, 1:2], None, ALU.mult), prob_ready)
            add_feed(first("mo"), named("ffn.1"), xb_hi, xb_lo)
            ffn(3, None)
            root()
            for c in range(DC):
                ins = v.scalar_tensor_tensor(out=tmp[:, c, :], in0=h[:, c, :], scalar=vec("final", c), in1=rstd[:, 0:S],
                                             op0=ALU.mult, op1=ALU.mult)
            me.give(ins, final_ready)

        @block.gpsimd
        def _(g):
            me = Side(g, pool_own)

            def tt(out, x, y, op, s=None):
                me.give(g.tensor_tensor(out, x, y, op), s)
                me.settle()

            W = slice(0, NS5)
            ar, ai, dt, mag, theta = (ang[j][:, W] for j in (0, 1, 3, 4, 5))
            g.wait_ge(s5_in, 48)
            me.take(dt_ready)
            tt(mag, ar, dt, ALU.mult, ndt_ready)
            tt(theta, ai, dt, ALU.mult, th_ready)
            den, xr, cr, ci, u1, u2 = (s5x[j][:, :] for j in range(6))
            tt(den, ar, ar, ALU.mult)
            tt(u1, ai, ai, ALU.mult)
            tt(den, den, u1, ALU.add, den_ready)
            me.take(trig_ready)
            g.wait_ge(mag_ready, 1)
            sin, cos = ang[7][:, W], ang[8][:, W]
            xi = u2
            for k, x in enumerate((ang[4], ang[8], ang[7])):
                me.give(g.tensor_copy(s5_st[:, k, :], x[:, 4 * P:NS5]))
            tt(xr, mag, cos, ALU.mult)
            tt(xi, mag, sin, ALU.mult)
            me.give(g.tensor_scalar(xr, xr, -1.0, None, ALU.add))
            me.settle()
            tt(cr, xr, ar, ALU.mult)
            tt(u1, xi, ai, ALU.mult)
            tt(cr, cr, u1, ALU.add)
            tt(ci, xi, ar, ALU.mult)
            tt(u1, xr, ai, ALU.mult)
            tt(ci, ci, u1, ALU.subtract)
            me.take(rden_ready)
            tt(cr, cr, den, ALU.mult)
            tt(ci, ci, den, ALU.mult)
            g.wait_ge(s5b_in, 16)
            cr, ci, u1 = cr[:, 0:4 * P], ci[:, 0:4 * P], u1[:, 0:4 * P]
            br, bi = s5b[:, 0, :], s5b[:, 1, :]
            bbr, bbi = (bb[:, j, :, :].rearrange("p c n -> p (c n)") for j in range(2))
            tt(bbr, cr, br, ALU.mult)
            tt(u1, ci, bi, ALU.mult)
            tt(bbr, bbr, u1, ALU.subtract)
            tt(bbi, cr, bi, ALU.mult)
            tt(u1, ci, br, ALU.mult)
            g.wait_ge(rope_kept, 1)
            tt(bbi, bbi, u1, ALU.add, bb_ready)

            def ffn(n):
                i = first("up_a", n)
                scale = rstd[:, 0:S].rearrange("p (o s) -> p o s", o=1).to_broadcast([P, 2, S])
                for j in range(PAIRS):
                    c = cv[:, j % 2, :, :]
                    me.take(act_ready)
                    me.give(g.tensor_tensor(c, c, scale, ALU.mult), act_scaled)
                    g.wait_ge(read_out, PLAN[i + 2 * j + 1].out)
                    me.take(y_hi)
                    me.give(g.tensor_tensor(yl[:, 2 * j:2 * j + 2, :], c, yh[:, 2 * j:2 * j + 2, :].bitcast(F32),
                                            ALU.subtract), y_ready)

            for layer in range(2):
                if layer:
                    ffn(0)
                    g.wait_ge(read_out, PLAN[first("down", 0) + 11].out)
                else:
                    g.wait_ge(tab_ready, GROUPS)
                me.give(g.memset(ub[:, :, :], 0.0), u_zero)
                for j in range(4):
                    g.wait_ge(read_out, PLAN[first("u", layer) + j].out)
                    src, length = ub[:, 2 * j:2 * j + 2, :], S + 2 * PADT
                    for k in range(j + 1):
                        step = 1 << k
                        length -= step
                        dst = pool_w[k % 2]
                        me.give(g.tensor_tensor(dst[:, :, 0:length], src[:, :, 0:length], src[:, :, step:step + length],
                                                ALU.add))
                        me.settle()
                        src = dst
                    o = PADT - (1 << j)
                    if j == 0:
                        g.wait_ge(mm_done, first("v", layer) + 2)
                    for c in range(2):
                        me.give(g.tensor_tensor(tmp[:, 2 * j + c, :], src[:, c, o:o + S], inv_count(j), ALU.mult))
                    me.settle()
                    me.give(g.tensor_tensor(tmp[:, 2 * j:2 * j + 2, :], tmp[:, 2 * j:2 * j + 2, :],
                                            ub[:, 2 * j:2 * j + 2, PADT:PADT + S], ALU.subtract), pooled)
            ffn(1)
            g.memset(ec[:, :, 0:1], 1.0)
            g.memset(es[:, :, 0:1], 0.0)
            g.tensor_copy(ec[:, :, 1:2], s5_st[:, 1, :].rearrange("p (c o) -> p c o", o=1))
            me.give(g.tensor_copy(es[:, :, 1:2], s5_st[:, 2, :].rearrange("p (c o) -> p c o", o=1)))
            me.settle()
            w = 1
            while w < S:
                n = min(w, S - 1 - w)
                if n:
                    dc, ds = ec[:, :, w + 1:w + 1 + n], es[:, :, w + 1:w + 1 + n]
                    sc, ss = ec[:, :, 1:1 + n], es[:, :, 1:1 + n]
                    ew = ec[:, :, w:w + 1].to_broadcast([P, SC, n])
                    fw = es[:, :, w:w + 1].to_broadcast([P, SC, n])
                    sx = etmp[:, :, 0:n]
                    tt(dc, sc, ew, ALU.mult)
                    tt(sx, ss, fw, ALU.mult)
                    tt(dc, dc, sx, ALU.subtract)
                    tt(ds, ss, ew, ALU.mult)
                    tt(sx, sc, fw, ALU.mult)
                    tt(ds, ds, sx, ALU.add, e_ready if w + n >= S - 1 else None)
                w *= 2
            g.wait_ge(read_out, PLAN[first("down", 1) + 11].out)
            me.give(g.memset(smask[:, :], 1.0))
            me.settle()
            me.give(g.memset(smask.rearrange("p (c s) -> p c s", s=CH)[:, :, 0:1], 0.0), smask_ready)
            g.wait_ge(ms2_ready, 1)
            me.give(g.memset(am[:, :, :], 0.0), am_zero)
            g.wait_ge(cc_in, 16)
            me.give(g.tensor_scalar(cc[:, 1, :, :], cc[:, 1, :, :], -1.0, None, ALU.mult), cc_ready)
            zr, zi, u1, u2, u3, u4 = (t_s5[j] for j in (4, 5, 6, 7, 8, 9))
            for k in range(4):
                gs = slice(4 * k, 4 * k + 4)
                ecg = ec[:, gs, :].rearrange("p c s -> p (c s)")
                esg = es[:, gs, :].rearrange("p c s -> p (c s)")
                me.take(z_ready)
                if k:
                    me.take(ys_ready)
                g.tensor_tensor(u1[:, :], zr[:, :], ecg, ALU.mult)
                g.tensor_tensor(u2[:, :], zi[:, :], esg, ALU.mult)
                g.tensor_tensor(u3[:, :], zr[:, :], esg, ALU.mult)
                me.give(g.tensor_tensor(u4[:, :], zi[:, :], ecg, ALU.mult), z_read)
                me.settle()
                g.tensor_tensor(u1[:, :], u1[:, :], u2[:, :], ALU.subtract)
                me.give(g.tensor_tensor(u3[:, :], u3[:, :], u4[:, :], ALU.add), s_ready)
                me.settle()
            ffn(2)
            ffn(3)


def _buckets(rel):
    n = -rel
    half = BUCKETS // 2
    ret = (n < 0).astype(np.int32) * half
    n = np.abs(n)
    exact = half // 2
    large = exact + (np.log(np.maximum(n, 1) / exact) / np.log(MAX_DISTANCE / exact) * (half - exact)).astype(np.int32)
    return (ret + np.where(n < exact, n, np.minimum(large, half - 1))).astype(np.int32)


def _constants():
    p = np.arange(P)
    rotate = np.zeros((P, P), np.float32)
    for m in range(P):
        if m % 64 < 32:
            rotate[m + 32, m] = -1.0
        else:
            rotate[m - 32, m] = 1.0
    inv = np.zeros((4, S), np.float32)
    i = np.arange(S)
    for g in range(4):
        w = 2 << g
        inv[g] = np.float32(1) / (np.clip(i - w // 2 + w, 0, S) - np.clip(i - w // 2, 0, S)).astype(np.float32)
    freq = (np.float32(10000.0) ** (-np.arange(0, 64, 2, dtype=np.float32) / np.float32(64))).astype(np.float32)
    parts = {
        "ident": np.eye(P, dtype=np.float32), "rotate": rotate,
        "causal": np.where(p[None, :] > p[:, None], NEG, 0.0).astype(np.float32),
        "inv_count": np.broadcast_to(inv.reshape(1, -1), (P, 4 * S)),
        "freq": freq[p % 32][:, None],
        "chunk_causal": ((p % CH)[:, None] <= np.arange(CH)[None, :]).astype(np.float32),
    }
    consts = np.concatenate([parts[n] for n, _ in CONSTS], axis=1).astype(np.float32)
    hot = np.zeros((BUCKETS + 1, GROUPS, TAB + 1), np.float32)
    rel = np.arange(TAB) - (S - 1)
    for g, d in enumerate(DILATIONS):
        ok = (np.abs(rel) <= HALF * d) & (rel % d == 0)
        hot[_buckets(rel)[ok], g, np.nonzero(ok)[0]] = 1.0
        hot[BUCKETS, g, np.nonzero(~ok)[0]] = NEG
        hot[BUCKETS, g, TAB] = NEG
    return np.ascontiguousarray(consts), hot.reshape(BUCKETS + 1, -1)


def _weights(a):
    out = []
    seen = {}
    w_in, e_in = a["w_in"], a["even_w_in_2"][0]
    mla = a["odd_w_in_2"][0]
    mla = np.concatenate([mla[:, :640], mla[:, 640:], mla[:, 640:]], axis=1)
    uq = a["mla_w_uq_2"][0].reshape(384, MH, 192)
    ukv = a["mla_w_ukv_2"][0].reshape(256, MH, 256)
    base = {"u": 0, "q": 1024, "k": 2560, "v": 4096, "g": 5632}
    even = {"ef": 512, "eq": 0, "ei": 1024, "eg": 1536, "eu": 2048}
    for b in PLAN:
        j = seen.get((b.kind, b.n), 0)
        seen[(b.kind, b.n)] = j + 1
        n, cols = b.n, slice(j * b.ncol, (j + 1) * b.ncol)
        if b.kind in base:
            w = w_in[n][:, base[b.kind] + j * 256:base[b.kind] + (j + 1) * 256]
        elif b.kind == "pool":
            w = a["w_pool"][n].reshape(D, 256)
        elif b.kind == "wa":
            w = a["w_a"][n][:, cols]
        elif b.kind == "wb":
            w = a["w_b"][n][:, cols]
        elif b.kind == "wo":
            w = a["w_o"][n][:, cols]
        elif b.kind in even:
            w = e_in[:, even[b.kind] + j * 256:even[b.kind] + (j + 1) * 256]
        elif b.kind == "glu":
            w = a["s5_w_glu_2"][0]
        elif b.kind == "eo":
            w = a["even_w_out_2"][0][:, cols]
        elif b.kind == "mp":
            w = mla[:, cols]
        elif b.kind == "uq":
            two = uq[:, 2 * j:2 * j + 2]
            w = np.concatenate([two[:, 0, :128], two[:, 1, :128], two[:, 0, 128:], two[:, 1, 128:]], axis=1)
        elif b.kind == "ukv":
            four = ukv[:, 4 * j:4 * j + 4]
            w = np.concatenate([four[:, :, :128].reshape(256, 512), four[:, :, 128:].reshape(256, 512)], axis=1)
        elif b.kind == "mo":
            w = a["odd_w_out_2"][0][:, cols]
        elif b.kind in ("up_a", "up_g"):
            up = a["w_up"][n] if n < 2 else a["ffn_w_in_2"][n - 2]
            c0 = j * 256 + (FF if b.kind == "up_g" else 0)
            w = up[:, c0:c0 + 256]
        else:
            down = a["w_down"][n] if n < 2 else a["ffn_w_out_2"][n - 2]
            r0 = (j % 3) * 1024
            w = down[r0:r0 + b.kc * P, (j // 3) * 256:(j // 3 + 1) * 256]
        assert w.shape == (b.kc * P, b.ncol), (b.kind, w.shape)
        out.append(np.ascontiguousarray(w.reshape(b.kc, P, b.ncol).transpose(1, 0, 2)).reshape(-1))
    return np.concatenate(out)


def _layouts(a):
    vectors = {"norm_f": a["norm_f"], "final": a["final_norm_g_2"], "lb0": a["hgrn_lb_logits_2"][0],
               "lb1": a["hgrn_lb_logits_2"][1], "hgrn_g": a["hgrn_norm_g_2"][0], "s5_d": a["s5_d_2"][0],
               "b_glu": a["s5_b_glu_2"][0], "q_g": a["mla_q_norm_g_2"][0], "kv_g": a["mla_kv_norm_g_2"][0]}
    for i in range(2):
        vectors |= {f"norm1.{i}": a["norm1"][i], f"norm2.{i}": a["norm2"][i], f"pool_scale.{i}": a["pool_scale"][i],
                    f"mix.{i}": a["norm_mix_g_2"][i], f"ffn.{i}": a["norm_ffn_g_2"][i],
                    f"convb.{i}": a["conv_b"][i], f"convb.{i + 2}": a["ffn_conv_b_2"][i]}
        for k in range(3):
            vectors |= {f"conv{k}.{i}": a["conv_w"][i, k], f"conv{k}.{i + 2}": a["ffn_conv_w_2"][i, k]}
    params = np.concatenate([vectors[n].reshape(-1, P).T for n, _ in VECTORS], axis=1)
    row, c4, col = np.meshgrid(np.arange(P), np.arange(4), np.arange(P), indexing="ij")
    chunk = 4 * c4 + row // 32
    group, state = 2 * chunk + col // SP_, col % SP_
    srow, sc = np.meshgrid(np.arange(P), np.arange(SC), indexing="ij")
    sgroup, sstate = 2 * sc + srow // SP_, srow % SP_
    abt = []
    for x in (a["s5_a_re_2"][0], a["s5_a_im_2"][0], np.broadcast_to(a["s5_log_dt_2"][0][:, None], (SG, SP_))):
        abt.append(np.concatenate([x[group, state].reshape(P, -1), x[sgroup, sstate]], axis=1))
    own = (row % 32) // 16 == col // SP_
    s5_b = np.zeros((P, 2, 4, P), np.float32)
    s5_c = np.zeros((P, 2, SC, 32), np.float32)
    for j, (b, c) in enumerate(((a["s5_b_re_2"][0], a["s5_c_re_2"][0]), (a["s5_b_im_2"][0], a["s5_c_im_2"][0]))):
        s5_b[:, j][own] = b[group, state, row % 16][own]
        for g in range(SG):
            r, f = SP_ * (g % 2), 16 * (g % 2)
            s5_c[r:r + SP_, j, g // 2, f:f + 16] = c[g].T
    consts, hot = _constants()
    return {
        "x": np.ascontiguousarray(a["x"][0].T), "params": np.ascontiguousarray(params), "consts": consts,
        "rel_bias": a["rel_bias"], "onehot": hot, "weights": _weights(a), "s5_abt": np.stack(abt),
        "s5_b": s5_b.reshape(P, 2, 4 * P), "s5_c": s5_c, "positions": a["positions_2"],
    }


def kernel(**inputs):
    import concourse.bacc as bacc
    from concourse.bass_utils import run_bass_kernel_spmd

    arrays = _layouts({k: np.asarray(v) for k, v in inputs.items()})
    nc = bacc.Bacc("TRN2", target_bir_lowering=False, num_devices=1)
    aps = {n: nc.dram_tensor(f"in_{n}", x.shape, mybir.dt.from_np(x.dtype), kind="ExternalInput").ap()
           for n, x in arrays.items()}
    aps["out"] = nc.dram_tensor("out_y", (D, S), F32, kind="ExternalOutput").ap()
    two_blocks_kernel(nc, aps)
    r = run_bass_kernel_spmd(nc, [{f"in_{n}": x for n, x in arrays.items()}], core_ids=[0])
    return np.ascontiguousarray(r.results[0]["out_y"].T)[None]
```

```python
from contextlib import ExitStack

import concourse.bass as bass
from concourse import mybir
import numpy as np

F32 = mybir.dt.float32
F32R = mybir.dt.float32r
I32 = mybir.dt.int32
ACT = mybir.ActivationFunctionType
ALU = mybir.AluOpType
AX = mybir.AxisListType

P = 128
S = 256
ST = S // P
D = 1024
DC = D // P
DH = 128
SLOTS = 4
GROUPS = 3
HEADS = SLOTS * GROUPS
DILATIONS = (1, 4, 16)
HALF = 64
BUCKETS, MAX_DISTANCE = 32, 1024
TAB = 2 * S - 1
FF = 2816
FC = FF // P
PAIRS = FF // 256
EPS = 1e-6
NEG = -1e30
PADT = 8
WIDE = 2048
RAW = 4
SPL = 3
BANK = 512
SG, SP_ = 32, 64
SC = SG * SP_ // P
NS5 = 4 * P + SC
NANG = NS5 + S
CH = 64
MH = 8
TWO_PI = float(2 * np.pi)
C1 = 6.28125
C2 = float(np.float32(0.0019350051879882812))
C3 = TWO_PI - C1 - C2
MAGIC = 12582912.0


class Block:

    def __init__(self, kind, n, ncol, kc, tiles, banks, start=True, stop=True):
        self.kind, self.n, self.ncol, self.kc, self.tiles, self.banks = kind, n, ncol, kc, tiles, banks
        self.start, self.stop, self.used = start, stop, kc * ncol


def ftiles(cols, kc, x0=0):
    return [(t * S, "f", [(c, x0 + c) for c in range(kc)], t * P, P, 0) for t in range(cols // P)]


def ttiles(cols, kc, c0=0, base=0):
    return [(base + t * cols, "t", [(c, c) for c in range(kc)], c0, cols, t) for t in range(ST)]


def make_plan():
    plan = []

    def ffn(n):
        for j in range(PAIRS):
            plan.append(Block("up_a", n, 256, DC, ftiles(256, DC), 1))
            plan.append(Block("up_g", n, 256, DC, ftiles(256, DC), 1))
        for j in range(4):
            for k, (c0, kc) in enumerate(((0, 8), (8, 8), (16, 6))):
                plan.append(Block("down", n, 256, kc, ftiles(256, kc, c0), 1, k == 0, k == 2))

    for layer in range(2):
        for kind in "vqkug":
            tiles = ttiles(256, DC) if kind == "v" else ftiles(256, DC)
            plan += [Block(kind, layer, 256, DC, tiles, 1) for _ in range({"v": 6, "q": 6, "k": 6, "u": 4, "g": 6}[kind])]
        pool = [((2 * g + t) * S, "f", [(2 * g + c, 2 * g + c) for c in range(2)], t * P, P, 0)
                for g in range(4) for t in range(2)]
        plan.append(Block("pool", layer, 256, DC, pool, 0))
        plan += [Block("g", layer, 256, DC, ftiles(256, DC), 1) for _ in range(2)]
        plan += [Block("wb", layer, 512, 4, ftiles(512, 4), 2) for _ in range(2)]
        plan += [Block("wa", layer, 256, DC, ftiles(256, DC), 1) for _ in range(4)]
        plan += [Block("wo", layer, 256, DC, ftiles(256, DC), 1) for _ in range(4)]
        ffn(layer)
    for kind in ("ef", "eq", "eu", "ei", "eg"):
        tiles = ttiles(256, DC) if kind == "ei" else ftiles(256, DC)
        plan += [Block(kind, 0, 256, DC, tiles, 1) for _ in range(2)]
    plan.append(Block("glu", 0, 512, 4, ftiles(512, 4, 4), 2))
    plan += [Block("eo", 0, 256, DC, ftiles(256, DC), 1) for _ in range(4)]
    ffn(2)
    plan += [Block("mp", 0, 256, DC, ftiles(256, DC), 1) for _ in range(3)]
    plan += [Block("uq", 0, 384, 3, ftiles(384, 3), 2) for _ in range(4)]
    plan += [Block("ukv", 0, 1024, 2, [(t * S, "f", [(c, 3 + c) for c in range(2)], t * P, P, 0) for t in range(4)]
                   + [(1024 + t * 512, "t", [(c, 3 + c) for c in range(2)], 512, 512, t) for t in range(ST)], 4)
             for _ in range(2)]
    plan += [Block("mo", 0, 256, DC, ftiles(256, DC), 1) for _ in range(4)]
    ffn(3)

    out, last, turn, two, bank = 0, [0] * 4, 0, 0, 0
    for b in plan:
        b.freed = 0
        if b.start and b.banks:
            if b.banks == 1:
                bank, turn = turn, (turn + 1) % 3
            elif b.banks == 2:
                bank, two, turn = two, 2 - two, 0
            else:
                bank, two, turn = 0, 0, 0
            b.freed = max(last[bank:bank + b.banks])
        b.bank = bank
        if b.stop and b.banks:
            out += 1
            b.out = out
            for k in range(bank, bank + b.banks):
                last[k] = out
    return plan


PLAN = make_plan()
OFFSETS = [0]
for _b in PLAN:
    OFFSETS.append(OFFSETS[-1] + _b.used)


def last(kind, n=0):
    return max(i for i, b in enumerate(PLAN) if b.kind == kind and b.n == n)


def first(kind, n=0):
    return next(i for i, b in enumerate(PLAN) if b.kind == kind and b.n == n)


VECTORS = ([(f"norm1.{i}", 8) for i in range(2)] + [(f"norm2.{i}", 8) for i in range(2)] + [("norm_f", 8)]
           + [(f"pool_scale.{i}", 8) for i in range(2)]
           + [(f"conv{k}.{n}", FC) for n in range(4) for k in range(3)] + [(f"convb.{n}", FC) for n in range(4)]
           + [(f"mix.{i}", 8) for i in range(2)] + [(f"ffn.{i}", 8) for i in range(2)] + [("final", 8)]
           + [("lb0", 4), ("lb1", 4), ("hgrn_g", 4), ("s5_d", 4), ("b_glu", 4), ("q_g", 3), ("kv_g", 2)])
COL, NPAR = {}, 0
for _name, _n in VECTORS:
    COL[_name] = NPAR
    NPAR += _n

CONSTS = (("ident", P), ("rotate", P), ("causal", P), ("inv_count", 4 * S), ("freq", 1), ("chunk_causal", CH))
CCOL, NCONST = {}, 0
for _name, _n in CONSTS:
    CCOL[_name] = NCONST
    NCONST += _n


class Side:

    def __init__(self, eng, own):
        self.eng, self.own, self.given, self.taken, self.last = eng, own, {}, {}, None

    def give(self, ins, sem=None):
        sem = sem or self.own
        ins.then_inc(sem, 1)
        self.given[sem.name] = self.given.get(sem.name, 0) + 1
        self.last = (sem, self.given[sem.name])
        return ins

    def take(self, sem, events=1):
        self.taken[sem.name] = self.taken.get(sem.name, 0) + events
        self.eng.wait_ge(sem, self.taken[sem.name])

    def settle(self):
        self.eng.wait_ge(*self.last)


def two_blocks_kernel(nc, a):
    ctx = ExitStack()
    with ctx:
        base = [(nc.sbuf_base + 31) // 32 * 32]

        def region(size):
            at = base[0]
            base[0] += size
            return at

        def tile(name, at, shape, dt=F32):
            return nc.alloc_sbuf_tensor_at(name, shape, dt, offset=at)

        K = 1024
        at_raw = [region(8 * K) for _ in range(RAW)]
        raw = [tile(f"raw{j}", at_raw[j], [P, WIDE]) for j in range(RAW)]
        w_hi = [tile(f"w_hi{j}", region(8 * K), [P, WIDE], F32R) for j in range(SPL)]
        w_lo = [tile(f"w_lo{j}", at_raw[j], [P, WIDE], F32R) for j in range(RAW)]
        h = tile("h", region(8 * K), [P, DC, S])
        x_hi = tile("x_hi", region(8 * K), [P, DC, S], F32R)
        x_lo = tile("x_lo", region(8 * K), [P, DC, S], F32R)
        at_tmp = region(8 * K)
        tmp = tile("tmp", at_tmp, [P, DC, S])
        r_bm, r_hid, r_gate, r_att = region(24 * K), region(45568), region(16 * K), region(14 * K)
        par = tile("par", region(NPAR * 4 + 31 & ~31), [P, NPAR])
        cst = tile("cst", region(NCONST * 4 + 31 & ~31), [P, NCONST])
        ones = tile("ones", region(512), [P, P])
        small = tile("small", region(256), [P, 64])
        rstd = tile("rstd", region(2080), [P, 2 * S + 2])
        gg = tile("gg", region(32), [P, DC])
        cos_r = tile("cos_r", region(K), [P, 1, S])
        sin_r = tile("sin_r", region(K), [P, 1, S])
        s5_st = tile("s5_st", region(256), [P, 4, SC])
        bb = tile("bb", region(4 * K), [P, 2, 4, P])
        assert base[0] <= nc.sbuf_usable_end, base[0]

        bm = tile("bm", r_bm, [P, ST, SLOTS, GROUPS * S])
        qt = tile("qt", r_hid, [P, HEADS, S])
        kt = tile("kt", r_hid + 12 * K, [P, HEADS, S])
        va = tile("va", r_hid + 24 * K, [P, ST, HEADS * DH])
        ub = tile("ub", r_hid + 36 * K, [P, DC, S + 2 * PADT])
        ph = tile("ph", r_hid, [P, DC, S], F32R)
        pl = tile("pl", r_hid + 8 * K, [P, DC, S], F32R)
        po_h = tile("po_h", r_hid + 16 * K, [P, DC, S], F32R)
        po_l = tile("po_l", r_hid + 36 * K, [P, DC, S], F32R)
        gate_p = tile("gate_p", r_gate, [P, DC, S])
        gate_a = tile("gate_a", r_gate + 8 * K, [P, DC, S])
        lg = tile("lg", r_att, [P, GROUPS * S])
        pt = tile("pt", r_att + 3 * K, [P, GROUPS * ST, P])
        ao_h = tile("ao_h", r_att + 6 * K, [P, SLOTS, S], F32R)
        ao_l = tile("ao_l", r_att + 10 * K, [P, SLOTS, S], F32R)
        yh = tile("yh", r_hid, [P, FC, S], F32R)
        yl = tile("yl", r_hid + FC * K, [P, FC, S], F32R)
        cv = tile("cv", r_att, [P, 2, 2, S])
        ar = tile("ar", r_att + 4 * K, [P, 2, 2, S])
        xb_hi = tile("xb_hi", r_gate, [P, DC, S], F32R)
        xb_lo = tile("xb_lo", r_gate + 8 * K, [P, DC, S], F32R)
        ec = tile("ec", r_bm, [P, SC, S])
        es = tile("es", r_gate, [P, SC, S])
        etmp = tile("etmp", r_bm + 16 * K, [P, SC, P])
        sq2 = tile("sq2", r_bm + 16 * K, [P, DC, S])
        rf = tile("rf", r_att, [P, S + 2])
        rf2 = tile("rf2", r_att + 1056, [P, S + 2])
        names = ("fe", "key", "qb", "cum", "dd", "eb", "enb", "v2", "sg", "mask")
        fe, key, qb, cum, dd, eb, enb, v2, sgate, smask = (
            tile(n, r_hid + 4 * K * j, [P, 4 * S]) for j, n in enumerate(names))
        uu = tile("uu", r_hid + 40 * K, [P, 4 * S])
        am = tile("am", r_bm + 16 * K, [P, 8, P])
        ket = tile("ket", r_bm + 20 * K, [P, 8, P])
        st = tile("st", r_att + 2 * K, [P, 3, 4, P])
        cc = tile("cc", r_att + 8 * K, [P, 3, SC, 32])
        t_s5 = [tile(f"t_s5_{n}", r_hid + 4 * K * names.index(n), [P, 4 * S]) for n in ("cum", "dd", "enb", "mask")]
        z_even = tile("z_even", r_hid + 4 * K * names.index("eb"), [P, 4 * S])
        z_odd = [tile(f"z_odd_{n}", r_hid + 4 * K * names.index(n), [P, 4 * S]) for n in ("v2", "qb")]
        z_second = tile("z_second", r_hid, [P, 4 * S])
        zs = [(z_even, tmp[:, 4:8, :].rearrange("p c s -> p (c s)")), z_odd, (z_even, z_second), z_odd]
        prods = [tile(f"prod{j}", at, [P, 4 * S]) for j, at in enumerate(
            (r_bm + 16 * K, r_bm + 20 * K, r_att + 2 * K, r_hid + 4 * K * names.index("key"),
             r_hid + 4 * K * names.index("sg"), at_tmp))]
        c6 = tile("c6", r_hid, [P, 6, S])
        qn = tile("qn", r_hid + 6 * K, [P, MH, S])
        rx = tile("rx", r_hid + 14 * K, [P, 4, S])
        kn = tile("kn", r_hid + 18 * K, [P, MH, S])
        v3 = tile("v3", r_hid + 26 * K, [P, ST, MH * DH])
        qr = tile("qr", r_hid + 34 * K, [P, 4, S])
        kr = tile("kr", r_hid + 38 * K, [P, 1, S])
        lm = tile("lm", r_att, [P, 2, 3, P])
        pm = tile("pm", r_att + 3 * K, [P, 3 * P])
        sqm = tile("sqm", r_att + 5 * K, [P, 5, S])
        NB = NANG * 4 + 31 & ~31
        ang = [tile(f"ang{j}", r_bm + NB * j if j < 7 else r_hid + 13 * K + NB * (j - 7), [P, NANG]) for j in range(10)]
        s5x = [tile(f"s5x{j}", r_hid + 2112 * j, [P, NS5]) for j in range(6)]
        relw = tile("relw", r_hid + 36 * K, [BUCKETS + 1, HEADS, P])
        pos_i = tile("pos_i", r_hid + 42 * K, [P, S], I32)
        tab = tile("tab", r_gate, [P, 2, SLOTS, TAB + 1])
        hot = tile("hot", r_att + 2 * K, [BUCKETS + 1, GROUPS * (TAB + 1)])
        relb = tile("relb", r_att + 8 * K, [BUCKETS + 1, HEADS])
        s5b = tile("s5b", r_att + 9 * K, [P, 2, 4 * P])
        assert 7 * NB <= 24 * K and 13 * K + 3 * NB <= 24 * K
        tab_dram = nc.dram_tensor("bias_table", (HEADS, P, TAB + 1), F32, kind="Internal").ap()

        pool_w = [tile(f"pool_w{j}", region(2176), [P, 2, S + 2 * PADT]) for j in range(2)]
        assert base[0] <= nc.sbuf_usable_end, base[0]

        G = ctx.enter_context(nc.psum_tensor("gemm", [P, 4 * BANK], F32))
        A = ctx.enter_context(nc.psum_tensor("aux", [P, 4 * BANK], F32))
        ident = cst[:, CCOL["ident"]:CCOL["ident"] + P]
        rotate = cst[:, CCOL["rotate"]:CCOL["rotate"] + P]
        causal = cst[:, CCOL["causal"]:CCOL["causal"] + P]
        freq = cst[:, CCOL["freq"]:CCOL["freq"] + 1]
        ccausal = cst[:, CCOL["chunk_causal"]:CCOL["chunk_causal"] + CH].bitcast(I32)
        eps = small[:, 0:1]
        fbase, fslope, hbglu = small[:, 4:8], small[:, 8:12], small[:, 12:16]
        lbt = small[:, 16:28]
        mx, nm, sums, rs = small[:, 28:29], small[:, 29:30], small[:, 30:31], small[:, 31:32]
        m_mx, m_nm, m_sums, m_rs = ([small[:, 48 + 4 * n + 2 * k:50 + 4 * n + 2 * k] for k in range(2)] for n in range(4))

        def vec(name, c):
            return par[:, COL[name] + c:COL[name] + c + 1]

        def inv_count(g):
            return cst[:, CCOL["inv_count"] + g * S:CCOL["inv_count"] + (g + 1) * S]

        def sem(name):
            return ctx.enter_context(nc.semaphore(name))

        x_in, par_in, cst_in = sem("x_in"), sem("par_in"), sem("cst_in")
        s5_in, s5b_in, pos_in, hot_in, cc_in = sem("s5_in"), sem("s5b_in"), sem("pos_in"), sem("hot_in"), sem("cc_in")
        relb_in, bm_in = sem("relb_in"), sem("bm_in")
        tab_out = [sem(f"tab_out{j}") for j in range(GROUPS)]
        raw_in = [sem(f"raw_in{j}") for j in range(RAW)]
        out_done = sem("out_done")
        w_hi_ready, w_lo_ready = sem("w_hi_ready"), sem("w_lo_ready")
        mm_done = sem("mm_done")
        read_out = sem("read_out")
        act_own, dve_own, pool_own = sem("act_own"), sem("dve_own"), sem("pool_own")
        ones_ready = sem("ones_ready")
        x_f32, x_hi_ready, x_ready = sem("x_f32"), sem("x_hi_ready"), sem("x_ready")
        pair_squared, sums_ready = sem("pair_squared"), sem("sums_ready")
        sq_ready, ms_ready, rms_ready = sem("sq_ready"), sem("ms_ready"), sem("rms_ready")
        relb_ready, tab_ready, tab_copied = sem("relb_ready"), sem("tab_ready"), sem("tab_copied")
        dt_ready, th_ready, mag_ready, red_ready = sem("dt_ready"), sem("th_ready"), sem("mag_ready"), sem("red_ready")
        trig_ready, den_ready, bb_ready, ndt_ready = sem("trig_ready"), sem("den_ready"), sem("bb_ready"), sem("ndt_ready")
        rope_kept = sem("rope_kept")
        qkv_ready, scores_ready, scores_read = sem("qkv_ready"), sem("scores_ready"), sem("scores_read")
        lg_ready, exp_ready, prob_ready = sem("lg_ready"), sem("exp_ready"), sem("prob_ready")
        tr_ready, pt_ready = sem("tr_ready"), sem("pt_ready")
        pv_ready, pv_hi, pv_read = sem("pv_ready"), sem("pv_hi"), sem("pv_read")
        u_zero, pooled = sem("u_zero"), sem("pooled")
        gate_ready = sem("gate_ready")
        conv_mid, conv_done, act_ready, act_scaled, y_hi, y_ready = (
            sem("conv_mid"), sem("conv_done"), sem("act_ready"), sem("act_scaled"), sem("y_hi"), sem("y_ready"))
        gate_in, rf_ready, rstd_ready, ms2_ready = sem("gate_in"), sem("rf_ready"), sem("rstd_ready"), sem("ms2_ready")
        e_ready, smask_ready, am_zero, cc_ready = sem("e_ready"), sem("smask_ready"), sem("am_zero"), sem("cc_ready")
        rden_ready, lbd_ready, lbe_ready = sem("rden_ready"), sem("lbd_ready"), sem("lbe_ready")
        f_ready, ln_ready, cum_ready, eb_ready, qd_ready = (sem("f_ready"), sem("ln_ready"), sem("cum_ready"),
                                                            sem("eb_ready"), sem("qd_ready"))
        att_ready, am_ready, ket_psum, ket_ready = sem("att_ready"), sem("am_ready"), sem("ket_psum"), sem("ket_ready")
        ds_ready, st_ready, o_ready = sem("ds_ready"), sem("st_ready"), sem("o_ready")
        bu_ready, bu_read, z_ready, z_read, s_ready, ys_ready = (sem("bu_ready"), sem("bu_read"), sem("z_ready"),
                                                                 sem("z_read"), sem("s_ready"), sem("ys_ready"))
        s_half_ready = sem("s_half_ready")
        yd_ready, zg_ready, s5_free = sem("yd_ready"), sem("zg_ready"), sem("s5_free")
        rx_ready, rot_ready, rope_ready = sem("rx_ready"), sem("rot_ready"), sem("rope_ready")
        final_ready = sem("final_ready")

        block = ctx.enter_context(nc.Block())
        N = len(PLAN)

        @block.sync
        def _(sp):
            def load(dst, src, s):
                sp.dma_start(dst, src).then_inc(s, 16)

            load(h[:, :, :], a["x"].rearrange("(c p) s -> p c s", p=P), x_in)
            load(par[:, :], a["params"], par_in)

            def weights(i):
                b = PLAN[i]
                if i >= RAW:
                    sp.wait_ge(mm_done, i - RAW + 1)
                load(raw[i % RAW][:, 0:b.used],
                     a["weights"][OFFSETS[i] * P:OFFSETS[i + 1] * P].rearrange("(p n) -> p n", p=P), raw_in[i % RAW])

            for i in range(RAW):
                weights(i)
            load(relb[0:BUCKETS, :], a["rel_bias"], relb_in)
            load(cst[:, :], a["consts"], cst_in)
            load(hot[:, :], a["onehot"], hot_in)
            for j in range(3):
                load(ang[j][:, 0:NS5], a["s5_abt"][j], s5_in)
            load(s5b[:, :, :], a["s5_b"], s5b_in)
            load(pos_i[:, :], a["positions"].to_broadcast([P, S]), pos_in)

            def store_table(g):
                sp.wait_ge(tab_copied, g + 1)
                load(tab_dram[g * SLOTS:(g + 1) * SLOTS].rearrange("h p n -> p h n"), tab[:, g % 2, :, :], tab_out[g])

            def load_bias(s):
                if s == 0:
                    for s_ in tab_out:
                        sp.wait_ge(s_, 16)
                    sp.wait_ge(bb_ready, 1)
                for q in range(ST):
                    src = bass.AP(tab_dram.tensor, s * P * (TAB + 1) + S - 1 - q * P,
                                  [[TAB, P], [SLOTS * P * (TAB + 1), GROUPS], [1, S]])
                    load(bm[:, q, s, :].rearrange("p (g n) -> p g n", g=GROUPS), src, bm_in)

            for i in range(RAW, N):
                weights(i)
                if i in (8, 10, 12):
                    store_table((i - 8) // 2)
                if 14 <= i < 14 + SLOTS:
                    load_bias(i - 14)
                if i == first("down", 1) + 6:
                    load(cc[:, 0:2, :, :], a["s5_c"], cc_in)
            out = a["out"].rearrange("(c p) s -> p c s", p=P)
            for j in range(4):
                sp.wait_ge(final_ready, j + 1)
                load(out[:, 2 * j:2 * j + 2, :], tmp[:, 2 * j:2 * j + 2, :], out_done)
            sp.wait_ge(out_done, 4 * 16)

        @block.tensor
        def _(pe):
            me = Side(pe, None)

            def gemm(i, hi, lo, chunks_at=(), dst=G):
                b = PLAN[i]
                wh = w_hi[i % SPL][:, 0:b.used].rearrange("p (c n) -> p c n", c=b.kc)
                wl = w_lo[i % RAW][:, 0:b.used].rearrange("p (c n) -> p c n", c=b.kc)
                pe.wait_ge(w_lo_ready, i + 1)
                if b.freed:
                    pe.wait_ge(read_out, b.freed)
                todo = dict(chunks_at)
                mm = None
                parts = [range(len(b.tiles[0][2]))]
                if 6 in todo:
                    parts = [range(0, 6), range(6, 8)]
                for part in parts:
                    for at, (off, kind, pairs, c0, n, t) in enumerate(b.tiles):
                        o = (b.bank * BANK if b.banks else 0) + off
                        for k in part:
                            wc, xc = pairs[k]
                            if xc in todo:
                                me.take(*todo.pop(xc))
                            fresh = b.start and k == 0 and (at == 0 or b.stop and len(parts) == 1)
                            end = b.stop and k == len(pairs) - 1
                            if kind == "f":
                                out = dst[:, o:o + S]
                                two = [(wh[:, wc, c0:c0 + P], hi[:, xc, :]), (wh[:, wc, c0:c0 + P], lo[:, xc, :]),
                                       (wl[:, wc, c0:c0 + P], hi[:, xc, :])]
                            else:
                                out = dst[:, o:o + n]
                                tok = slice(t * P, (t + 1) * P)
                                two = [(hi[:, xc, tok], wh[:, wc, c0:c0 + n]), (hi[:, xc, tok], wl[:, wc, c0:c0 + n]),
                                       (lo[:, xc, tok], wh[:, wc, c0:c0 + n])]
                            for m, (lhs, rhs) in enumerate(two):
                                mm = pe.matmul(out, lhs, rhs, start=fresh and m == 0, stop=end and m == 2,
                                               skip_group_check=True)
                me.give(mm, mm_done)

            def mean_square(chunks, outs):
                me.take(sq_ready)
                mm = None
                for cs, o in zip(chunks, outs):
                    for k, c in enumerate(cs):
                        mm = pe.matmul(A[:, o:o + S], ones[:, :], tmp[:, c, :], start=k == 0, stop=k == len(cs) - 1,
                                       skip_group_check=True)
                me.give(mm, ms_ready)

            def sums_of_squares(src, count, pairs=0, bank=0, tokens=True, ready=ms_ready):
                o = bank * BANK
                mm = None
                for c in range(count):
                    if pairs and c % (count // pairs) == 0:
                        me.take(sq_ready)
                    mm = pe.matmul(A[:, o:o + S], ones[:, :], src[:, c, :], start=c == 0, stop=c == count - 1,
                                   skip_group_check=True)
                for t in range(ST if tokens else 0):
                    for c in range(count):
                        mm = pe.matmul(A[:, o + S + t:o + S + t + 1], src[:, c, t * P:(t + 1) * P], ones[:, 0:1],
                                       start=c == 0, stop=c == count - 1, skip_group_check=True)
                me.give(mm, ready)

            def norm(tokens=True):
                me.take(sums_ready)
                sums_of_squares(tmp, 2, tokens=tokens)

            BY_PAIR = {c: (x_ready, 1) for c in (0, 2, 4, 6)}

            def ffn(n):
                i = first("up_a", n)
                xh, xl = (x_hi, x_lo) if n < 2 else (xb_hi, xb_lo)
                for j in range(2 * PAIRS):
                    gemm(i + j, xh, xl, BY_PAIR if j == 0 else ())
                    if j == 0:
                        norm(tokens=False)
                i += 2 * PAIRS
                for j in range(12):
                    wait = {0: {0: (y_ready, 4)}, 1: {8: (y_ready, 4)}, 2: {16: (y_ready, 3)}}.get(j, ())
                    gemm(i + j, yh, yl, wait)

            def scores(u):
                s, q = divmod(u, ST)
                me.take(scores_read) if u else None
                mm = None
                for g in range(GROUPS):
                    hd = g * SLOTS + s
                    mm = pe.matmul(A[:, g * S:(g + 1) * S], qt[:, hd, q * P:(q + 1) * P], kt[:, hd, :],
                                   start=True, stop=True, skip_group_check=True)
                me.give(mm, scores_ready)

            def turn(u):
                me.take(prob_ready)
                mm = None
                for k in range(GROUPS * ST):
                    mm = pe.transpose(A[:, 2 * BANK + k * P:2 * BANK + (k + 1) * P], lg[:, k * P:(k + 1) * P], ident)
                me.give(mm, tr_ready)

            def pv(u):
                s, q = divmod(u, ST)
                me.take(pt_ready)
                if u:
                    me.take(pv_read)
                mm = None
                for k in range(GROUPS * ST):
                    hd = (k // ST) * SLOTS + s
                    mm = pe.matmul(G[:, 3 * BANK:3 * BANK + P], va[:, k % ST, hd * DH:(hd + 1) * DH], pt[:, k, :],
                                   start=k == 0, stop=k == GROUPS * ST - 1, skip_group_check=True)
                me.give(mm, pv_ready)

            def table(g):
                if g:
                    me.take(tab_copied)
                mm = None
                for s in range(SLOTS):
                    mm = pe.matmul(A[:, s * BANK:(s + 1) * BANK], relw[:, g * SLOTS + s, :],
                                   hot[:, g * (TAB + 1):(g + 1) * (TAB + 1)], start=True, stop=True)
                me.give(mm, tab_ready)

            def mixer(layer):
                i = first("v", layer)
                for j in range(18):
                    gemm(i + j, x_hi, x_lo, BY_PAIR if j == 0 else ())
                    if j == 0:
                        if layer == 0:
                            me.take(ones_ready)
                        norm()
                    if layer == 0 and j in (3, 5, 7):
                        if j == 3:
                            pe.wait_ge(hot_in, 16)
                            me.take(relb_ready)
                            pe.wait_ge(rstd_ready, 1)
                        table((j - 3) // 2)
                for j in range(10):
                    gemm(i + 18 + j, x_hi, x_lo)
                    if j == 0:
                        if layer == 0:
                            me.take(tab_copied)
                            pe.wait_ge(cst_in, 16)
                        me.take(qkv_ready)
                    if j < 8:
                        scores(j)
                    if 2 <= j:
                        pv(j - 2)
                    if 1 <= j < 9:
                        turn(j - 1)
                me.take(scores_read)
                gemm(first("pool", layer), ph, pl, {0: (x_ready, 1)}, dst=A)
                for j in range(2):
                    gemm(first("pool", layer) + 1 + j, x_hi, x_lo)
                me.take(pv_read)
                for j in range(2):
                    gemm(first("wb", layer) + j, ao_h, ao_l)
                for j in range(4):
                    gemm(first("wa", layer) + j, po_h, po_l, {0: (x_ready, 1), 4: (x_ready, 1)} if j == 0 else ())
                for j in range(4):
                    gemm(first("wo", layer) + j, ph, pl, BY_PAIR if j == 0 else ())
                ffn(layer)

            for layer in range(2):
                mixer(layer)

            i = first("ef")
            for j in range(10):
                gemm(i + j, x_hi, x_lo, BY_PAIR if j == 0 else ())
                if j == 0:
                    norm()
                    sums_of_squares(sq2, DC, pairs=1, bank=1, ready=ms2_ready)
            me.take(qd_ready)
            q4 = qb.rearrange("p (c s) -> p c s", c=4)
            k4 = enb.rearrange("p (c s) -> p c s", c=4)
            ke4 = dd.rearrange("p (c s) -> p c s", c=4)
            v24 = v2.rearrange("p (t n) -> p t n", t=ST)
            for c in range(4):
                for n in range(4):
                    r, o = CH * (n % 2), (2 * c + n // 2) * CH
                    mm = pe.matmul(A[r:r + CH, o:o + CH], k4[:, c, n * CH:(n + 1) * CH], q4[:, c, n * CH:(n + 1) * CH],
                                   start=True, stop=True, skip_group_check=True)
            me.give(mm, att_ready)
            for c in range(4):
                for t in range(ST):
                    o = BANK + (2 * c + t) * P
                    mm = pe.transpose(A[:, o:o + P], ke4[:, c, t * P:(t + 1) * P], ident)
            me.give(mm, ket_psum)
            me.take(cc_ready)
            me.take(bb_ready)
            u4 = uu.rearrange("p (c s) -> p c s", c=4)

            def s5_in_mm(g):
                m = None
                for part in range(2):
                    for k in range(4):
                        o = k * BANK + part * S
                        m = pe.matmul((G if g < 2 else A)[:, o:o + S], bb[32 * k:32 * k + 32, part, g, :],
                                      u4[32 * k:32 * k + 32, g, :],
                                      start=True, stop=True, skip_group_check=True, tile_position=(32 * k, 0))
                me.give(m, bu_ready)

            pe.wait_ge(read_out, PLAN[first("eg") + 1].out)
            s5_in_mm(0)
            me.take(ket_ready)
            for n in range(3):
                if n:
                    me.take(st_ready)
                r, t = CH * (n % 2), n // 2
                for c in range(4):
                    mm = pe.matmul(A[:, 3 * BANK + c * P:3 * BANK + (c + 1) * P], ket[r:r + CH, 2 * c + t, :],
                                   v24[r:r + CH, t, c * P:(c + 1) * P], start=True, stop=True, skip_group_check=True)
                me.give(mm, ds_ready)
            me.take(am_ready)
            me.take(st_ready)
            for c in range(4):
                for t in range(ST):
                    o = BANK + c * S + t * P
                    mm = pe.matmul(A[:, o:o + P], v24[:, t, c * P:(c + 1) * P], am[:, 2 * c + t, :],
                                   start=True, stop=False, skip_group_check=True)
                    for n in range(2 * t, 2 * t + 2):
                        if n:
                            oo = o + (n % 2) * CH
                            mm = pe.matmul(A[:, oo:oo + CH], st[:, n - 1, c, :], q4[:, c, n * CH:(n + 1) * CH],
                                           start=False, stop=n % 2 == 1, skip_group_check=True)
            me.give(mm, o_ready)
            mean_square([[0], [1], [2], [3]], [0, S, 3 * BANK, 3 * BANK + S])

            def s5_out_mm(g):
                me.take(s_ready)
                bufs = [prods[(4 * g + j) % 6] for j in range(4)]
                if g == 3:
                    me.take(s_half_ready)
                    bufs[2:4] = [t_s5[1], t_s5[3]]
                m = None
                for k in range(4):
                    o = G[32 * k:32 * k + 32, g * BANK:g * BANK + S]
                    for j, part in enumerate((0, 2, 1, 1)):
                        m = pe.matmul(o, cc[:, part, 4 * g + k, :], bufs[j][:, k * S:(k + 1) * S],
                                      start=j == 0, stop=j == 3, skip_group_check=True, tile_position=(0, 32 * k))
                me.give(m, ys_ready)

            me.take(bu_read)
            s5_in_mm(1)
            me.take(s5_free)
            for g in range(4):
                if g < 2:
                    me.take(bu_read)
                    s5_in_mm(g + 2)
                s5_out_mm(g)
            me.take(x_ready)
            pe.wait_ge(yd_ready, 4)
            gemm(first("glu"), x_hi, x_lo, {4: (x_ready, 1)})
            for j in range(4):
                gemm(first("eo") + j, x_hi, x_lo, {4: (x_ready, 1)} if j == 0 else ())
            ffn(2)

            for j in range(3):
                gemm(first("mp") + j, x_hi, x_lo, BY_PAIR if j == 0 else ())
                if j == 0:
                    norm(tokens=False)
            for j in range(4):
                gemm(first("uq") + j, xb_hi, xb_lo, {0: (x_ready, 1), 2: (x_ready, 1)} if j == 0 else ())
                if j == 0:
                    me.take(sq_ready)
                    for o, cs in ((0, (0, 1, 2)), (S, (3, 4))):
                        for c in cs:
                            pe.matmul(A[:, o:o + S], ones[:, :], sqm[:, c, :], start=c == cs[0], stop=c == cs[-1],
                                      skip_group_check=True)
                    for t in range(ST):
                        for c in (3, 4):
                            mm = pe.matmul(A[:, 2 * S + t:2 * S + t + 1], sqm[:, c, t * P:(t + 1) * P], ones[:, 0:1],
                                           start=c == 3, stop=c == 4, skip_group_check=True)
                    me.give(mm, ms_ready)
            gemm(first("ukv"), xb_hi, xb_lo, {3: (x_ready, 1)})
            me.take(rx_ready)
            rxf = rx.rearrange("p c s -> p (c s)")
            for k in range(2):
                pe.matmul(A[:, k * BANK:(k + 1) * BANK], rotate, rxf[:, k * BANK:(k + 1) * BANK], start=True, stop=True)
            mm = pe.matmul(A[:, 2 * BANK:2 * BANK + S], rotate, c6[:, 5, :], start=True, stop=True)
            me.give(mm, rot_ready)
            gemm(first("ukv") + 1, xb_hi, xb_lo)
            me.take(rope_ready)
            pe.wait_ge(read_out, PLAN[first("ukv") + 1].out)

            def m_scores(hd):
                if hd >= 2:
                    me.take(scores_read)
                b0, r = (hd % 2) * BANK, 64 * (hd % 2)
                m = None
                for q in range(ST):
                    nk = (q + 1) * P
                    o = A[:, b0 + q * P:b0 + q * P + nk]
                    pe.matmul(o, qn[:, hd, q * P:(q + 1) * P], kn[:, hd, 0:nk], start=True, stop=False,
                              skip_group_check=True)
                    m = pe.matmul(o, qr[r:r + 64, hd // 2, q * P:(q + 1) * P], kr[r:r + 64, 0, 0:nk], start=False,
                                  stop=True, skip_group_check=True)
                me.give(m, scores_ready)

            m_scores(0)
            for j in range(MH + 2):
                if j + 1 < MH:
                    m_scores(j + 1)
                if j >= 2:
                    hd = j - 2
                    me.take(pt_ready)
                    if hd:
                        me.take(pv_read)
                    o = 3 * BANK
                    pe.matmul(A[:, o:o + S], v3[:, 0, hd * DH:(hd + 1) * DH], pm[:, 0:S], start=True, stop=False,
                              skip_group_check=True)
                    mm = pe.matmul(A[:, o + P:o + S], v3[:, 1, hd * DH:(hd + 1) * DH], pm[:, S:S + P], start=False,
                                   stop=True, skip_group_check=True)
                    me.give(mm, pv_ready)
                if 1 <= j <= MH:
                    me.take(prob_ready)
                    for k in range(3):
                        mm = pe.transpose(A[:, 2 * BANK + k * P:2 * BANK + (k + 1) * P], lm[:, (j - 1) % 2, k, :], ident)
                    me.give(mm, tr_ready)
            me.take(scores_read, 2)
            me.take(pv_read)
            for j in range(4):
                gemm(first("mo") + j, x_hi, x_lo)
            ffn(3)
            sums_of_squares(tmp, DC, pairs=4, tokens=False)

        @block.scalar
        def _(act):
            me = Side(act, act_own)

            def split(i):
                if i >= N:
                    return
                n = PLAN[i].used
                act.wait_ge(raw_in[i % RAW], 16 * (i // RAW + 1))
                if i >= SPL:
                    act.wait_ge(mm_done, i - SPL + 1)
                me.give(act.activation(w_hi[i % SPL][:, 0:n], raw[i % RAW][:, 0:n], ACT.Copy), w_hi_ready)

            def split_next(i):
                split(i + SPL)

            def split_all(i, n):
                for k in range(n):
                    split_next(i + k)

            def hi(dst, src, scale=1.0):
                me.take(x_f32)
                me.give(act.activation(dst, src, ACT.Copy, scale=scale), x_hi_ready)

            def root(outs):
                me.take(ms_ready)
                for k, (dst, off, width, count_) in enumerate(outs):
                    ins = act.activation(dst, A[:, off:off + width], ACT.Sqrt, bias=eps, scale=1.0 / count_)
                me.give(ins, rms_ready)

            def feed(j, g, xh=x_hi, x=h, sq=tmp):
                for c in (2 * j, 2 * j + 1):
                    ins = act.activation(xh[:, c, :], x[:, c, :], ACT.Copy, scale=g(c))
                me.give(ins, x_hi_ready)
                me.give(act.activation(sq[:, 2 * j:2 * j + 2, :], x[:, 2 * j:2 * j + 2, :], ACT.Square), pair_squared)

            def named(name):
                return lambda c: vec(name, c)

            def feed_after(i, g, xh=x_hi, step=1):
                for j in range(4):
                    for k in range(step - 1):
                        split_next(i + step * j + k)
                    act.wait_ge(read_out, PLAN[i + step * j + step - 1].out)
                    feed(j, g, xh)
                    split_next(i + step * j + step - 1)

            def tokens_root():
                root([(rstd[:, 0:S + 2], 0, S + 2, D)])

            def psum(i):
                b = PLAN[i]
                act.wait_ge(mm_done, i + 1)
                return G[:, b.bank * BANK:(b.bank + b.banks) * BANK]

            def ffn(n, then, xh=x_hi):
                i = first("up_a", n)
                centre = 1 if n < 2 else 2
                func = ACT.Gelu_apprx_tanh if n < 2 else ACT.Silu
                split_next(i)
                root([(rstd[:, 0:S], 0, S, D)])

                def y_half(j):
                    act.wait_ge(read_out, PLAN[i + 2 * j + 1].out)
                    me.give(act.activation(yh[:, 2 * j:2 * j + 2, :], cv[:, j % 2, :, :], ACT.Copy), y_hi)

                for j in range(PAIRS):
                    ia, c, x = i + 2 * j, cv[:, j % 2, :, :], ar[:, j % 2, :, :]
                    if j:
                        split_next(ia)
                        y_half(j - 1)
                    if j >= 2:
                        act.wait_ge(y_ready, n * PAIRS + j - 1)
                    act.wait_ge(read_out, PLAN[ia].out)
                    for t in range(2):
                        ins = act.activation(c[:, t, :], x[:, t, :], ACT.Identity, bias=vec(f"convb.{n}", 2 * j + t),
                                             scale=vec(f"conv{centre}.{n}", 2 * j + t))
                    me.give(ins, conv_mid)
                    split_next(ia + 1)
                    me.take(conv_done)
                    me.give(act.activation(c, c, func), act_ready)
                y_half(PAIRS - 1)
                then(first("down", n))

            def pv_half(u):
                s, q = divmod(u, ST)
                me.take(pv_ready)
                me.give(act.activation(ao_h[:, s, q * P:(q + 1) * P], G[:, 3 * BANK:3 * BANK + P], ACT.Copy), pv_hi)

            def gate(layer, j):
                act.wait_ge(gate_in, 8 * layer + j + 1)
                g = (gate_p if j < 4 else gate_a)[:, 2 * (j % 4):2 * (j % 4) + 2, :]
                me.give(act.activation(g, g, ACT.Tanh, scale=0.5), gate_ready)

            def mixer(layer):
                i = first("v", layer)
                split_next(i)
                tokens_root()
                for j in range(1, 18):
                    split_next(i + j)
                    if layer == 0:
                        setup.get(j, lambda: None)()
                for j in range(10):
                    ib = i + 18 + j
                    split_next(ib)
                    if j >= 4:
                        gate(layer, j - 4)
                    if j < 8:
                        me.take(lg_ready)
                        me.give(act.activation(lg[:, :], lg[:, :], ACT.Exp, bias=nm[:, 0:1], accum_out=sums[:, 0:1]),
                                exp_ready)
                    if 2 <= j:
                        pv_half(j - 2)
                    if 1 <= j < 9:
                        me.take(tr_ready)
                        ptf = pt.rearrange("p k n -> p (k n)")
                        act.activation(ptf[:, 0:BANK], A[:, 2 * BANK:3 * BANK], ACT.Copy)
                        me.give(act.activation(ptf[:, BANK:6 * P], A[:, 3 * BANK:3 * BANK + 2 * P], ACT.Copy), pt_ready)
                    if j == 8:
                        me.take(pooled, 4)
                        me.give(act.activation(ph[:, :, :], tmp[:, :, :], ACT.Copy), x_hi_ready)
                ip = first("pool", layer)
                act.wait_ge(mm_done, ip + 1)
                for k in range(DC):
                    ins = act.activation(po_h[:, k, :], A[:, k * S:(k + 1) * S], ACT.Copy,
                                         scale=vec(f"pool_scale.{layer}", k))
                    if k % 4 == 3:
                        me.give(ins, x_hi_ready)
                split_next(ip)
                for j in range(2):
                    split_next(ip + 1 + j)
                    gate(layer, 6 + j)
                split_all(first("wb", layer), 2)
                for j in range(4):
                    split_next(first("wa", layer) + j)
                    hi(ph[:, 2 * j:2 * j + 2, :], tmp[:, 2 * j:2 * j + 2, :], 0.5)
                feed_after(first("wo", layer), named(f"norm2.{layer}"))

            act.wait_ge(par_in, 16)
            act.wait_ge(x_in, 16)
            for j in range(4):
                feed(j, named("norm1.0"))
                if j == 0:
                    split(0)
            for i in range(1, SPL):
                split(i)

            dt, mag = ang[3], ang[4]

            def setup_dt():
                act.wait_ge(s5_in, 48)
                me.give(act.activation(dt[:, 0:NS5], ang[2][:, 0:NS5], ACT.Exp), dt_ready)
                me.take(lbd_ready)
                me.give(act.activation(lbt[:, 0:8], lbt[:, 0:8], ACT.Exp), lbe_ready)

            def setup_mag():
                me.take(ndt_ready)
                me.give(act.activation(mag[:, 0:NS5], mag[:, 0:NS5], ACT.Exp), mag_ready)

            def setup_trig():
                me.take(red_ready)
                act.activation(ang[7][:, :], ang[7][:, :], ACT.Sin)
                me.give(act.activation(ang[8][:, :], ang[8][:, :], ACT.Sin), trig_ready)

            def setup_table(g):
                me.take(tab_ready)
                if g == 2:
                    act.wait_ge(tab_out[0], 16)
                me.give(act.activation(tab[:, g % 2, :, :].rearrange("p h n -> p (h n)"), A[:, :], ACT.Copy), tab_copied)

            setup = {1: setup_dt, 2: setup_mag, 3: setup_trig, 4: lambda: setup_table(0), 6: lambda: setup_table(1),
                     8: lambda: setup_table(2)}
            mixer(0)
            ffn(0, lambda i: feed_after(i, named("norm1.1"), step=3))
            mixer(1)

            def feed_two(i):
                feed_after(i, lambda c: gg[:, c:c + 1], step=3)
                act.wait_ge(e_ready, 1)
                for c in range(DC):
                    ins = act.activation(sq2[:, c, :], h[:, c, :], ACT.Square, scale=vec("norm_f", c))
                me.give(ins, sq_ready)

            ffn(1, feed_two)
            i = first("ef")
            split_next(i)
            root([(rf[:, :], 0, S + 2, D)])
            me.take(rf_ready)
            me.give(act.activation(rstd[:, 0:S + 2], rstd[:, 0:S + 2], ACT.Sqrt, bias=eps, scale=1.0 / D), rms_ready)
            for j in range(2):
                act.wait_ge(gate_in, 17 + j)
                f = fe[:, j * BANK:(j + 1) * BANK]
                me.give(act.activation(f, f, ACT.Tanh, scale=0.5), gate_ready)
                if j:
                    split_next(i + 1)
            split_next(i + 2)
            me.take(f_ready)
            me.give(act.activation(fe[:, :], fe[:, :], ACT.Ln), ln_ready)
            split_next(i + 3)
            me.take(cum_ready)
            act.activation(eb[:, :], cum[:, :], ACT.Exp)
            act.activation(enb[:, :], cum[:, :], ACT.Exp, scale=-1.0)
            me.give(act.activation(dd[:, :], dd[:, :], ACT.Exp), eb_ready)
            split_all(i + 4, 4)
            for j in range(2):
                act.wait_ge(gate_in, 19 + j)
                me.give(act.activation(sgate[:, j * BANK:(j + 1) * BANK], fe[:, j * BANK:(j + 1) * BANK], ACT.Tanh,
                                       scale=0.5), gate_ready)
                split_next(i + 8 + j)
            me.take(ket_psum)
            me.give(act.activation(ket.rearrange("p k n -> p (k n)"), A[:, BANK:3 * BANK], ACT.Copy), ket_ready)
            me.take(o_ready)
            me.give(act.activation(tmp[:, 0:4, :].rearrange("p c s -> p (c s)"), A[:, BANK:3 * BANK], ACT.Square),
                    sq_ready)
            root([(fe[:, 0:BANK], 0, BANK, DH), (fe[:, BANK:2 * BANK], 3 * BANK, BANK, DH)])
            hi(x_hi[:, 0:4, :], tmp[:, 0:4, :])
            for g in range(4):
                me.take(yd_ready)
                me.give(act.activation(tmp[:, 4 + g, :], tmp[:, 4 + g, :], ACT.Gelu_apprx_tanh), zg_ready)
            me.settle()
            me.give(act.activation(x_hi[:, 4:8, :], tmp[:, 4:8, :], ACT.Copy), x_hi_ready)
            ig = first("glu")
            p = psum(ig)
            for k in range(4):
                ins = act.activation(z_second[:, k * S:(k + 1) * S], p[:, k * S:(k + 1) * S], ACT.Tanh, bias=hbglu[:, k:k + 1],
                                     scale=0.5)
            me.give(ins, gate_ready)
            split_next(ig)
            hi(x_hi[:, 4:8, :], tmp[:, 4:8, :], 0.5)
            feed_after(first("eo"), named("ffn.0"), xb_hi)
            ffn(2, lambda i: feed_after(i, named("mix.1"), step=3))
            i = first("mp")
            split_next(i)
            root([(rstd[:, 0:S], 0, S, D)])
            for j in range(3):
                act.wait_ge(read_out, PLAN[i + j].out)
                cs = range(2 * j, min(2 * j + 2, 5))
                for c in cs:
                    ins = act.activation(xb_hi[:, c, :], c6[:, c, :], ACT.Copy,
                                         scale=vec("q_g", c) if c < 3 else vec("kv_g", c - 3))
                me.give(ins, x_hi_ready)
                ins = act.activation(sqm[:, cs[0]:cs[-1] + 1, :], c6[:, cs[0]:cs[-1] + 1, :], ACT.Square)
                if j == 2:
                    me.give(ins, sq_ready)
                else:
                    split_next(i + 1 + j)
            split_next(first("uq"))
            root([(rstd[:, 0:S], 0, S, 384), (rstd[:, S:2 * S + 2], S, S + 2, 256)])
            split_all(first("uq") + 1, 5)
            for j in range(MH + 2):
                if j < MH:
                    me.take(lg_ready)
                    l = lm[:, j % 2, :, :].rearrange("p k n -> p (k n)")
                    act.activation(l[:, 0:P], l[:, 0:P], ACT.Exp, bias=m_nm[j % 2][:, 0:1],
                                   accum_out=m_sums[j % 2][:, 0:1])
                    me.give(act.activation(l[:, P:3 * P], l[:, P:3 * P], ACT.Exp, bias=m_nm[j % 2][:, 1:2],
                                           accum_out=m_sums[j % 2][:, 1:2]), exp_ready)
                if j >= 2:
                    me.take(pv_ready)
                    me.give(act.activation(x_hi[:, j - 2, :], A[:, 3 * BANK:3 * BANK + S], ACT.Copy), pv_hi)
                if 1 <= j <= MH:
                    me.take(tr_ready)
                    me.give(act.activation(pm[:, :], A[:, 2 * BANK:2 * BANK + 3 * P], ACT.Copy), pt_ready)
            feed_after(first("mo"), named("ffn.1"), xb_hi)

            def squares(i):
                for j in range(4):
                    split_all(i + 3 * j, 3)
                    act.wait_ge(read_out, PLAN[i + 3 * j + 2].out)
                    me.give(act.activation(tmp[:, 2 * j:2 * j + 2, :], h[:, 2 * j:2 * j + 2, :], ACT.Square), sq_ready)

            ffn(3, squares)
            root([(rstd[:, 0:S], 0, S, D)])

        @block.vector
        def _(v):
            me = Side(v, dve_own)

            def split(i):
                if i >= N:
                    return
                n = PLAN[i].used
                me.taken[w_hi_ready.name] = i
                me.take(w_hi_ready)
                me.give(v.tensor_tensor(w_lo[i % RAW][:, 0:n], raw[i % RAW][:, 0:n],
                                        w_hi[i % SPL][:, 0:n].bitcast(F32), ALU.subtract), w_lo_ready)

            def split_next(i):
                split(i + SPL)

            def lo(dst, src, hi_, scale=1.0):
                me.take(x_hi_ready)
                me.give(v.scalar_tensor_tensor(out=dst, in0=src, scalar=scale, in1=hi_.bitcast(F32), op0=ALU.mult,
                                               op1=ALU.subtract), x_ready)

            def psum(i):
                b = PLAN[i]
                v.wait_ge(mm_done, i + 1)
                return G[:, b.bank * BANK:(b.bank + b.banks) * BANK]

            def feed(j, g, xh=x_hi, xl=x_lo, x=h):
                me.take(x_hi_ready)
                for c in (2 * j, 2 * j + 1):
                    ins = v.scalar_tensor_tensor(out=xl[:, c, :], in0=x[:, c, :], scalar=g(c), in1=xh[:, c, :].bitcast(F32),
                                                 op0=ALU.mult, op1=ALU.subtract)
                me.give(ins, x_ready)

            def named(name):
                return lambda c: vec(name, c)

            def add_feed(i, g, xh=x_hi, xl=x_lo, step=1):
                for j in range(4):
                    for k in range(step - 1):
                        split_next(i + step * j + k)
                    add_h(i + step * j + step - 1, j)
                    me.settle()
                    if g is not None:
                        feed(j, g, xh, xl)
                    split_next(i + step * j + step - 1)

            def root(width=S):
                me.take(rms_ready)
                me.give(v.reciprocal(rstd[:, 0:width], rstd[:, 0:width]), rstd_ready)
                me.settle()

            def by_token(dst, i, chunks=2, r=0):
                scale = rstd[:, r:r + S].rearrange("p (o s) -> p o s", o=1).to_broadcast([P, chunks, S])
                me.give(v.tensor_tensor(dst, scale, psum(i)[:, 0:chunks * S].rearrange("p (c s) -> p c s", c=chunks),
                                        ALU.mult), read_out)

            def add_h(i, j):
                hh = h[:, 2 * j:2 * j + 2, :].rearrange("p c s -> p (c s)")
                me.give(v.tensor_tensor(hh, hh, psum(i), ALU.add), read_out)

            def ffn(n, g, xh=x_hi, xl=x_lo):
                i = first("up_a", n)
                centre = 1 if n < 2 else 2
                split_next(i)
                root()
                for j in range(PAIRS):
                    ia, c, x = i + 2 * j, cv[:, j % 2, :, :], ar[:, j % 2, :, :]
                    by_token(x, ia)
                    if j:
                        split_next(ia)
                    me.take(conv_mid)
                    taps = [k for k in range(3) if k != centre]
                    for k in taps:
                        sh = k - centre
                        o0, o1 = max(0, -sh), S - max(0, sh)
                        for t in range(2):
                            ins = v.scalar_tensor_tensor(out=c[:, t, o0:o1], in0=x[:, t, o0 + sh:o1 + sh],
                                                         scalar=vec(f"conv{k}.{n}", 2 * j + t), in1=c[:, t, o0:o1],
                                                         op0=ALU.mult, op1=ALU.add)
                        me.give(ins, None if k == taps[0] else conv_done)
                        if k == taps[0]:
                            me.settle()
                    split_next(ia + 1)
                    me.take(act_scaled)
                    cf = c.rearrange("p c s -> p (c s)")
                    me.give(v.tensor_tensor(cf, cf, psum(ia + 1), ALU.mult), read_out)
                add_feed(first("down", n), g, xh, xl, step=3)

            def soft_a(u):
                s, q = divmod(u, ST)
                if u:
                    me.take(tr_ready)
                me.take(scores_ready)
                v.tensor_tensor(lg[:, 0:BANK], A[:, 0:BANK], bm[:, q, s, 0:BANK], ALU.add)
                me.give(v.tensor_tensor(lg[:, BANK:3 * S], A[:, BANK:BANK + S], bm[:, q, s, BANK:3 * S], ALU.add),
                        scores_read)
                me.settle()
                me.give(v.tensor_reduce(mx[:, 0:1], lg[:, :], AX.X, ALU.max))
                me.settle()
                me.give(v.tensor_scalar(nm[:, 0:1], mx[:, 0:1], -1.0, None, ALU.mult), lg_ready)

            def soft_b():
                me.take(exp_ready)
                me.give(v.reciprocal(rs[:, 0:1], sums[:, 0:1]))
                me.settle()
                me.give(v.tensor_scalar(lg[:, :], lg[:, :], rs[:, 0:1], None, ALU.mult), prob_ready)

            def gated(dst, g, x, signal=None):
                me.give(v.scalar_tensor_tensor(out=dst, in0=g, scalar=1.0, in1=x, op0=ALU.add, op1=ALU.mult), signal)

            def gate_of(j):
                return (gate_p if j < 4 else gate_a)[:, 2 * (j % 4):2 * (j % 4) + 2, :]

            def mixer(layer):
                i = first("v", layer)
                split_next(i)
                root(S + 2)
                for j in range(18):
                    k = 2 * (j % 6)
                    if layer == 0 and j == 6:
                        v.wait_ge(bb_ready, 1)
                    if j < 6:
                        p = psum(i + j)
                        for t in range(ST):
                            ins = v.tensor_scalar(va[:, t, j * S:(j + 1) * S], p[:, t * S:(t + 1) * S],
                                                  rstd[:, S + t:S + t + 1], None, ALU.mult)
                        me.give(ins, read_out)
                    elif j < 12:
                        scale = rstd[:, 0:S].rearrange("p (o s) -> p o s", o=1).to_broadcast([P, 2, S])
                        me.give(v.scalar_tensor_tensor(out=qt[:, k:k + 2, :], in0=psum(i + j).rearrange("p (c s) -> p c s", c=2),
                                                       scalar=DH ** -0.5, in1=scale, op0=ALU.mult, op1=ALU.mult),
                                read_out)
                    else:
                        by_token(kt[:, k:k + 2, :], i + j)
                    if j:
                        split_next(i + j)
                    if layer == 0:
                        setup.get(j, lambda: None)()
                me.settle()
                me.give(v.tensor_copy(small[:, 41:42], small[:, 0:1]), qkv_ready)
                me.take(u_zero)
                if layer == 0:
                    v.wait_ge(bm_in, 16 * ST * SLOTS)

                for j in range(10):
                    ib = i + 18 + j
                    if j < 4:
                        by_token(ub[:, 2 * j:2 * j + 2, PADT:PADT + S], ib)
                    else:
                        by_token(gate_of(j - 4), ib)
                        me.settle()
                        me.give(v.tensor_copy(small[:, 42:43], small[:, 0:1]), gate_in)
                    split_next(ib)
                    if j < 8:
                        soft_a(j)
                    if 2 <= j:
                        s, q = divmod(j - 2, ST)
                        me.take(pv_hi)
                        me.give(v.tensor_tensor(ao_l[:, s, q * P:(q + 1) * P], G[:, 3 * BANK:3 * BANK + P],
                                                ao_h[:, s, q * P:(q + 1) * P].bitcast(F32), ALU.subtract), pv_read)
                    if j < 8:
                        soft_b()
                    if j == 8:
                        me.take(tr_ready)
                        lo(pl[:, :, :], tmp[:, :, :], ph[:, :, :])
                ip = first("pool", layer)
                v.wait_ge(mm_done, ip + 1)
                for k in range(DC):
                    if k % 4 == 0:
                        me.take(x_hi_ready)
                    ins = v.scalar_tensor_tensor(out=po_l[:, k, :], in0=A[:, k * S:(k + 1) * S],
                                                 scalar=vec(f"pool_scale.{layer}", k), in1=po_h[:, k, :].bitcast(F32),
                                                 op0=ALU.mult, op1=ALU.subtract)
                    if k % 4 == 3:
                        me.give(ins, x_ready)
                split_next(ip)
                for j in range(2):
                    by_token(gate_of(6 + j), ip + 1 + j)
                    me.settle()
                    me.give(v.tensor_copy(small[:, 42:43], small[:, 0:1]), gate_in)
                    split_next(ip + 1 + j)
                me.take(gate_ready, 8)
                for j in range(2):
                    g = gate_a[:, 4 * j:4 * j + 4, :].rearrange("p c s -> p (c s)")
                    gated(g, g, psum(first("wb", layer) + j), read_out)
                    split_next(first("wb", layer) + j)
                ia = first("wa", layer)
                for j in range(4):
                    g = gate_p[:, 2 * j:2 * j + 2, :].rearrange("p c s -> p (c s)")
                    gated(g, g, psum(ia + j), read_out)
                    me.settle()
                    me.give(v.tensor_tensor(tmp[:, 2 * j:2 * j + 2, :], gate_a[:, 2 * j:2 * j + 2, :],
                                            gate_p[:, 2 * j:2 * j + 2, :], ALU.add), x_f32)
                    lo(pl[:, 2 * j:2 * j + 2, :], tmp[:, 2 * j:2 * j + 2, :], ph[:, 2 * j:2 * j + 2, :], 0.5)
                    split_next(ia + j)
                add_feed(first("wo", layer), named(f"norm2.{layer}"))

            v.memset(ones[:, :], 1.0)
            v.memset(small[:, 0:1], EPS)
            me.give(v.memset(small[:, 1:4], 0.0), ones_ready)
            v.wait_ge(par_in, 16)
            v.wait_ge(x_in, 16)
            for j in range(4):
                feed(j, named("norm1.0"))
                if j == 0:
                    split(0)
            for i in range(1, SPL):
                split(i)
            theta, red = ang[5], ang[6]

            def setup_bounds():
                v.wait_ge(relb_in, 16)
                me.give(v.memset(relb[BUCKETS:BUCKETS + 1, :], 1.0))
                me.settle()
                me.give(v.tensor_copy(relw[:, :, :], relb[:, :].rearrange("p (h o) -> p h o", o=1)
                                      .to_broadcast([BUCKETS + 1, HEADS, P])), relb_ready)
                v.tensor_tensor(gg[:, :], par[:, COL["norm_f"]:COL["norm_f"] + 8], par[:, COL["mix.0"]:COL["mix.0"] + 8],
                                ALU.mult)
                l0, l1 = par[:, COL["lb0"]:COL["lb0"] + 4], par[:, COL["lb1"]:COL["lb1"] + 4]
                me.give(v.tensor_tensor(lbt[:, 8:12], l0, l1, ALU.max))
                me.settle()
                v.tensor_tensor(lbt[:, 0:4], l0, lbt[:, 8:12], ALU.subtract)
                v.tensor_scalar(hbglu, par[:, COL["b_glu"]:COL["b_glu"] + 4], 0.5, None, ALU.mult)
                me.give(v.tensor_tensor(lbt[:, 4:8], l1, lbt[:, 8:12], ALU.subtract), lbd_ready)

            def setup_angles():
                v.wait_ge(pos_in, 16)
                v.wait_ge(cst_in, 16)
                me.give(v.tensor_copy(theta[:, NS5:NANG], pos_i[:, :]))
                me.settle()
                me.give(v.tensor_scalar(theta[:, NS5:NANG], theta[:, NS5:NANG], freq, None, ALU.mult))
                me.settle()
                me.take(th_ready)
                k = ang[9]
                me.give(v.tensor_scalar(k[:, :], theta[:, :], 1.0 / TWO_PI, MAGIC, ALU.mult, ALU.add))
                me.settle()
                me.give(v.tensor_scalar(k[:, :], k[:, :], MAGIC, None, ALU.subtract))
                me.settle()
                src = theta
                for c in (C1, C2, C3):
                    me.give(v.scalar_tensor_tensor(out=red[:, :], in0=k[:, :], scalar=-c, in1=src[:, :], op0=ALU.mult,
                                                   op1=ALU.add))
                    me.settle()
                    src = red
                lim = 3.1415925
                me.give(v.tensor_scalar(ang[7][:, :], red[:, :], lim, -lim, ALU.min, ALU.max))
                me.settle()
                me.give(v.scalar_tensor_tensor(out=ang[8][:, :], in0=ang[7][:, :], scalar=-1.0, in1=ang[7][:, :],
                                               op0=ALU.mult, op1=ALU.max))
                me.settle()
                me.give(v.tensor_scalar(ang[8][:, :], ang[8][:, :], -1.0, float(np.pi / 2), ALU.mult, ALU.add), red_ready)

            def setup_kept():
                me.take(trig_ready)
                v.tensor_copy(sin_r[:, 0, :], ang[7][:, NS5:NANG])
                me.give(v.tensor_copy(cos_r[:, 0, :], ang[8][:, NS5:NANG]), rope_kept)
                me.take(lbe_ready)
                me.give(v.tensor_tensor(lbt[:, 8:12], lbt[:, 0:4], lbt[:, 4:8], ALU.add))
                me.settle()
                me.give(v.reciprocal(lbt[:, 8:12], lbt[:, 8:12]))
                me.settle()
                me.give(v.scalar_tensor_tensor(out=fslope, in0=lbt[:, 4:8], scalar=0.5, in1=lbt[:, 8:12], op0=ALU.mult,
                                               op1=ALU.mult))
                me.give(v.tensor_tensor(lbt[:, 0:4], lbt[:, 0:4], lbt[:, 8:12], ALU.mult))
                me.settle()
                me.give(v.tensor_tensor(fbase, lbt[:, 0:4], fslope, ALU.add))
                me.take(den_ready)
                me.give(v.reciprocal(s5x[0][:, :], s5x[0][:, :]), rden_ready)

            setup = {0: setup_bounds, 2: setup_angles, 3: setup_kept}
            mixer(0)
            ffn(0, named("norm1.1"))
            mixer(1)
            ffn(1, lambda c: gg[:, c:c + 1])
            i = first("ef")
            split_next(i)
            me.take(rms_ready)
            me.give(v.reciprocal(rf[:, :], rf[:, :]))
            me.settle()
            me.give(v.tensor_tensor(rf2[:, :], rf[:, :], rf[:, :], ALU.mult))
            me.settle()
            me.take(ms2_ready)
            me.give(v.tensor_tensor(rstd[:, 0:S + 2], rf2[:, :], A[:, BANK:BANK + S + 2], ALU.mult), rf_ready)
            me.take(rms_ready)
            me.give(v.reciprocal(rstd[:, 0:S + 2], rstd[:, 0:S + 2]))
            me.settle()
            me.give(v.tensor_tensor(rstd[:, 0:S + 2], rstd[:, 0:S + 2], rf[:, :], ALU.mult), rstd_ready)
            me.settle()
            for j in range(2):
                f = fe[:, j * BANK:(j + 1) * BANK]
                by_token(f.rearrange("p (c s) -> p c s", c=2), i + j)
                me.settle()
                me.give(v.tensor_copy(small[:, 42:43], small[:, 0:1]), gate_in)
                if j:
                    split_next(i + 1)
                me.take(gate_ready)
                for c in range(2):
                    fc = fe[:, j * BANK + c * S:j * BANK + (c + 1) * S]
                    ins = v.tensor_scalar(fc, fc, fslope[:, 2 * j + c:2 * j + c + 1], fbase[:, 2 * j + c:2 * j + c + 1],
                                          ALU.mult, ALU.add)
                me.give(ins)
                me.settle()
                me.give(v.tensor_scalar(key[:, j * BANK:(j + 1) * BANK], f, -1.0, 1.0, ALU.mult, ALU.add),
                        f_ready if j else None)
            for c in range(DC):
                ins = v.scalar_tensor_tensor(out=h[:, c, :], in0=h[:, c, :], scalar=vec("norm_f", c), in1=rf[:, 0:S],
                                             op0=ALU.mult, op1=ALU.mult)
            me.give(ins)
            by_token(qb[:, 0:BANK].rearrange("p (c s) -> p c s", c=2), i + 2)
            split_next(i + 2)
            me.take(ln_ready)
            me.take(smask_ready)
            me.give(v.tensor_tensor_scan(cum[:, :], smask[:, :], fe[:, :], 0.0, ALU.mult, ALU.add))
            me.settle()
            c16 = cum.rearrange("p (c s) -> p c s", s=CH)
            last = c16[:, :, CH - 1:CH].to_broadcast([P, 16, CH])
            me.give(v.tensor_tensor(dd.rearrange("p (c s) -> p c s", s=CH), last, c16, ALU.subtract), cum_ready)
            by_token(qb[:, BANK:2 * BANK].rearrange("p (c s) -> p c s", c=2), i + 3)
            split_next(i + 3)
            me.settle()
            me.take(eb_ready)
            v.tensor_tensor(qb[:, :], qb[:, :], eb[:, :], ALU.mult)
            v.tensor_tensor(enb[:, :], enb[:, :], key[:, :], ALU.mult)
            me.give(v.tensor_tensor(dd[:, :], dd[:, :], key[:, :], ALU.mult), qd_ready)
            for j in range(2):
                by_token(uu[:, j * BANK:(j + 1) * BANK].rearrange("p (c s) -> p c s", c=2), i + 4 + j)
                split_next(i + 4 + j)
            v24 = v2.rearrange("p (t n) -> p t n", t=ST)
            for j in range(2):
                p = psum(i + 6 + j)
                for t in range(ST):
                    ins = v.tensor_scalar(v24[:, t, j * S:(j + 1) * S], p[:, t * S:(t + 1) * S], rstd[:, S + t:S + t + 1],
                                          None, ALU.mult)
                me.give(ins, read_out)
                split_next(i + 6 + j)
            for j in range(2):
                g = sgate[:, j * BANK:(j + 1) * BANK]
                f = fe[:, j * BANK:(j + 1) * BANK]
                by_token(f.rearrange("p (c s) -> p c s", c=2), i + 8 + j)
                me.settle()
                me.give(v.tensor_copy(small[:, 42:43], small[:, 0:1]), gate_in)
                split_next(i + 8 + j)
                me.take(gate_ready)
                gated(g, g, f)
            me.take(att_ready)
            me.take(am_zero)
            att = A[:, 0:BANK].rearrange("p (k n) -> p k n", n=CH)
            for r in (0, CH):
                ins = v.copy_predicated(am[r:r + CH, :, r:r + CH],
                                        ccausal[r:r + CH, :].rearrange("p (o n) -> p o n", o=1).to_broadcast([CH, 8, CH]),
                                        att[r:r + CH, :, :])
            me.give(ins, am_ready)
            for n in range(3):
                me.take(ds_ready)
                if n == 0:
                    me.give(v.tensor_copy(st[:, 0, :, :].rearrange("p c n -> p (c n)"), A[:, 3 * BANK:4 * BANK]), st_ready)
                else:
                    me.settle()
                    for c in range(4):
                        e = c * S + n * CH + CH - 1
                        ins = v.scalar_tensor_tensor(out=st[:, n, c, :], in0=st[:, n - 1, c, :], scalar=eb[:, e:e + 1],
                                                     in1=A[:, 3 * BANK + c * P:3 * BANK + (c + 1) * P],
                                                     op0=ALU.mult, op1=ALU.add)
                    me.give(ins, st_ready)
            me.take(e_ready)
            t1, t2, t3, t4 = t_s5

            def s5_states(g):
                gs = slice(4 * g, 4 * g + 4)
                ecg, esg = ec[:, gs, :], es[:, gs, :]
                bu = (G if g < 2 else A)[:, :].rearrange("p (k n) -> p k n", k=4)
                re, im = bu[:, :, 0:S], bu[:, :, S:2 * S]
                u1, u2, u3, u4 = (t.rearrange("p (k n) -> p k n", k=4) for t in (t1, t2, t3, t4))
                me.take(bu_ready)
                v.tensor_tensor(u1, ecg, re, ALU.mult)
                v.tensor_tensor(u2, esg, im, ALU.mult)
                v.tensor_tensor(u3, ecg, im, ALU.mult)
                me.give(v.tensor_tensor(u4, esg, re, ALU.mult), bu_read)
                me.settle()
                v.tensor_tensor(t1[:, :], t1[:, :], t2[:, :], ALU.add)
                me.give(v.tensor_tensor(t3[:, :], t3[:, :], t4[:, :], ALU.subtract))
                me.settle()
                if g >= 2:
                    me.take(z_read)
                zr, zi = zs[g]
                for k in range(4):
                    m = s5_st[:, 0, 4 * g + k:4 * g + k + 1].to_broadcast([P, S])
                    ks = slice(k * S, (k + 1) * S)
                    v.tensor_tensor_scan(zr[:, ks], m, t1[:, ks], 0.0, ALU.mult, ALU.add)
                    ins = v.tensor_tensor_scan(zi[:, ks], m, t3[:, ks], 0.0, ALU.mult, ALU.add)
                me.give(ins, z_ready)
                me.settle()

            me.settle()
            s5_states(0)
            me.take(rms_ready)
            me.give(v.reciprocal(fe[:, :], fe[:, :]))
            me.settle()
            for c in range(4):
                cs = slice(c * S, (c + 1) * S)
                ins = v.scalar_tensor_tensor(out=key[:, cs], in0=A[:, BANK + c * S:BANK + (c + 1) * S],
                                             scalar=vec("hgrn_g", c), in1=fe[:, cs], op0=ALU.mult, op1=ALU.mult)
            me.give(ins)
            me.settle()
            me.give(v.scalar_tensor_tensor(out=tmp[:, 0:4, :].rearrange("p c s -> p (c s)"), in0=key[:, :], scalar=0.5,
                                           in1=sgate[:, :], op0=ALU.mult, op1=ALU.mult), x_f32)
            lo(x_lo[:, 0:4, :], tmp[:, 0:4, :], x_hi[:, 0:4, :])
            me.settle()
            me.give(v.tensor_copy(small[:, 44:45], small[:, 0:1]), s5_free)
            def s5_y(g):
                me.take(ys_ready)
                me.give(v.scalar_tensor_tensor(out=tmp[:, 4 + g, :], in0=uu[:, g * S:(g + 1) * S], scalar=vec("s5_d", g),
                                               in1=G[:, g * BANK:g * BANK + S], op0=ALU.mult, op1=ALU.add), yd_ready)

            s5_states(1)
            s5_states(2)
            s5_y(0)
            s5_states(3)
            esg, ecg = (e[:, 12:16, :].rearrange("p c s -> p (c s)") for e in (es, ec))
            v.tensor_tensor(t2[:, :], zs[3][0][:, :], esg, ALU.mult)
            me.give(v.tensor_tensor(t4[:, :], zs[3][1][:, :], ecg, ALU.mult), s_half_ready)
            s5_y(1)
            s5_y(2)
            s5_y(3)
            me.take(zg_ready, 4)
            lo(x_lo[:, 4:8, :], tmp[:, 4:8, :], x_hi[:, 4:8, :])
            ig = first("glu")
            me.take(gate_ready)
            z = tmp[:, 4:8, :].rearrange("p c s -> p (c s)")
            gated(z, z_second[:, :], z, x_f32)
            me.settle()
            me.give(v.tensor_copy(small[:, 46:47], small[:, 0:1]), read_out)
            split_next(ig)
            lo(x_lo[:, 4:8, :], tmp[:, 4:8, :], x_hi[:, 4:8, :], 0.5)
            add_feed(first("eo"), named("ffn.0"), xb_hi, xb_lo)
            ffn(2, named("mix.1"))
            i = first("mp")
            split_next(i)
            root()
            for j in range(3):
                by_token(c6[:, 2 * j:2 * j + 2, :], i + j)
                if j:
                    split_next(i + j)
                me.take(x_hi_ready)
                for c in range(2 * j, min(2 * j + 2, 5)):
                    ins = v.scalar_tensor_tensor(out=xb_lo[:, c, :], in0=c6[:, c, :],
                                                 scalar=vec("q_g", c) if c < 3 else vec("kv_g", c - 3),
                                                 in1=xb_hi[:, c, :].bitcast(F32), op0=ALU.mult, op1=ALU.subtract)
                me.give(ins, x_ready)
            i = first("uq")
            split_next(i)
            root(2 * S + 2)
            for j in range(4):
                p = psum(i + j)
                me.give(v.tensor_tensor(qn[:, 2 * j:2 * j + 2, :],
                                        rstd[:, 0:S].rearrange("p (o s) -> p o s", o=1).to_broadcast([P, 2, S]),
                                        p[:, 0:2 * S].rearrange("p (c s) -> p c s", c=2), ALU.mult))
                me.give(v.tensor_tensor(rx[:, j, :], rstd[:, 0:S], p[:, 2 * S:3 * S], ALU.mult), read_out)
                if j:
                    split_next(i + j)
            me.settle()
            me.give(v.tensor_copy(small[:, 45:46], small[:, 0:1]), rx_ready)
            cb = cos_r[:, :, :].to_broadcast([P, 4, S])
            sb_ = sin_r[:, :, :].to_broadcast([P, 4, S])
            v.tensor_tensor(tmp[:, 0:4, :], rx[:, :, :], cb, ALU.mult)
            me.give(v.tensor_tensor(tmp[:, 4, :], c6[:, 5, :], cos_r[:, 0, :], ALU.mult))
            i = first("ukv")
            for j in range(2):
                p = psum(i + j)
                me.give(v.tensor_tensor(kn[:, 4 * j:4 * j + 4, :],
                                        rstd[:, S:2 * S].rearrange("p (o s) -> p o s", o=1).to_broadcast([P, 4, S]),
                                        p[:, 0:2 * BANK].rearrange("p (c s) -> p c s", c=4), ALU.mult))
                for t in range(ST):
                    ins = v.tensor_scalar(v3[:, t, j * 512:(j + 1) * 512], p[:, (2 + t) * BANK:(3 + t) * BANK],
                                          rstd[:, 2 * S + t:2 * S + t + 1], None, ALU.mult)
                me.give(ins, read_out)
                split_next(i + j)
                if j == 0:
                    me.take(rot_ready)
                    v.tensor_tensor(qr[:, :, :], sb_, A[:, 0:2 * BANK].rearrange("p (c s) -> p c s", c=4), ALU.mult)
                    me.give(v.tensor_tensor(kr[:, 0, :], sin_r[:, 0, :], A[:, 2 * BANK:2 * BANK + S], ALU.mult))
                    me.settle()
                    v.tensor_tensor(qr[:, :, :], qr[:, :, :], tmp[:, 0:4, :], ALU.add)
                    me.give(v.tensor_tensor(kr[:, 0, :], kr[:, 0, :], tmp[:, 4, :], ALU.add), rope_ready)
            scale = 192 ** -0.5
            cz = causal.rearrange("p (o n) -> p o n", o=1).to_broadcast([P, 2, P])

            def m_soft_a(j):
                if j >= 2:
                    me.take(tr_ready)
                me.take(scores_ready)
                l, k = lm[:, j % 2, :, :], j % 2
                ps = A[:, k * BANK:k * BANK + 3 * P].rearrange("p (k n) -> p k n", k=3)
                v.tensor_scalar(l[:, 1, :], ps[:, 1, :], scale, None, ALU.mult)
                me.give(v.scalar_tensor_tensor(out=l[:, 0:3:2, :], in0=ps[:, 0:3:2, :], scalar=scale, in1=cz,
                                               op0=ALU.mult, op1=ALU.add), scores_read)
                me.settle()
                lf = l.rearrange("p k n -> p (k n)")
                v.tensor_reduce(m_mx[k][:, 0:1], lf[:, 0:P], AX.X, ALU.max)
                me.give(v.tensor_reduce(m_mx[k][:, 1:2], lf[:, P:3 * P], AX.X, ALU.max))
                me.settle()
                me.give(v.tensor_scalar(m_nm[k], m_mx[k], -1.0, None, ALU.mult), lg_ready)

            def m_soft_b(j):
                lf, k = lm[:, j % 2, :, :].rearrange("p k n -> p (k n)"), j % 2
                me.take(exp_ready)
                me.give(v.reciprocal(m_rs[k], m_sums[k]))
                me.settle()
                v.tensor_scalar(lf[:, 0:P], lf[:, 0:P], m_rs[k][:, 0:1], None, ALU.mult)
                me.give(v.tensor_scalar(lf[:, P:3 * P], lf[:, P:3 * P], m_rs[k][:, 1:2], None, ALU.mult), prob_ready)

            for j in range(MH + 2):
                if j < MH:
                    m_soft_a(j)
                if 1 <= j <= MH:
                    m_soft_b(j - 1)
                if j >= 2:
                    me.take(pv_hi)
                    me.give(v.tensor_tensor(x_lo[:, j - 2, :], A[:, 3 * BANK:3 * BANK + S],
                                            x_hi[:, j - 2, :].bitcast(F32), ALU.subtract), pv_read)
            add_feed(first("mo"), named("ffn.1"), xb_hi, xb_lo)
            ffn(3, None)
            root()
            for c in range(DC):
                ins = v.scalar_tensor_tensor(out=tmp[:, c, :], in0=h[:, c, :], scalar=vec("final", c), in1=rstd[:, 0:S],
                                             op0=ALU.mult, op1=ALU.mult)
                if c % 2:
                    me.give(ins, final_ready)

        @block.gpsimd
        def _(g):
            me = Side(g, pool_own)

            def tt(out, x, y, op, s=None):
                me.give(g.tensor_tensor(out, x, y, op), s)
                me.settle()

            def sum_squares():
                me.take(pair_squared)
                for j in range(1, 4):
                    me.take(pair_squared)
                    tt(tmp[:, 0:2, :], tmp[:, 0:2, :], tmp[:, 2 * j:2 * j + 2, :], ALU.add, sums_ready if j == 3 else None)

            sum_squares()
            W = slice(0, NS5)
            ar, ai, dt, mag, theta = (ang[j][:, W] for j in (0, 1, 3, 4, 5))
            g.wait_ge(s5_in, 48)
            me.take(dt_ready)
            tt(mag, ar, dt, ALU.mult, ndt_ready)
            tt(theta, ai, dt, ALU.mult, th_ready)
            den, xr, cr, ci, u1, u2 = (s5x[j][:, :] for j in range(6))
            tt(den, ar, ar, ALU.mult)
            tt(u1, ai, ai, ALU.mult)
            tt(den, den, u1, ALU.add, den_ready)
            me.take(trig_ready)
            g.wait_ge(mag_ready, 1)
            sin, cos = ang[7][:, W], ang[8][:, W]
            xi = u2
            for k, x in enumerate((ang[4], ang[8], ang[7])):
                me.give(g.tensor_copy(s5_st[:, k, :], x[:, 4 * P:NS5]))
            tt(xr, mag, cos, ALU.mult)
            tt(xi, mag, sin, ALU.mult)
            me.give(g.tensor_scalar(xr, xr, -1.0, None, ALU.add))
            me.settle()
            tt(cr, xr, ar, ALU.mult)
            tt(u1, xi, ai, ALU.mult)
            tt(cr, cr, u1, ALU.add)
            tt(ci, xi, ar, ALU.mult)
            tt(u1, xr, ai, ALU.mult)
            tt(ci, ci, u1, ALU.subtract)
            me.take(rden_ready)
            tt(cr, cr, den, ALU.mult)
            tt(ci, ci, den, ALU.mult)
            g.wait_ge(s5b_in, 16)
            cr, ci, u1 = cr[:, 0:4 * P], ci[:, 0:4 * P], u1[:, 0:4 * P]
            br, bi = s5b[:, 0, :], s5b[:, 1, :]
            bbr, bbi = (bb[:, j, :, :].rearrange("p c n -> p (c n)") for j in range(2))
            tt(bbr, cr, br, ALU.mult)
            tt(u1, ci, bi, ALU.mult)
            tt(bbr, bbr, u1, ALU.subtract)
            tt(bbi, cr, bi, ALU.mult)
            tt(u1, ci, br, ALU.mult)
            g.wait_ge(rope_kept, 1)
            tt(bbi, bbi, u1, ALU.add, bb_ready)

            def first_turns():
                g.wait_ge(read_out, PLAN[first("wo", 1) + 3].out)
                g.memset(ec[:, :, 0:1], 1.0)
                g.memset(es[:, :, 0:1], 0.0)
                g.tensor_copy(ec[:, :, 1:2], s5_st[:, 1, :].rearrange("p (c o) -> p c o", o=1))
                me.give(g.tensor_copy(es[:, :, 1:2], s5_st[:, 2, :].rearrange("p (c o) -> p c o", o=1)))
                me.settle()

            def turns(w):
                n = min(w, S - 1 - w)
                dc, ds = ec[:, :, w + 1:w + 1 + n], es[:, :, w + 1:w + 1 + n]
                sc, ss = ec[:, :, 1:1 + n], es[:, :, 1:1 + n]
                ew = ec[:, :, w:w + 1].to_broadcast([P, SC, n])
                fw = es[:, :, w:w + 1].to_broadcast([P, SC, n])
                sx = etmp[:, :, 0:n]
                tt(dc, sc, ew, ALU.mult)
                tt(sx, ss, fw, ALU.mult)
                tt(dc, dc, sx, ALU.subtract)
                tt(ds, ss, ew, ALU.mult)
                tt(sx, sc, fw, ALU.mult)
                tt(ds, ds, sx, ALU.add, e_ready if w + n >= S - 1 else None)

            def ffn(n, between=()):
                i = first("up_a", n)
                scale = rstd[:, 0:S].rearrange("p (o s) -> p o s", o=1).to_broadcast([P, 2, S])
                for j in range(PAIRS):
                    c = cv[:, j % 2, :, :]
                    me.take(act_ready)
                    me.give(g.tensor_tensor(c, c, scale, ALU.mult), act_scaled)
                    g.wait_ge(read_out, PLAN[i + 2 * j + 1].out)
                    me.take(y_hi)
                    me.give(g.tensor_tensor(yl[:, 2 * j:2 * j + 2, :], c, yh[:, 2 * j:2 * j + 2, :].bitcast(F32),
                                            ALU.subtract), y_ready)
                    if j < len(between):
                        between[j]()

            for layer in range(2):
                if layer:
                    sum_squares()
                    ffn(0)
                    sum_squares()
                else:
                    g.wait_ge(tab_ready, GROUPS)
                me.give(g.memset(ub[:, :, :], 0.0), u_zero)
                for j in range(4):
                    g.wait_ge(read_out, PLAN[first("u", layer) + j].out)
                    src, length = ub[:, 2 * j:2 * j + 2, :], S + 2 * PADT
                    for k in range(j + 1):
                        step = 1 << k
                        length -= step
                        dst = pool_w[k % 2]
                        me.give(g.tensor_tensor(dst[:, :, 0:length], src[:, :, 0:length], src[:, :, step:step + length],
                                                ALU.add))
                        me.settle()
                        src = dst
                    o = PADT - (1 << j)
                    if j == 0:
                        g.wait_ge(mm_done, first("v", layer) + 2)
                    for c in range(2):
                        me.give(g.tensor_tensor(tmp[:, 2 * j + c, :], src[:, c, o:o + S], inv_count(j), ALU.mult))
                    me.settle()
                    me.give(g.tensor_tensor(tmp[:, 2 * j:2 * j + 2, :], tmp[:, 2 * j:2 * j + 2, :],
                                            ub[:, 2 * j:2 * j + 2, PADT:PADT + S], ALU.subtract), pooled)
            sum_squares()
            ffn(1, [first_turns] + [lambda w=w: turns(w) for w in (1, 2, 4, 8, 16)])
            for w in (32, 64, 128):
                turns(w)
            sum_squares()
            g.wait_ge(read_out, PLAN[first("down", 1) + 11].out)
            me.give(g.memset(smask[:, :], 1.0))
            me.settle()
            me.give(g.memset(smask.rearrange("p (c s) -> p c s", s=CH)[:, :, 0:1], 0.0), smask_ready)
            g.wait_ge(ms2_ready, 1)
            me.give(g.memset(am[:, :, :], 0.0), am_zero)
            g.wait_ge(cc_in, 16)
            g.tensor_scalar(cc[:, 2, :, :], cc[:, 0, :, :], -1.0, None, ALU.mult)
            me.give(g.tensor_scalar(cc[:, 1, :, :], cc[:, 1, :, :], -1.0, None, ALU.mult), cc_ready)
            for k in range(4):
                gs = slice(4 * k, 4 * k + 4)
                ecg = ec[:, gs, :].rearrange("p c s -> p (c s)")
                esg = es[:, gs, :].rearrange("p c s -> p (c s)")
                zr, zi = zs[k]
                me.take(z_ready)
                if k == 0:
                    me.take(o_ready)
                for j, (z, e) in enumerate(((zr, ecg), (zi, esg), (zr, esg), (zi, ecg))):
                    if k == 0 and j == 3:
                        me.take(s5_free)
                    if k == 3 and j >= 2:
                        continue
                    if k and j == 2:
                        me.take(ys_ready)
                    ins = g.tensor_tensor(prods[(4 * k + j) % 6][:, :], z[:, :], e, ALU.mult)
                me.give(ins, s_ready)
                me.settle()
                me.give(g.tensor_copy(small[:, 47:48], small[:, 0:1]), z_read)
            sum_squares()
            ffn(2)
            sum_squares()
            sum_squares()
            ffn(3)


def _buckets(rel):
    n = -rel
    half = BUCKETS // 2
    ret = (n < 0).astype(np.int32) * half
    n = np.abs(n)
    exact = half // 2
    large = exact + (np.log(np.maximum(n, 1) / exact) / np.log(MAX_DISTANCE / exact) * (half - exact)).astype(np.int32)
    return (ret + np.where(n < exact, n, np.minimum(large, half - 1))).astype(np.int32)


def _constants():
    p = np.arange(P)
    rotate = np.zeros((P, P), np.float32)
    for m in range(P):
        if m % 64 < 32:
            rotate[m + 32, m] = -1.0
        else:
            rotate[m - 32, m] = 1.0
    inv = np.zeros((4, S), np.float32)
    i = np.arange(S)
    for g in range(4):
        w = 2 << g
        inv[g] = np.float32(1) / (np.clip(i - w // 2 + w, 0, S) - np.clip(i - w // 2, 0, S)).astype(np.float32)
    freq = (np.float32(10000.0) ** (-np.arange(0, 64, 2, dtype=np.float32) / np.float32(64))).astype(np.float32)
    parts = {
        "ident": np.eye(P, dtype=np.float32), "rotate": rotate,
        "causal": np.where(p[None, :] > p[:, None], NEG, 0.0).astype(np.float32),
        "inv_count": np.broadcast_to(inv.reshape(1, -1), (P, 4 * S)),
        "freq": freq[p % 32][:, None],
        "chunk_causal": ((p % CH)[:, None] <= np.arange(CH)[None, :]).astype(np.float32),
    }
    consts = np.concatenate([parts[n] for n, _ in CONSTS], axis=1).astype(np.float32)
    hot = np.zeros((BUCKETS + 1, GROUPS, TAB + 1), np.float32)
    rel = np.arange(TAB) - (S - 1)
    for g, d in enumerate(DILATIONS):
        ok = (np.abs(rel) <= HALF * d) & (rel % d == 0)
        hot[_buckets(rel)[ok], g, np.nonzero(ok)[0]] = 1.0
        hot[BUCKETS, g, np.nonzero(~ok)[0]] = NEG
        hot[BUCKETS, g, TAB] = NEG
    return np.ascontiguousarray(consts), hot.reshape(BUCKETS + 1, -1)


def _weights(a):
    out = []
    seen = {}
    w_in, e_in = a["w_in"], a["even_w_in_2"][0]
    mla = a["odd_w_in_2"][0]
    mla = np.concatenate([mla[:, :640], mla[:, 640:], mla[:, 640:]], axis=1)
    uq = a["mla_w_uq_2"][0].reshape(384, MH, 192)
    ukv = a["mla_w_ukv_2"][0].reshape(256, MH, 256)
    base = {"u": 0, "q": 1024, "k": 2560, "v": 4096, "g": 5632}
    even = {"ef": 512, "eq": 0, "ei": 1024, "eg": 1536, "eu": 2048}
    for b in PLAN:
        j = seen.get((b.kind, b.n), 0)
        seen[(b.kind, b.n)] = j + 1
        n, cols = b.n, slice(j * b.ncol, (j + 1) * b.ncol)
        if b.kind in base:
            w = w_in[n][:, base[b.kind] + j * 256:base[b.kind] + (j + 1) * 256]
        elif b.kind == "pool":
            w = a["w_pool"][n].reshape(D, 256)
        elif b.kind == "wa":
            w = a["w_a"][n][:, cols]
        elif b.kind == "wb":
            w = a["w_b"][n][:, cols]
        elif b.kind == "wo":
            w = a["w_o"][n][:, cols]
        elif b.kind in even:
            w = e_in[:, even[b.kind] + j * 256:even[b.kind] + (j + 1) * 256]
        elif b.kind == "glu":
            w = a["s5_w_glu_2"][0]
        elif b.kind == "eo":
            w = a["even_w_out_2"][0][:, cols]
        elif b.kind == "mp":
            w = mla[:, cols]
        elif b.kind == "uq":
            two = uq[:, 2 * j:2 * j + 2]
            w = np.concatenate([two[:, 0, :128], two[:, 1, :128], two[:, 0, 128:], two[:, 1, 128:]], axis=1)
        elif b.kind == "ukv":
            four = ukv[:, 4 * j:4 * j + 4]
            w = np.concatenate([four[:, :, :128].reshape(256, 512), four[:, :, 128:].reshape(256, 512)], axis=1)
        elif b.kind == "mo":
            w = a["odd_w_out_2"][0][:, cols]
        elif b.kind in ("up_a", "up_g"):
            up = a["w_up"][n] if n < 2 else a["ffn_w_in_2"][n - 2]
            c0 = j * 256 + (FF if b.kind == "up_g" else 0)
            w = up[:, c0:c0 + 256]
        else:
            down = a["w_down"][n] if n < 2 else a["ffn_w_out_2"][n - 2]
            r0 = (j % 3) * 1024
            w = down[r0:r0 + b.kc * P, (j // 3) * 256:(j // 3 + 1) * 256]
        assert w.shape == (b.kc * P, b.ncol), (b.kind, w.shape)
        out.append(np.ascontiguousarray(w.reshape(b.kc, P, b.ncol).transpose(1, 0, 2)).reshape(-1))
    return np.concatenate(out)


def _layouts(a):
    vectors = {"norm_f": a["norm_f"], "final": a["final_norm_g_2"], "lb0": a["hgrn_lb_logits_2"][0],
               "lb1": a["hgrn_lb_logits_2"][1], "hgrn_g": a["hgrn_norm_g_2"][0], "s5_d": a["s5_d_2"][0],
               "b_glu": a["s5_b_glu_2"][0], "q_g": a["mla_q_norm_g_2"][0], "kv_g": a["mla_kv_norm_g_2"][0]}
    for i in range(2):
        vectors |= {f"norm1.{i}": a["norm1"][i], f"norm2.{i}": a["norm2"][i], f"pool_scale.{i}": a["pool_scale"][i],
                    f"mix.{i}": a["norm_mix_g_2"][i], f"ffn.{i}": a["norm_ffn_g_2"][i],
                    f"convb.{i}": a["conv_b"][i], f"convb.{i + 2}": a["ffn_conv_b_2"][i]}
        for k in range(3):
            vectors |= {f"conv{k}.{i}": a["conv_w"][i, k], f"conv{k}.{i + 2}": a["ffn_conv_w_2"][i, k]}
    params = np.concatenate([vectors[n].reshape(-1, P).T for n, _ in VECTORS], axis=1)
    row, c4, col = np.meshgrid(np.arange(P), np.arange(4), np.arange(P), indexing="ij")
    chunk = 4 * c4 + row // 32
    group, state = 2 * chunk + col // SP_, col % SP_
    srow, sc = np.meshgrid(np.arange(P), np.arange(SC), indexing="ij")
    sgroup, sstate = 2 * sc + srow // SP_, srow % SP_
    abt = []
    for x in (a["s5_a_re_2"][0], a["s5_a_im_2"][0], np.broadcast_to(a["s5_log_dt_2"][0][:, None], (SG, SP_))):
        abt.append(np.concatenate([x[group, state].reshape(P, -1), x[sgroup, sstate]], axis=1))
    own = (row % 32) // 16 == col // SP_
    s5_b = np.zeros((P, 2, 4, P), np.float32)
    s5_c = np.zeros((P, 2, SC, 32), np.float32)
    for j, (b, c) in enumerate(((a["s5_b_re_2"][0], a["s5_c_re_2"][0]), (a["s5_b_im_2"][0], a["s5_c_im_2"][0]))):
        s5_b[:, j][own] = b[group, state, row % 16][own]
        for g in range(SG):
            r, f = SP_ * (g % 2), 16 * (g % 2)
            s5_c[r:r + SP_, j, g // 2, f:f + 16] = c[g].T
    consts, hot = _constants()
    return {
        "x": np.ascontiguousarray(a["x"][0].T), "params": np.ascontiguousarray(params), "consts": consts,
        "rel_bias": a["rel_bias"], "onehot": hot, "weights": _weights(a), "s5_abt": np.stack(abt),
        "s5_b": s5_b.reshape(P, 2, 4 * P), "s5_c": s5_c, "positions": a["positions_2"],
    }


def kernel(**inputs):
    import concourse.bacc as bacc
    from concourse.bass_utils import run_bass_kernel_spmd

    arrays = _layouts({k: np.asarray(v) for k, v in inputs.items()})
    nc = bacc.Bacc("TRN2", target_bir_lowering=False, num_devices=1)
    aps = {n: nc.dram_tensor(f"in_{n}", x.shape, mybir.dt.from_np(x.dtype), kind="ExternalInput").ap()
           for n, x in arrays.items()}
    aps["out"] = nc.dram_tensor("out_y", (D, S), F32, kind="ExternalOutput").ap()
    two_blocks_kernel(nc, aps)
    r = run_bass_kernel_spmd(nc, [{f"in_{n}": x for n, x in arrays.items()}], core_ids=[0])
    return np.ascontiguousarray(r.results[0]["out_y"].T)[None]
```
